# Optimizing a Trainium2 kernel written in Bass

```python
import math
import jax
import jax.numpy as jnp
from jax import lax
import numpy as np

D_MODEL = 2048
BATCH = 1
SEQ = 256
DEPTH = 2

N_MIXERS = 2
N_POOL_LAYERS = (DEPTH + 1) // 2
N_MLA_LAYERS = DEPTH // 2

POOL_WINDOWS = (2, 4, 8, 16)
N_POOL_GROUPS = len(POOL_WINDOWS)
POOL_GROUP_DIM = D_MODEL // N_POOL_GROUPS

MLA_HEADS = 16
Q_LORA_RANK = 512
KV_LORA_RANK = 512
QK_NOPE_DIM = 128
QK_ROPE_DIM = 64
V_HEAD_DIM = 128
ROPE_THETA = 10000.0
Q_BLOCK = 128

MEM_TOKENS = 256
XATTN_HEADS = 4
XATTN_HEAD_DIM = 128

FFN_HIDDEN = ((8 * D_MODEL // 3 + 255) // 256) * 256

NORM_EPS = 1e-6
MASK_VALUE = -1e30

kernel_name = "hybrid_pool_mla_memxattn_swiglu"

def rms_norm(x, g):
    xf = x.astype(jnp.float32)
    var = jnp.mean(xf * xf, axis=-1, keepdims=True)
    return (xf * lax.rsqrt(var + NORM_EPS)).astype(x.dtype) * g

def multiscale_pool_mixer(h, w_pool, scale):
    B, S, D = h.shape
    hg = h.reshape(B, S, N_POOL_GROUPS, POOL_GROUP_DIM).astype(jnp.float32)
    cs = jnp.cumsum(hg, axis=1)
    t = jnp.arange(S)
    means = []
    for g, w in enumerate(POOL_WINDOWS):
        c = cs[:, :, g]
        lagged = jnp.pad(c, ((0, 0), (w, 0), (0, 0)))[:, :S]
        cnt = jnp.minimum(t + 1, w).astype(jnp.float32)[None, :, None]
        means.append((c - lagged) / cnt)
    pooled = (jnp.stack(means, axis=2) - hg).astype(h.dtype)
    mixed = jnp.einsum('bsgc,gcd->bsgd', pooled, w_pool)
    return mixed.reshape(B, S, D) * scale

def rope_cos_sin(positions):
    inv_freq = 1.0 / (ROPE_THETA ** (jnp.arange(0, QK_ROPE_DIM, 2, dtype=jnp.float32) / QK_ROPE_DIM))
    ang = positions.astype(jnp.float32)[..., None] * inv_freq
    return jnp.cos(ang), jnp.sin(ang)

def apply_rope(x, cos, sin):
    half = x.shape[-1] // 2
    x1, x2 = x[..., :half], x[..., half:]
    c = cos[:, :, None, :].astype(x.dtype)
    s = sin[:, :, None, :].astype(x.dtype)
    return jnp.concatenate([x1 * c - x2 * s, x2 * c + x1 * s], axis=-1)

def causal_block_attention(q, k, v, scale):
    B, S, H, Dk = q.shape
    Dv = v.shape[-1]
    nb = S // Q_BLOCK
    qb = q.reshape(B, nb, Q_BLOCK, H, Dk).transpose(1, 0, 2, 3, 4)
    k_pos = jnp.arange(S)

    def one_block(args):
        q_blk, i = args
        s = jnp.einsum('bqhd,bkhd->bhqk', q_blk, k).astype(jnp.float32) * scale
        q_pos = i * Q_BLOCK + jnp.arange(Q_BLOCK)
        mask = k_pos[None, :] <= q_pos[:, None]
        s = jnp.where(mask[None, None], s, MASK_VALUE)
        p = jax.nn.softmax(s, axis=-1).astype(v.dtype)
        return jnp.einsum('bhqk,bkhd->bqhd', p, v)

    out = lax.map(one_block, (qb, jnp.arange(nb)))
    return out.transpose(1, 0, 2, 3, 4).reshape(B, S, H, Dv)

def mla_mixer(h, cos, sin, w_in, q_norm_g, w_q_up, kv_norm_g, w_kv_up, w_out):
    B, S, _ = h.shape
    c = h @ w_in
    c_q = c[..., :Q_LORA_RANK]
    c_kv = c[..., Q_LORA_RANK:Q_LORA_RANK + KV_LORA_RANK]
    k_rope = c[..., Q_LORA_RANK + KV_LORA_RANK:][:, :, None, :]
    q = (rms_norm(c_q, q_norm_g) @ w_q_up).reshape(B, S, MLA_HEADS, QK_NOPE_DIM + QK_ROPE_DIM)
    kv = (rms_norm(c_kv, kv_norm_g) @ w_kv_up).reshape(B, S, MLA_HEADS, QK_NOPE_DIM + V_HEAD_DIM)
    q_nope, q_rope = q[..., :QK_NOPE_DIM], q[..., QK_NOPE_DIM:]
    k_nope, v = kv[..., :QK_NOPE_DIM], kv[..., QK_NOPE_DIM:]
    q_rope = apply_rope(q_rope, cos, sin)
    k_rope = jnp.broadcast_to(apply_rope(k_rope, cos, sin), (B, S, MLA_HEADS, QK_ROPE_DIM))
    q_full = jnp.concatenate([q_nope, q_rope], axis=-1)
    k_full = jnp.concatenate([k_nope, k_rope], axis=-1)
    scale = 1.0 / math.sqrt(QK_NOPE_DIM + QK_ROPE_DIM)
    o = causal_block_attention(q_full, k_full, v, scale)
    return o.reshape(B, S, MLA_HEADS * V_HEAD_DIM) @ w_out

def memory_cross_attention(h, mem_n, w_q, w_kv, w_o):
    B, S, _ = h.shape
    M = mem_n.shape[1]
    width = XATTN_HEADS * XATTN_HEAD_DIM
    q = (h @ w_q).reshape(B, S, XATTN_HEADS, XATTN_HEAD_DIM)
    kv = mem_n @ w_kv
    k = kv[..., :width].reshape(B, M, XATTN_HEADS, XATTN_HEAD_DIM)
    v = kv[..., width:].reshape(B, M, XATTN_HEADS, XATTN_HEAD_DIM)
    s = jnp.einsum('bshd,bmhd->bhsm', q, k).astype(jnp.float32) * (1.0 / math.sqrt(XATTN_HEAD_DIM))
    p = jax.nn.softmax(s, axis=-1).astype(v.dtype)
    o = jnp.einsum('bhsm,bmhd->bshd', p, v)
    return o.reshape(B, S, width) @ w_o

def swiglu_ffn(h, w_in, w_out):
    gu = h @ w_in
    gate, up = gu[..., :FFN_HIDDEN], gu[..., FFN_HIDDEN:]
    return (jax.nn.silu(gate) * up) @ w_out

def _w(key, shape, fan_in):
    return jax.random.normal(key, shape, jnp.float32) * (fan_in ** -0.5)

def _gain(key, shape):
    return 1.0 + 0.05 * jax.random.normal(key, shape, jnp.float32)

def setup_inputs(seed: int = 0) -> dict:
    key = jax.random.key(seed)
    ks = jax.random.split(key, 24)
    D = D_MODEL
    xw = XATTN_HEADS * XATTN_HEAD_DIM
    offsets = jax.random.randint(ks[2], (BATCH, 1), 0, 1024, dtype=jnp.int32)
    positions = offsets + jnp.arange(SEQ, dtype=jnp.int32)[None, :]
    return {
        "x": jax.random.normal(ks[0], (BATCH, SEQ, D), jnp.float32),
        "mem": jax.random.normal(ks[1], (BATCH, MEM_TOKENS, D), jnp.float32),
        "positions": positions,
        "norm_mix_g": _gain(ks[3], (DEPTH, D)),
        "norm_xattn_g": _gain(ks[4], (DEPTH, D)),
        "norm_mem_g": _gain(ks[5], (DEPTH, D)),
        "norm_ffn_g": _gain(ks[6], (DEPTH, D)),
        "pool_w": _w(ks[7], (N_POOL_LAYERS, N_POOL_GROUPS, POOL_GROUP_DIM, POOL_GROUP_DIM), POOL_GROUP_DIM),
        "pool_scale": 1.0 + 0.1 * jax.random.normal(ks[8], (N_POOL_LAYERS, D), jnp.float32),
        "mla_w_in": _w(ks[9], (N_MLA_LAYERS, D, Q_LORA_RANK + KV_LORA_RANK + QK_ROPE_DIM), D),
        "mla_q_norm_g": _gain(ks[10], (N_MLA_LAYERS, Q_LORA_RANK)),
        "mla_w_q_up": _w(ks[11], (N_MLA_LAYERS, Q_LORA_RANK, MLA_HEADS * (QK_NOPE_DIM + QK_ROPE_DIM)), Q_LORA_RANK),
        "mla_kv_norm_g": _gain(ks[12], (N_MLA_LAYERS, KV_LORA_RANK)),
        "mla_w_kv_up": _w(ks[13], (N_MLA_LAYERS, KV_LORA_RANK, MLA_HEADS * (QK_NOPE_DIM + V_HEAD_DIM)), KV_LORA_RANK),
        "mla_w_out": _w(ks[14], (N_MLA_LAYERS, MLA_HEADS * V_HEAD_DIM, D), MLA_HEADS * V_HEAD_DIM),
        "xattn_w_q": _w(ks[15], (DEPTH, D, xw), D),
        "xattn_w_kv": _w(ks[16], (DEPTH, D, 2 * xw), D),
        "xattn_w_o": _w(ks[17], (DEPTH, xw, D), xw),
        "ffn_w_in": _w(ks[18], (DEPTH, D, 2 * FFN_HIDDEN), D),
        "ffn_w_out": _w(ks[19], (DEPTH, FFN_HIDDEN, D), FFN_HIDDEN),
        "final_norm_g": _gain(ks[20], (D,)),
    }

def reference(x, mem, positions, norm_mix_g, norm_xattn_g, norm_mem_g, norm_ffn_g,
              pool_w, pool_scale, mla_w_in, mla_q_norm_g, mla_w_q_up, mla_kv_norm_g,
              mla_w_kv_up, mla_w_out, xattn_w_q, xattn_w_kv, xattn_w_o,
              ffn_w_in, ffn_w_out, final_norm_g):
    cos, sin = rope_cos_sin(positions)
    for i in range(DEPTH):
        j = i // N_MIXERS
        h = rms_norm(x, norm_mix_g[i])
        if i % N_MIXERS == 0:
            x = x + multiscale_pool_mixer(h, pool_w[j], pool_scale[j])
        else:
            x = x + mla_mixer(h, cos, sin, mla_w_in[j], mla_q_norm_g[j], mla_w_q_up[j],
                              mla_kv_norm_g[j], mla_w_kv_up[j], mla_w_out[j])
        h = rms_norm(x, norm_xattn_g[i])
        mem_n = rms_norm(mem, norm_mem_g[i])
        x = x + memory_cross_attention(h, mem_n, xattn_w_q[i], xattn_w_kv[i], xattn_w_o[i])
        h = rms_norm(x, norm_ffn_g[i])
        x = x + swiglu_ffn(h, ffn_w_in[i], ffn_w_out[i])
    return rms_norm(x, final_norm_g)


_drawn_inputs = setup_inputs


def setup_inputs(seed=0):
    import zlib

    import numpy as np

    out = dict(_drawn_inputs(seed))
    spreads = {}
    factors = {'norm_xattn_g': 8.0, 'norm_mem_g': 6.346, 'mla_q_norm_g': 8.0, 'mla_kv_norm_g': 5.951}
    for name, (base, spread) in spreads.items():
        noise = np.random.default_rng([zlib.crc32(name.encode()), seed]).standard_normal(out[name].shape)
        drawn = base * np.exp(spread * noise) if base else spread * noise
        out[name] = jnp.asarray(drawn.astype(out[name].dtype))
    for name, factor in factors.items():
        out[name] = (out[name] * factor).astype(out[name].dtype)
    return out
```

```python
import math
from contextlib import ExitStack

import concourse.bass as bass
from concourse import mybir

F32 = mybir.dt.float32
F32R = mybir.dt.float32r
I32 = mybir.dt.int32
BF16 = mybir.dt.bfloat16
ALU = mybir.AluOpType
ACT = mybir.ActivationFunctionType
AX_X = mybir.AxisListType.X

P = 128
D = 2048
S = 256
TB = S // P
KB = D // P
CW = 512
NC = D // CW
CK = CW // P
F = 5632
FK = F // P
NP = F // CW
XH = 4
HEADS = 16
NOPE, ROPE, VD = 128, 64, 128
HR = ROPE // 2
RANK = 512
RK = RANK // P
QW = 2 * (NOPE + ROPE)
PAIRS = HEADS // 2
WINDOWS = (2, 4, 8, 16)
REACH = P + max(WINDOWS)
EPS = 1e-6
XSCALE = 1.0 / P ** 0.5
MSCALE = 1.0 / (NOPE + ROPE) ** 0.5
MASK = -1e30
RING = 4
UK = 2
UW = UK * CW
AHEAD = RING - 1
BANKS = 4
TWO_PI = 6.283185307179586


def _parts(value, count):
    out = []
    for _ in range(count):
        top = 2.0 ** (math.floor(math.log2(abs(value))) - 11)
        out.append(math.floor(value / top) * top)
        value -= out[-1]
    return out


TWO_PI_PARTS = _parts(TWO_PI, 4)
ROUND = 1.5 * 2.0 ** 23

N_MEM, N_POOL, N_X0, N_F0, N_MLA, N_CQ, N_CKV, N_X1, N_F1, N_OUT = range(10)
STATS = [8, 8, 8, 8, 8, 2, 2, 8, 8, 8]
STAT_END = [sum(STATS[:n + 1]) for n in range(len(STATS))]

G_MIX, G_X, G_MEM, G_FFN, G_CQ, G_CKV = 0, 32, 64, 96, 128, 132


class Phase:
    pass


def plan():
    table = [
        ("mem", 32, 4, (6, 5, 5, 5), 16, 0),
        ("pool", 8, 4, (0, 0, 4, 4), 8, 4),
        ("xq0", 8, 1, (3, 3, 4, 4), 4, 0), ("xo0", 8, 4, (0, 0, 4, 4), 8, 4),
        ("fi0", 16 * NP, 2 * NP, (NP, NP, 0, 0), 2 * NP, 0), ("fo0", 4 * FK // UK, 4, (0, 0, 4, 4), 8, 4),
        ("mi", 17, 3, (2, 1, 1, 1), 4, 0),
        ("mp", 4 * PAIRS, 2 * PAIRS, (3 * PAIRS, 2 * PAIRS, 2 * PAIRS, 2 * PAIRS), 2 * PAIRS, 0),
        ("mo", 32, 4, (0, 0, 4, 4), 8, 4),
        ("xq1", 8, 1, (3, 3, 4, 4), 4, 0), ("xo1", 8, 4, (0, 0, 4, 4), 8, 4),
        ("fi1", 16 * NP, 2 * NP, (NP, NP, 0, 0), 2 * NP, 0), ("fo1", 4 * FK // UK, 4, (0, 0, 0, 0), 0, 4),
    ]
    phases, u, g, b, h, c = {}, 0, 0, [0] * BANKS, 0, 0
    for name, nu, ng, nb, nh, nc_ in table:
        p = Phase()
        p.unit, p.group, p.bank, p.half, p.chunk = u, g, tuple(b), h, c
        phases[name] = p
        u, g, h, c = u + nu, g + ng, h + nh, c + nc_
        b = [x + y for x, y in zip(b, nb)]
    return phases, u


def hybrid_kernel(nc, a, out):
    PH, UNITS = plan()
    with ExitStack() as ctx:
        def sb(name, shape, dt=F32):
            return ctx.enter_context(nc.sbuf_tensor(name, shape, dt))

        def sem(name):
            return ctx.enter_context(nc.semaphore(name))

        raw = sb("raw", [P, RING, UW])
        w_hi = sb("w_hi", [P, RING, UW], F32R)
        w_lo = sb("w_lo", [P, RING, UW], F32R)
        x = sb("x", [P, TB, D])
        xs = sb("xs", [P, 2, TB, CW])
        k_mem1 = sb("k_mem1", [P, XH, S])
        v_mem1 = sb("v_mem1", [P, TB, XH, P])
        area_x = nc.sbuf_base
        sb("area_x", [P, 2 * KB * S])
        area_h = nc.sbuf_base
        sb("area_h", [P, 2 * FK * S])
        small = {}
        for name, shape, dt in (
                ("gains", [P, 136], F32), ("gain_rows", [P, P], F32), ("gain_rows2", [2 * RK, P], F32),
                ("ident", [P, P], F32), ("mask", [P, S], F32), ("cos", [P, TB, HR], F32), ("sin", [P, TB, HR], F32),
                ("junk", [P, CW], BF16), ("sums", [P, 10, TB, NC], F32), ("var", [P, 10, TB], F32),
                ("total", [P, 10, TB], F32), ("rs", [P, 10, TB], F32), ("rsq", [P, 10, TB], F32),
                ("minus_half", [P, TB], F32), ("pace", [P, 2], F32), ("neg_max", [P, HEADS, TB], F32),
                ("exp_sum", [P, HEADS, TB], F32), ("inv_sum", [P, HEADS, TB], F32)):
            small[name] = sb(name, shape, dt)
        gains, gain_rows, gain_rows2 = small["gains"], small["gain_rows"], small["gain_rows2"]
        ident, mask, cos, sin, junk = (small[n] for n in ("ident", "mask", "cos", "sin", "junk"))
        sums, var, total, rs, rsq = (small[n] for n in ("sums", "var", "total", "rs", "rsq"))
        minus_half, pace, neg_max, exp_sum, inv_sum = (
            small[n] for n in ("minus_half", "pace", "neg_max", "exp_sum", "inv_sum"))

        def at(name, shape, offset, dt=F32):
            return nc.alloc_sbuf_tensor_at(name, shape, dt, offset=offset)

        KBYTES = S * 4
        x_hi = at("x_hi", [P, KB, S], area_x, F32R)
        x_lo = at("x_lo", [P, KB, S], area_x + KB * KBYTES, F32R)
        mem = at("mem_tok", [P, TB, D], area_x)
        g_out = at("g_out", [P, D], area_x)
        xg = at("xg", [P, TB, D], area_x + KB * KBYTES)
        h_hi = at("h_hi", [P, FK, S], area_h, F32R)
        lo0 = area_h + FK * KBYTES
        h_lo = at("h_lo", [P, FK, S], lo0, F32R)
        r1, r2 = area_h + 32 * KBYTES, lo0 + 32 * KBYTES
        k_mem0 = at("k_mem0", [P, XH, S], r1)
        v_mem0 = at("v_mem0", [P, TB, XH, P], r1 + 4 * KBYTES)
        k_tok = at("k_tok", [P, TB, CW], r1 + 8 * KBYTES)
        pool_s = at("pool_s", [P, D], r2)
        xa = area_h + 8 * KBYTES
        q_tok = at("q_tok", [P, TB, CW], xa)
        q_t = at("q_t", [P, XH, S], xa + 4 * KBYTES)
        probs = at("probs", [P, 2, TB, S], xa + 8 * KBYTES)
        probs_t = at("probs_t", [P, 2, TB, S], xa + 12 * KBYTES)
        ma, mb = area_h + 24 * KBYTES, lo0 + 24 * KBYTES
        cq_tok = at("cq_tok", [P, TB, RANK], ma)
        ckv_tok = at("ckv_tok", [P, TB, RANK], ma + 4 * KBYTES)
        kh_tok = at("kh_tok", [P, TB, 2, NOPE], ma + 8 * KBYTES)
        vh_tok = at("vh_tok", [P, TB, 2, VD], ma + 10 * KBYTES)
        qh_tok = at("qh_tok", [P, TB, 2, NOPE + ROPE], ma + 12 * KBYTES)
        kr_tok = at("kr_tok", [P, TB, ROPE], ma + 15 * KBYTES)
        rope_t = at("rope_t", [P, 4, TB, 2, HR], ma + 16 * KBYTES)
        qh_t = at("qh_t", [P, 2, S], mb)
        kh_t = at("kh_t", [P, 2, S], mb + 2 * KBYTES)
        qr_t = at("qr_t", [ROPE, 2, S], mb + 4 * KBYTES)
        kr_t = at("kr_t", [ROPE, S], mb + 6 * KBYTES)
        neg_s = at("neg_s", [P, 2, 3 * P], mb + 7 * KBYTES)
        mprobs = at("mprobs", [P, 2, 3 * P], mb + 10 * KBYTES)
        mprobs_t = at("mprobs_t", [P, 2, 3 * P], mb + 13 * KBYTES)
        BAND = 4 * (REACH + P)
        bands = xs[:, :, :, :].rearrange("p a b n -> p (a b n)")[:, 0:BAND]
        band_of = (bands[:, 0:4 * REACH].rearrange("p (g n) -> p g n", g=4),
                   bands[:, 4 * REACH:BAND].rearrange("p (g n) -> p g n", g=4))
        s_tok, h_tok = xs[:, 0, :, :], xs[:, 1, :, :]
        angle_t = at("angle_t", [P, 6, TB, HR], r2 + 8 * KBYTES)
        pos_i = at("pos_i", [P, TB], r2 + 8 * KBYTES + 6 * TB * HR * 4, I32)
        pos_f = at("pos_f", [P, TB], r2 + 8 * KBYTES + 6 * TB * HR * 4 + 32)
        freq = at("freq", [P, HR], r2 + 8 * KBYTES + 6 * TB * HR * 4 + 64)

        acc = ctx.enter_context(nc.psum_tensor("acc", [P, 2, TB, CW], F32))
        bank = ctx.enter_context(nc.psum_tensor("bank", [P, BANKS, CW], F32))

        loaded = [sem(f"loaded{s}") for s in range(RING)]
        hi_ready = sem("hi_ready")
        lo_ready = sem("lo_ready")
        unit_used = sem("unit_used")
        acc_free = [sem(f"acc_free{s}") for s in range(2)]
        bank_full = [sem(f"bank_full{k}") for k in range(BANKS)]
        bank_free = [sem(f"bank_free{k}") for k in range(BANKS)]
        halved_hi = sem("halved_hi")
        stats = sem("stats")
        var_ready = sem("var_ready")
        rs_ready = sem("rs_ready")
        x_back = sem("x_back")
        k_ready = sem("k_ready")
        roped = sem("roped")
        max_ready = sem("max_ready")
        exp_ready = sem("exp_ready")
        probs_ready = sem("probs_ready")
        mem_in, x_in, band_in, rows_in, rope_in, scale_in, g_in = (
            sem(n) for n in ("mem_in", "x_in", "band_in", "rows_in", "rope_in", "scale_in", "g_in"))
        ident_ready, mask_ready, half_ready = sem("ident_ready"), sem("mask_ready"), sem("half_ready")
        bands_ready, angle_ready, table_ready = (sem(n) for n in ("bands_ready", "angle_ready", "table_ready"))
        dve_step, pool_step = sem("dve_step"), sem("pool_step")
        dve_recip, rope_step = sem("dve_recip"), sem("rope_step")
        xg_ready, stored = sem("xg_ready"), sem("stored")
        y_ready = [sem(f"y_ready{t}") for t in range(TB)]

        def slot_count(g):
            return g // 2

        def weights(w, k0, kbs, c0, width):
            return w[k0 * P:(k0 + kbs) * P, bass.ds(c0, width)].rearrange("(b p) n -> p b n", p=P)

        block = ctx.enter_context(nc.Block())

        @block.sync
        def _(sp):
            def load(n, slot, w, k0, c0, kbs=UK, width=CW):
                if not isinstance(n, int) or n >= RING:
                    sp.wait_ge(lo_ready, n - RING + 1)
                sp.dma_start(raw[:, slot, 0:kbs * width].rearrange("p (b n) -> p b n", b=kbs),
                             weights(w, k0, kbs, c0, width)).then_inc(loaded[slot], 16)

            def group(n, base, w, c0, nk, width=CW):
                for j in range(nk // UK):
                    load(n + j, (base + j) % RING, w, UK * j, c0, width=width)

            mem_v = a["mem"][0].rearrange("(t p) d -> p t d", p=P)
            for c in range(NC):
                sp.dma_start(mem[:, :, c * CW:(c + 1) * CW], mem_v[:, :, c * CW:(c + 1) * CW]).then_inc(mem_in, 16)
            for l in range(2):
                for c in range(2):
                    n = PH["mem"].unit + 16 * l + 8 * c
                    group(n, n, a["xattn_w_kv"][l], c * CW, KB)
                    if l == 0 and c == 0:
                        sp.dma_start(x[:, :, :], a["x"][0].rearrange("(t p) d -> p t d", p=P)).then_inc(x_in, 16)
                        sp.dma_start(bands, a["bands"]).then_inc(band_in, 16)

            for g in range(len(WINDOWS)):
                n = PH["pool"].unit + 2 * g
                group(n, n, a["pool_w"][0, g], 0, CK)

            def wide_out(base, w, nk):
                per = nk // UK
                with sp.Fori(0, NC // 2) as i:
                    for c in range(2):
                        group(base + per * c + i * (2 * per), base + per * c, w, i * (2 * CW) + c * CW, nk)

            def xattn(l):
                n = PH[f"xq{l}"].unit
                group(n, n, a["xattn_w_q"][l], 0, KB)
                for c in range(NC):
                    n = PH[f"xo{l}"].unit + 2 * c
                    group(n, n, a["xattn_w_o"][l], c * CW, XH)

            def ffn(l):
                base = PH[f"fi{l}"].unit
                with sp.Fori(0, NP) as i:
                    group(base + i * 16, base, a["ffn_w_in"][l], i * CW, KB)
                    group(base + 8 + i * 16, base + 8, a["ffn_w_in"][l], i * CW + F, KB)
                wide_out(PH[f"fo{l}"].unit, a["ffn_w_out"][l], FK)

            xattn(0)
            ffn(0)
            n = PH["mi"].unit
            group(n, n, a["mla_w_in"][0], 0, KB)
            group(n + 8, n + 8, a["mla_w_in"][0], RANK, KB)
            load(n + 16, (n + 16) % RING, a["mla_w_in"][0], 0, 2 * RANK, kbs=KB, width=ROPE)
            base = PH["mp"].unit
            with sp.Fori(0, PAIRS) as i:
                group(base + i * 4, base, a["mla_w_q_up"][0], i * QW, RK, width=QW)
                group(base + 2 + i * 4, base + 2, a["mla_w_kv_up"][0], i * CW, RK)
            wide_out(PH["mo"].unit, a["mla_w_out"][0], KB)
            xattn(1)
            ffn(1)
            out_v = out[0].rearrange("(t p) d -> p t d", p=P)
            for t in range(TB):
                sp.wait_ge(y_ready[t], 1)
                sp.dma_start(out_v[:, t, :], xg[:, t, :]).then_inc(stored, 16)
            sp.wait_ge(stored, 16 * TB)

        @block.tensor
        def _(pe):
            def unit(n, base, src_hi, src_lo, k0, g_slot, first, last, kbs=UK, width=CW):
                slot = base % RING
                pe.wait_ge(lo_ready, n + 1)
                for b in range(kbs):
                    cols = slice(b * width, (b + 1) * width)
                    for t in range(TB):
                        o = acc[:, g_slot, t, 0:width]
                        hi = src_hi[:, k0 + b, t * P:(t + 1) * P]
                        lo = src_lo[:, k0 + b, t * P:(t + 1) * P]
                        pe.matmul(o, hi, w_hi[:, slot, cols], start=(first and b == 0), stop=False)
                        pe.matmul(o, hi, w_lo[:, slot, cols], start=False, stop=False)
                        mm = pe.matmul(o, lo, w_hi[:, slot, cols], start=False, stop=(last and b == kbs - 1))
                mm.then_inc(unit_used, 1)

            def slot_ready(g, count):
                if not isinstance(count, int) or count > 0:
                    pe.wait_ge(acc_free[g % 2], count)

            def bank_ready(k, count):
                if not isinstance(count, int) or count > 0:
                    pe.wait_ge(bank_free[k], count)

            def four(k, count, parts, rows=P):
                if count is not None:
                    bank_ready(k, count)
                for j, src in enumerate(parts):
                    tr = pe.transpose(bank[0:rows, k, j * P:(j + 1) * P], src, ident[:, :])
                tr.then_inc(bank_full[k], 1)

            def turn_chunk(g, count, b2, xslot):
                pe.wait_ge(acc_free[g % 2], count + 1)
                for m in range(2):
                    four(2 + m, b2, [xs[:, xslot, t, (2 * m + k) * P:(2 * m + k + 1) * P]
                                     for k in range(2) for t in range(TB)])

            pe.wait_ge(ident_ready, 2)
            pe.wait_ge(rows_in, 16 * 6)
            pe.transpose(bank[:, 0, 0:P], gain_rows[:, :], ident[:, :])
            pe.transpose(bank[:, 0, P:P + 2 * RK], gain_rows2[:, :], ident[0:2 * RK, 0:2 * RK]).then_inc(bank_full[0], 1)
            turn = [1, 0, 0, 0]
            for m in range(KB // 2):
                if m % 2 == 0:
                    pe.wait_ge(mem_in, 16 * NC)
                four(m % 4, turn[m % 4], [mem[:, t, (2 * m + k) * P:(2 * m + k + 1) * P]
                                          for k in range(2) for t in range(TB)])
                turn[m % 4] += 1
            ph = PH["mem"]
            for l in range(2):
                for c in range(2):
                    g = ph.group + 2 * l + c
                    slot_ready(g, slot_count(g))
                    for j in range(8):
                        n = ph.unit + 16 * l + 8 * c + j
                        if l == 0 and c == 0:
                            pe.wait_ge(bank_free[j % 4], (2 if j % 4 == 0 else 1) + j // 4)
                        unit(n, n, h_hi[:, 16 * l:16 * l + 16, :], h_lo[:, 16 * l:16 * l + 16, :],
                             UK * j, g % 2, j == 0, j == 7)
                        if c == 1 and j == 0:
                            pe.wait_ge(acc_free[(g - 1) % 2], slot_count(g - 1) + 1)
                            for m in range(2):
                                k = 2 * l + m
                                four(k, turn[k], [k_tok[:, t, (2 * m + hh) * P:(2 * m + hh + 1) * P]
                                                  for hh in range(2) for t in range(TB)])
                                turn[k] += 1
                        if l == 1 and c == 1:
                            if j == 0:
                                pe.wait_ge(bands_ready, 2)
                            bank_ready(j % 4, turn[j % 4])
                            for k in range(2):
                                kb = 2 * j + k
                                o = bank[:, j % 4, k * S:(k + 1) * S]
                                for t in range(TB):
                                    to = slice(0, REACH) if t == 0 else slice(P, S)
                                    mm = pe.matmul(o[:, to], x[:, t, kb * P:(kb + 1) * P],
                                                   band_of[t][:, kb // CK, :], start=(k == 0 and t == 0),
                                                   stop=(t == 1), skip_group_check=True)
                            mm.then_inc(bank_full[j % 4], 1)
                            turn[j % 4] += 1

            def narrow_out(name, src_hi, src_lo, waits):
                ph = PH[name]
                for c in range(NC):
                    g = ph.group + c
                    slot_ready(g, slot_count(g))
                    for j in range(2):
                        waits(c, j)
                        n = ph.unit + 2 * c + j
                        k0 = UK * j + (CK * c if name == "pool" else 0)
                        unit(n, n, src_hi, src_lo, k0, g % 2, j == 0, j == 1)
                        if j == 0 and c > 0:
                            turn_chunk(g - 1, slot_count(g - 1), ph.bank[2] + c - 1, (c - 1) % 2)
                g = ph.group + NC - 1
                turn_chunk(g, slot_count(g), ph.bank[2] + NC - 1, (NC - 1) % 2)

            def pooled(c, j):
                b = 2 * c + j
                pe.wait_ge(bank_free[b % 4], PH["pool"].bank[b % 4] - 1 + b // 4)

            narrow_out("pool", x_hi, x_lo, pooled)

            def wait_x(ph, j):
                pe.wait_ge(bank_free[2 + j % 2], ph.bank[2 + j % 2] - 3 + j // 2)

            def xattn(l):
                ph = PH[f"xq{l}"]
                k_mem, v_mem = (k_mem0, v_mem0) if l == 0 else (k_mem1, v_mem1)
                g, b = ph.group, list(ph.bank)
                slot_ready(g, slot_count(g))
                for j in range(8):
                    wait_x(ph, j)
                    unit(ph.unit + j, ph.unit + j, x_hi, x_lo, UK * j, g % 2, j == 0, j == 7)
                pe.wait_ge(acc_free[g % 2], slot_count(g) + 1)
                for m in range(2):
                    four(m, b[m], [q_tok[:, t, (2 * m + hh) * P:(2 * m + hh + 1) * P]
                                   for hh in range(2) for t in range(TB)])

                def scores(h):
                    bank_ready(h % 2, b[h % 2] + 1 + h // 2)
                    if h == 0:
                        bank_ready(1, b[1] + 1)
                    for t in range(TB):
                        mm = pe.matmul(bank[:, h % 2, t * S:(t + 1) * S], q_t[:, h, t * P:(t + 1) * P],
                                       k_mem[:, h, :], start=(t == 0), stop=True, skip_group_check=True)
                    mm.then_inc(bank_full[h % 2], 1)

                def turn_probs(h):
                    pe.wait_ge(probs_ready, XH * l + (HEADS if l else 0) + h + 1)
                    four(2, b[2] + h, [probs[:, h % 2, t, k * P:(k + 1) * P] for k in range(TB) for t in range(TB)])

                def values(h):
                    bank_ready(2, b[2] + h + 1)
                    bank_ready(3, b[3] + h)
                    for k in range(TB):
                        mm = pe.matmul(bank[:, 3, 0:S], v_mem[:, k, h, :], probs_t[:, h % 2, k, :],
                                       start=(k == 0), stop=(k == TB - 1))
                    mm.then_inc(bank_full[3], 1)

                scores(0)
                scores(1)
                for h in range(XH):
                    turn_probs(h)
                    if h + 2 < XH:
                        scores(h + 2)
                    if h:
                        values(h - 1)
                values(XH - 1)
                narrow_out(f"xo{l}", h_hi, h_lo,
                           lambda c, j: bank_ready(3, b[3] + UK * (j + 1)) if c == 0 else None)

            def ffn(l):
                ph = PH[f"fi{l}"]

                def turn_hidden(i, cnt_up):
                    pe.wait_ge(acc_free[(ph.group + 1) % 2], cnt_up)
                    for m in range(2):
                        four(m, ph.bank[m] + i, [h_tok[:, t, (2 * m + k) * P:(2 * m + k + 1) * P]
                                                 for k in range(2) for t in range(TB)])

                def pair(i, first):
                    for c in range(2):
                        g = ph.group + c
                        slot_ready(g, slot_count(g) + i)
                        for j in range(8):
                            if first and c == 0:
                                wait_x(ph, j)
                            unit(ph.unit + 8 * c + j + i * 16, ph.unit + 8 * c + j, x_hi, x_lo, UK * j,
                                 g % 2, j == 0, j == 7)
                            if c == 0 and j == 0 and not first:
                                turn_hidden(i - 1, slot_count(ph.group + 1) + i)

                pair(0, True)
                with pe.Fori(1, NP) as i:
                    pair(i, False)
                turn_hidden(NP - 1, slot_count(ph.group + 1) + NP)
                for m in range(2):
                    bank_ready(m, ph.bank[m] + NP)
                wide_out(f"fo{l}", FK, turned=(l == 0))

            def wide_out(name, nk, turned):
                ph, per = PH[name], nk // UK

                def two(i):
                    for c in range(2):
                        g = ph.group + c
                        slot_ready(g, slot_count(g) + i)
                        for j in range(per):
                            unit(ph.unit + per * c + j + i * (2 * per), ph.unit + per * c + j, h_hi, h_lo, UK * j,
                                 g % 2, j == 0, j == per - 1)
                            if turned and c == 1 and j == 0:
                                turn_chunk(g - 1, slot_count(g - 1) + i, ph.bank[2] + i * 2, 0)
                    if turned:
                        turn_chunk(g, slot_count(g) + i, ph.bank[2] + 1 + i * 2, 1)

                with pe.Fori(0, NC // 2) as i:
                    two(i)

            xattn(0)
            ffn(0)

            ph, pp = PH["mi"], PH["mp"]
            cq, ckv, kr = ph.group, ph.group + 1, ph.group + 2
            for n, g in enumerate((cq, ckv)):
                slot_ready(g, slot_count(g))
                for j in range(8):
                    if n == 0:
                        wait_x(ph, j)
                    unit(ph.unit + 8 * n + j, ph.unit + 8 * n + j, x_hi, x_lo, UK * j, g % 2, j == 0, j == 7)
                    if n == 1 and j == 0:
                        pe.wait_ge(acc_free[cq % 2], slot_count(cq) + 1)
                        for m in range(2):
                            four(m, ph.bank[m], [cq_tok[:, t, (2 * m + k) * P:(2 * m + k + 1) * P]
                                                 for k in range(2) for t in range(TB)])
            slot_ready(kr, slot_count(kr))
            unit(ph.unit + 16, ph.unit + 16, x_hi, x_lo, 0, kr % 2, True, True, kbs=KB, width=ROPE)

            def q_up(i, j):
                g = pp.group
                if j == 0:
                    slot_ready(g, slot_count(g) + i)
                unit(pp.unit + j + i * 4, pp.unit + j, h_hi[:, 16:20, :], h_lo[:, 16:20, :], UK * j, g % 2,
                     j == 0, j == 1, width=QW)

            def kv_up(i, j):
                g = pp.group + 1
                if j == 0:
                    slot_ready(g, slot_count(g) + i)
                unit(pp.unit + 2 + j + i * 4, pp.unit + 2 + j, h_hi[:, 20:24, :], h_lo[:, 20:24, :], UK * j, g % 2,
                     j == 0, j == 1)

            for m in range(2):
                bank_ready(m, ph.bank[m] + 1)
            q_up(0, 0)
            q_up(0, 1)
            pe.wait_ge(acc_free[ckv % 2], slot_count(ckv) + 1)
            for m in range(2):
                four(2 + m, ph.bank[2 + m], [ckv_tok[:, t, (2 * m + k) * P:(2 * m + k + 1) * P]
                                             for k in range(2) for t in range(TB)])
            pe.wait_ge(roped, 1)
            four(0, ph.bank[0] + 1, [kr_tok[:, t, :] for t in range(TB)], rows=ROPE)
            for m in range(2):
                bank_ready(2 + m, ph.bank[2 + m] + 1)
            kv_up(0, 0)
            kv_up(0, 1)

            def attend(i, more):
                b = pp.bank
                heads = range(2)
                pe.wait_ge(acc_free[pp.group % 2], slot_count(pp.group) + 1 + i)
                four(0, b[0] + i * 3, [qh_tok[:, t, h, 0:NOPE] for h in heads for t in range(TB)])
                pe.wait_ge(roped, i + 2)
                bank_ready(2, b[2] + i * 2)
                pe.wait_ge(k_ready, i + 1)
                four(1, b[1] + i * 2, [kh_tok[:, t, h, :] for h in heads for t in range(TB)])
                four(2, None, [qh_tok[:, t, h, NOPE:] for h in heads for t in range(TB)], rows=ROPE)
                if more:
                    q_up(i + 1, 0)
                for k, count in ((0, b[0] + 1 + i * 3), (1, b[1] + 1 + i * 2), (2, b[2] + 1 + i * 2)):
                    bank_ready(k, count)
                for h in heads:
                    k, count = (3, b[3] + i * 2) if h == 0 else (0, b[0] + 1 + i * 3)
                    bank_ready(k, count)
                    for t in range(TB):
                        keys = (t + 1) * P
                        o = bank[:, k, t * P:t * P + keys]
                        pe.matmul(o, qh_t[:, h, t * P:(t + 1) * P], kh_t[:, h, 0:keys], start=True, stop=False)
                        mm = pe.matmul(o, qr_t[:, h, t * P:(t + 1) * P], kr_t[:, 0:keys], start=False, stop=True)
                    mm.then_inc(bank_full[k], 1)
                if more:
                    q_up(i + 1, 1)
                    kv_up(i + 1, 0)
                for h in heads:
                    pe.wait_ge(probs_ready, XH + h + 1 + i * 2)
                    four(1 + h, b[1 + h] + 1 + i * 2, [mprobs[:, h, j * P:(j + 1) * P] for j in range(3)])
                if more:
                    kv_up(i + 1, 1)
                for h in heads:
                    k, count = (3, b[3] + 1 + i * 2) if h == 0 else (0, b[0] + 2 + i * 3)
                    bank_ready(1 + h, b[1 + h] + 2 + i * 2)
                    bank_ready(k, count)
                    if h == 0:
                        pe.wait_ge(acc_free[(pp.group + 1) % 2], slot_count(pp.group + 1) + 1 + i)
                    pe.matmul(bank[:, k, 0:S], vh_tok[:, 0, h, :], mprobs_t[:, h, 0:S], start=True, stop=False)
                    pe.matmul(bank[:, k, P:S], vh_tok[:, 1, h, :], mprobs_t[:, h, S:S + P], start=False,
                              stop=True).then_inc(bank_full[k], 1)

            with pe.Fori(0, PAIRS - 1) as i:
                attend(i, True)
            attend(PAIRS - 1, False)
            for k, per in ((0, 3), (3, 2)):
                bank_ready(k, pp.bank[k] + per * PAIRS)
            wide_out("mo", KB, turned=True)
            xattn(1)
            ffn(1)

        def width_of(n):
            j = n - PH["mp"].unit
            return UK * QW if 0 <= j < 4 * PAIRS and j % 4 < 2 else UW

        flat = "p k s -> p (k s)"
        x_hi32, x_lo_f = x_hi[:, :, :].bitcast(F32), x_lo
        h_hi32 = h_hi[:, :, :].bitcast(F32)
        h_hi_flat, h_lo_flat = h_hi[:, :, :].rearrange(flat), h_lo[:, :, :].rearrange(flat)
        h_hi32_flat = h_hi32.rearrange(flat)

        TURNED = {"pool": (G_X, N_X0), "xo0": (G_FFN, N_F0), "fo0": (G_MIX + KB, N_MLA), "mo": (G_X + KB, N_X1),
                  "xo1": (G_FFN + KB, N_F1), "fo1": (None, N_OUT)}

        @block.scalar
        def _(act):
            def half(s, i=0, per=0, width=None):
                if isinstance(i, int):
                    s, i, per = s + i * per, 0, 0
                if s >= UNITS:
                    return
                width = width or width_of(s)
                slot = s % RING
                act.wait_ge(loaded[slot], i * (16 * per // RING) + 16 * (s // RING + 1))
                if s >= RING:
                    act.wait_ge(unit_used, i * per + s - RING + 1)
                act.activation(w_hi[:, slot, 0:width], raw[:, slot, 0:width], ACT.Copy).then_inc(hi_ready, 1)

            def squares(norm, t, c, src, before):
                before = before + STAT_END[norm] - STATS[norm]
                if not isinstance(before, int) or before > 0:
                    act.wait_ge(stats, before)
                act.activation(junk[:, :], src, ACT.Square, accum_out=sums[:, norm, t, c:c + 1] if isinstance(c, int)
                               else sums[:, norm, t, bass.ds(c, 1)]).then_inc(stats, 1)

            def turned(k, count, dst, kbs, gain):
                act.wait_ge(bank_full[k], count)
                for j, kb in enumerate(kbs):
                    last = act.activation(dst(kb), bank[:, k, j * S:(j + 1) * S], ACT.Copy, scale=gain(kb))
                last.then_inc(halved_hi, 1)

            for n, name in enumerate(("norm_mix_g", "norm_xattn_g", "norm_mem_g", "norm_ffn_g")):
                act.dma_start(gain_rows[32 * n:32 * n + 32, :],
                              a[name].rearrange("l (k p) -> (l k) p", p=P)).then_inc(rows_in, 16)
            act.dma_start(gain_rows2[0:RK, :], a["mla_q_norm_g"].rearrange("l (k p) -> (l k) p", p=P)).then_inc(rows_in, 16)
            act.dma_start(gain_rows2[RK:2 * RK, :], a["mla_kv_norm_g"].rearrange("l (k p) -> (l k) p", p=P)).then_inc(rows_in, 16)
            act.dma_start(pos_i[:, :], a["positions"][0].rearrange("(t p) -> p t", p=P),
                          allow_slow_non_contiguous=True).then_inc(rope_in, 16)
            act.dma_start(freq[:, :], a["inv_freq"].partition_broadcast(P)).then_inc(rope_in, 16)
            act.dma_start(pool_s[:, :], a["pool_scale"][0].partition_broadcast(P)).then_inc(scale_in, 16)

            act.wait_ge(bank_free[0], 1)
            for m in range(KB // 2):
                act.wait_ge(bank_full[m % 4], (2 if m % 4 == 0 else 1) + m // 4)
                for l in range(2):
                    for k in range(2):
                        kb = 2 * m + k
                        last = act.activation(h_hi[:, 16 * l + kb, :], bank[:, m % 4, k * S:(k + 1) * S], ACT.Copy,
                                              scale=gains[:, G_MEM + 16 * l + kb:G_MEM + 16 * l + kb + 1])
                last.then_inc(halved_hi, 1)
            for s in range(AHEAD):
                half(s)
            ph = PH["mem"]
            for j in range(32):
                half(ph.unit + j + AHEAD)
                if j == 0:
                    for t in range(TB):
                        for c in range(NC):
                            squares(N_MEM, t, c, mem[:, t, c * CW:(c + 1) * CW], NC * t + c)
                if j == 2:
                    act.wait_ge(x_in, 16)
                    for t in range(TB):
                        for c in range(NC):
                            squares(N_POOL, t, c, x[:, t, c * CW:(c + 1) * CW], NC * t + c)
                if j == 6:
                    act.wait_ge(angle_ready, 1)
                    act.activation(sin[:, :, :], angle_t[:, 1, :, :], ACT.Sin)
                    act.activation(cos[:, :, :], angle_t[:, 2, :, :], ACT.Sin).then_inc(table_ready, 1)
                if j in (8, 24):
                    l = j // 16
                    k_mem = k_mem1 if l else k_mem0
                    for m in range(2):
                        k = 2 * l + m
                        act.wait_ge(bank_full[k], 4 if k == 0 else 3)
                        act.activation(k_mem[:, 2 * m:2 * m + 2, :].rearrange(flat), bank[:, k, :],
                                       ACT.Copy).then_inc(bank_free[k], 1)
                if j >= 24:
                    m = j - 24
                    k = m % 4
                    turned(k, PH["pool"].bank[k] - 1 + m // 4, lambda kb: x_hi[:, kb, :], (2 * m, 2 * m + 1),
                           lambda kb: gains[:, G_MIX + kb:G_MIX + kb + 1])

            def chunk_squares(name, c, xslot, g, count):
                act.wait_ge(acc_free[g % 2], count)
                for t in range(TB):
                    src = xs[:, xslot, t, :] if name != "fo1" else x[:, t, bass.ds(c * CW, CW)]
                    squares(TURNED[name][1], t, c, src, c * 2 + t)

            def chunk_turned(name, c, b2):
                gain = TURNED[name][0]
                for m in range(2):
                    if isinstance(c, int):
                        c0 = c * CK + 2 * m
                        turned(2 + m, b2, lambda kb: x_hi[:, kb, :], (c0, c0 + 1),
                               lambda kb: gains[:, gain + kb:gain + kb + 1])
                    else:
                        c0 = c * CK + 2 * m
                        turned(2 + m, b2, lambda kb: x_hi[:, bass.ds(kb, 1), :].rearrange(flat), (c0, c0 + 1),
                               lambda kb: gains[:, bass.ds(kb + gain, 1)])

            def narrow_out(name):
                ph = PH[name]
                for c in range(NC):
                    g = ph.group + c
                    for j in range(2):
                        half(ph.unit + 2 * c + j + AHEAD)
                        if j == 0 and c > 0:
                            chunk_turned(name, c - 1, ph.bank[2] + c)
                    chunk_squares(name, c, c % 2, g, slot_count(g) + 1)
                chunk_turned(name, NC - 1, ph.bank[2] + NC)

            def wide_out(name, nk):
                ph, per = PH[name], nk // UK

                def two(i):
                    for c in range(2):
                        g = ph.group + c
                        for j in range(per):
                            half(ph.unit + per * c + j + AHEAD, i, 2 * per)
                            if c == 1 and j == 0 and name != "fo1":
                                chunk_turned(name, i * 2, i * 2 + ph.bank[2] + 1)
                        chunk_squares(name, i * 2 + c, c, g, i + slot_count(g) + 1)
                    if name != "fo1":
                        chunk_turned(name, i * 2 + 1, i * 2 + ph.bank[2] + 2)

                if name == "fo1":
                    for i in range(NC // 2):
                        two(i)
                else:
                    with act.Fori(0, NC // 2) as i:
                        two(i)

            def by_token(g, count, unit_count, dst, scale, width=CW):
                act.wait_ge(unit_used, unit_count)
                for t in range(TB):
                    last = act.activation(dst(t), acc[:, g % 2, t, 0:width], ACT.Copy, scale=scale(t))
                last.then_inc(acc_free[g % 2], 1)

            def xattn(l):
                ph = PH[f"xq{l}"]
                norm, b = (N_X0, N_X1)[l], ph.bank
                for j in range(8):
                    half(ph.unit + j + AHEAD)
                act.wait_ge(rs_ready, norm + 1)
                by_token(ph.group, None, ph.unit + 8, lambda t: q_tok[:, t, :], lambda t: rsq[:, norm, t:t + 1])
                for m in range(2):
                    act.wait_ge(bank_full[m], b[m] + 1)
                    act.activation(q_t[:, 2 * m:2 * m + 2, :].rearrange(flat), bank[:, m, :],
                                   ACT.Copy).then_inc(bank_free[m], 1)

                def exps(h):
                    act.wait_ge(max_ready, XH * l + h + 1)
                    for t in range(TB):
                        last = act.activation(probs[:, h % 2, t, :], bank[:, h % 2, t * S:(t + 1) * S], ACT.Exp,
                                              bias=neg_max[:, h, t:t + 1], accum_out=exp_sum[:, h, t:t + 1])
                    last.then_inc(bank_free[h % 2], 1)

                def output(h):
                    act.wait_ge(bank_full[3], b[3] + h + 1)
                    act.activation(h_hi[:, h, :], bank[:, 3, 0:S], ACT.Copy).then_inc(halved_hi, 1)

                exps(0)
                exps(1)
                exps(2)
                output(0)
                exps(3)
                output(1)
                output(2)
                output(3)
                narrow_out(f"xo{l}")

            def ffn(l):
                ph, norm = PH[f"fi{l}"], (N_F0, N_F1)[l]

                def hidden(i):
                    for m in range(2):
                        act.wait_ge(bank_full[m], i + ph.bank[m] + 1)
                        act.activation(h_hi_flat[:, bass.ds(i * (CK * S) + 2 * m * S, 2 * S)], bank[:, m, :],
                                       ACT.Copy).then_inc(halved_hi, 1)

                def pair(i, first):
                    for j in range(16):
                        half(ph.unit + j + AHEAD, i, 16)
                        if j == 0 and not first:
                            hidden(i - 1)
                        if j == 7:
                            if first:
                                act.wait_ge(rs_ready, norm + 1)
                                act.wait_ge(x_back, ph.chunk)
                            act.wait_ge(unit_used, i * 16 + ph.unit + 8)
                            for t in range(TB):
                                last = act.activation(s_tok[:, t, :], acc[:, ph.group % 2, t, :], ACT.Silu,
                                                      scale=rs[:, norm, t:t + 1])
                            last.then_inc(acc_free[ph.group % 2], 1)

                pair(0, True)
                with act.Fori(1, NP) as i:
                    pair(i, False)
                hidden(NP - 1)
                if l == 1:
                    act.wait_ge(unit_used, PH["fo1"].unit)
                    act.dma_start(g_out[:, :], a["final_norm_g"].partition_broadcast(P)).then_inc(g_in, 16)
                wide_out(f"fo{l}", FK)

            narrow_out("pool")
            xattn(0)
            ffn(0)

            ph, pp = PH["mi"], PH["mp"]
            cq, ckv, kr = ph.group, ph.group + 1, ph.group + 2

            def latent(g, n, dst, norm):
                by_token(g, None, n, lambda t: dst[:, t, :], lambda t: rs[:, N_MLA, t:t + 1])
                act.wait_ge(acc_free[g % 2], slot_count(g) + 1)
                for t in range(TB):
                    squares(norm, t, 0, dst[:, t, :], t)

            def latent_turned(k, count, m, kb0, gain):
                turned(k, count, lambda kb: h_hi[:, kb0 + kb, :], (2 * m, 2 * m + 1),
                       lambda kb: gains[:, gain + kb:gain + kb + 1])

            for j in range(17):
                half(ph.unit + j + AHEAD)
                if j == 7:
                    act.wait_ge(rs_ready, N_MLA + 1)
                    latent(cq, ph.unit + 8, cq_tok, N_CQ)
                if j == 8:
                    for m in range(2):
                        latent_turned(m, ph.bank[m] + 1, m, 16, G_CQ)
                if j == 15:
                    latent(ckv, ph.unit + 16, ckv_tok, N_CKV)
                if j == 16:
                    by_token(kr, None, ph.unit + 17, lambda t: kr_tok[:, t, :], lambda t: rs[:, N_MLA, t:t + 1], ROPE)

            def queries(i):
                by_token(pp.group, None, i * 4 + pp.unit + 2,
                         lambda t: qh_tok[:, t, :, :].rearrange("p h n -> p (h n)"), lambda t: rsq[:, N_CQ, t:t + 1], QW)

            half(pp.unit + AHEAD)
            half(pp.unit + 1 + AHEAD)
            for m in range(2):
                latent_turned(2 + m, ph.bank[2 + m] + 1, m, 20, G_CKV)
            act.wait_ge(bank_full[0], ph.bank[0] + 2)
            act.activation(kr_t[:, :], bank[0:ROPE, 0, 0:S], ACT.Copy).then_inc(bank_free[0], 1)
            act.wait_ge(rs_ready, N_CQ + 1)
            queries(0)
            half(pp.unit + 2 + AHEAD)
            half(pp.unit + 3 + AHEAD)

            def attend(i, more):
                b = pp.bank

                def ahead(j):
                    if more:
                        n = pp.unit + 4 + j + AHEAD
                        half(n, i, 4, width_of(n + (i * 4 if isinstance(i, int) else 0)))

                act.wait_ge(bank_full[0], i * 3 + b[0] + 1)
                act.activation(qh_t[:, :, :].rearrange(flat), bank[:, 0, :], ACT.Copy).then_inc(bank_free[0], 1)
                act.wait_ge(bank_full[2], i * 2 + b[2] + 1)
                act.activation(qr_t[:, :, :].rearrange(flat), bank[0:ROPE, 2, :], ACT.Copy).then_inc(bank_free[2], 1)
                ahead(0)
                for h in range(2):
                    k, count = (3, i * 2 + b[3] + 1) if h == 0 else (0, i * 3 + b[0] + 2)
                    act.wait_ge(bank_free[k], count)
                    for t, cols in enumerate((slice(0, P), slice(P, 3 * P))):
                        last = act.activation(mprobs[:, h, cols], neg_s[:, h, cols], ACT.Exp, scale=-1.0,
                                              bias=neg_max[:, h, t:t + 1], accum_out=exp_sum[:, h, t:t + 1])
                    last.then_inc(exp_ready, 1)
                ahead(1)
                if more:
                    queries(i + 1)
                ahead(2)
                ahead(3)
                for h in range(2):
                    k, count = (3, i * 2 + b[3] + 2) if h == 0 else (0, i * 3 + b[0] + 3)
                    act.wait_ge(bank_full[k], count)
                    act.activation(h_hi_flat[:, bass.ds(i * (2 * S) + h * S, S)], bank[:, k, 0:S],
                                   ACT.Copy).then_inc(halved_hi, 1)

            with act.Fori(0, PAIRS - 2) as i:
                attend(i, True)
            attend(PAIRS - 2, True)
            attend(PAIRS - 1, False)
            wide_out("mo", KB)
            xattn(1)
            ffn(1)
            act.wait_ge(rs_ready, N_OUT + 1)
            act.wait_ge(xg_ready, NC)
            act.activation(xg[:, 1, :], xg[:, 1, :], ACT.Copy, scale=rs[:, N_OUT, 1:2]).then_inc(y_ready[1], 1)

        @block.vector
        def _(dve):
            steps = [0]

            def step(ins):
                steps[0] += 1
                ins.then_inc(dve_step, 1)
                dve.wait_ge(dve_step, steps[0])

            def low(s, i=0, per=0, width=None):
                if isinstance(i, int):
                    s, i, per = s + i * per, 0, 0
                if s >= UNITS:
                    return
                width = width or width_of(s)
                slot = s % RING
                dve.wait_ge(hi_ready, i * per + s + 1)
                dve.tensor_tensor(w_lo[:, slot, 0:width], raw[:, slot, 0:width],
                                  w_hi[:, slot, 0:width].bitcast(F32), ALU.subtract).then_inc(lo_ready, 1)

            def turned(k, count, dst, hi32, kbs, gain):
                dve.wait_ge(halved_hi, count)
                for j, kb in enumerate(kbs):
                    last = dve.scalar_tensor_tensor(out=dst(kb), in0=bank[:, k, j * S:(j + 1) * S], scalar=gain(kb),
                                                    in1=hi32(kb), op0=ALU.mult, op1=ALU.subtract)
                last.then_inc(bank_free[k], 1)

            def variance(norm, width=D):
                dve.wait_ge(stats, STAT_END[norm])
                if width == D:
                    step(dve.tensor_reduce(total[:, norm, :], sums[:, norm, :, :], AX_X, ALU.add))
                    src = total[:, norm, :]
                else:
                    src = sums[:, norm, :, 0]
                dve.tensor_scalar(var[:, norm, :], src, 1.0 / width, EPS, ALU.mult, ALU.add).then_inc(var_ready, 1)

            def rope_angles():
                dve.wait_ge(rope_in, 32)
                step(dve.tensor_copy(pos_f[:, :], pos_i[:, :]))
                for t in range(TB):
                    ins = dve.tensor_scalar(angle_t[:, 0, t, :], freq[:, :], pos_f[:, t:t + 1], None, ALU.mult)
                step(ins)
                r, whole = angle_t[:, 0, :, :], angle_t[:, 3, :, :]
                for block_of in (2048.0, 1.0):
                    step(dve.tensor_scalar(whole, r, 1.0 / (TWO_PI * block_of), ROUND, ALU.mult, ALU.add))
                    step(dve.tensor_scalar(whole, whole, ROUND, None, ALU.subtract))
                    for part in TWO_PI_PARTS:
                        step(dve.scalar_tensor_tensor(out=angle_t[:, 1, :, :], in0=whole, scalar=-part * block_of,
                                                      in1=r, op0=ALU.mult, op1=ALU.add))
                        r = angle_t[:, 1, :, :]
                step(dve.tensor_scalar(r, r, 3.1415925, -3.1415925, ALU.min, ALU.max))
                step(dve.tensor_scalar(whole, r, -1.0, None, ALU.mult))
                step(dve.tensor_tensor(whole, whole, r, ALU.max))
                dve.tensor_scalar(angle_t[:, 2, :, :], whole, -1.0, TWO_PI / 4, ALU.mult, ALU.add).then_inc(angle_ready, 1)

            dve.wait_ge(bank_full[0], 1)
            dve.tensor_copy(gains[:, :], bank[:, 0, 0:136]).then_inc(bank_free[0], 1)
            dve.wait_ge(bank_free[0], 1)
            for m in range(KB // 2):
                dve.wait_ge(halved_hi, m + 1)
                for l in range(2):
                    for k in range(2):
                        kb = 16 * l + 2 * m + k
                        last = dve.scalar_tensor_tensor(
                            out=h_lo[:, kb, :], in0=bank[:, m % 4, k * S:(k + 1) * S],
                            scalar=gains[:, G_MEM + kb:G_MEM + kb + 1], in1=h_hi32[:, kb, :],
                            op0=ALU.mult, op1=ALU.subtract)
                last.then_inc(bank_free[m % 4], 1)
            for s in range(AHEAD):
                low(s)
            ph = PH["mem"]
            for j in range(32):
                low(ph.unit + j + AHEAD)
                if j == 0:
                    rope_angles()
                if j == 2:
                    variance(N_MEM)
                if j == 4:
                    variance(N_POOL)
                if j == 10:
                    dve.wait_ge(band_in, 16)
                    dve.wait_ge(rs_ready, N_POOL + 1)
                    for t in range(TB):
                        dve.tensor_scalar(band_of[t], band_of[t], rs[:, N_POOL, t:t + 1], None,
                                          ALU.mult).then_inc(bands_ready, 1)
                if j % 8 == 7:
                    g = ph.group + j // 8
                    l, values = j // 16, j // 8 % 2
                    if j == 7:
                        dve.wait_ge(rs_ready, N_MEM + 1)
                    dve.wait_ge(unit_used, ph.unit + j + 1)
                    v_mem = (v_mem0, v_mem1)[l]
                    for t in range(TB):
                        dst = v_mem[:, t, :, :].rearrange("p h n -> p (h n)") if values else k_tok[:, t, :]
                        last = dve.tensor_scalar(dst, acc[:, g % 2, t, :], rs[:, N_MEM, t:t + 1], None, ALU.mult)
                    last.then_inc(acc_free[g % 2], 1)
                if j >= 24:
                    m = j - 24
                    turned(m % 4, PH["mem"].half + 8 + m + 1, lambda kb: x_lo[:, kb, :], lambda kb: x_hi32[:, kb, :],
                           (2 * m, 2 * m + 1), lambda kb: gains[:, G_MIX + kb:G_MIX + kb + 1])

            def add_chunk(name, c, xslot, g, count, units, chunk):
                dve.wait_ge(unit_used, units)
                if name == "fo1":
                    for t in range(TB):
                        xc = x[:, t, c * CW:(c + 1) * CW]
                        last = dve.tensor_tensor(xc, acc[:, g % 2, t, :], xc, ALU.add)
                    last.then_inc(acc_free[g % 2], 1)
                    return
                if not isinstance(chunk, int) or chunk > 1:
                    dve.wait_ge(x_back, chunk - 1)
                dst = xs[:, xslot, :, :]
                old = x[:, :, c * CW:(c + 1) * CW] if isinstance(c, int) else x[:, :, bass.ds(c * CW, CW)]
                if name == "pool":
                    if c == 0:
                        dve.wait_ge(scale_in, 16)
                    for t in range(TB):
                        last = dve.tensor_tensor(dst[:, t, :], acc[:, g % 2, t, :], pool_s[:, c * CW:(c + 1) * CW],
                                                 ALU.mult)
                    step(last)
                    dve.tensor_tensor(dst, dst, old, ALU.add).then_inc(acc_free[g % 2], 1)
                else:
                    for t in range(TB):
                        last = dve.tensor_tensor(dst[:, t, :], acc[:, g % 2, t, :], old[:, t, :], ALU.add)
                    last.then_inc(acc_free[g % 2], 1)

            def chunk_turned(name, c, half0):
                gain = TURNED[name][0]
                for m in range(2):
                    c0 = c * CK + 2 * m
                    if isinstance(c, int):
                        turned(2 + m, half0 + m + 1, lambda kb: x_lo[:, kb, :], lambda kb: x_hi32[:, kb, :], (c0, c0 + 1),
                               lambda kb: gains[:, gain + kb:gain + kb + 1])
                    else:
                        turned(2 + m, half0 + m + 1, lambda kb: x_lo[:, bass.ds(kb, 1), :].rearrange(flat),
                               lambda kb: x_hi32[:, bass.ds(kb, 1), :].rearrange(flat), (c0, c0 + 1),
                               lambda kb: gains[:, bass.ds(kb + gain, 1)])

            def narrow_out(name):
                ph = PH[name]
                for c in range(NC):
                    g = ph.group + c
                    for j in range(2):
                        low(ph.unit + 2 * c + j + AHEAD)
                        if j == 0 and c > 0:
                            chunk_turned(name, c - 1, ph.half + 2 * (c - 1))
                    add_chunk(name, c, c % 2, g, slot_count(g), ph.unit + 2 * c + 2, ph.chunk + c)
                chunk_turned(name, NC - 1, ph.half + 2 * (NC - 1))

            def wide_out(name, nk):
                ph, per = PH[name], nk // UK

                def two(i):
                    for c in range(2):
                        g = ph.group + c
                        for j in range(per):
                            low(ph.unit + per * c + j + AHEAD, i, 2 * per)
                            if c == 1 and j == 0 and name != "fo1":
                                chunk_turned(name, i * 2, i * 4 + ph.half)
                        add_chunk(name, i * 2 + c, c, g, i + slot_count(g), i * (2 * per) + ph.unit + per * (c + 1),
                                  i * 2 + ph.chunk + c)
                    if name != "fo1":
                        chunk_turned(name, i * 2 + 1, i * 4 + ph.half + 2)

                if name == "fo1":
                    for i in range(NC // 2):
                        two(i)
                else:
                    with dve.Fori(0, NC // 2) as i:
                        two(i)

            def xattn(l):
                ph = PH[f"xq{l}"]
                b, norm = ph.bank, (N_X0, N_X1)[l]
                for j in range(8):
                    low(ph.unit + j + AHEAD)
                    if j == 0:
                        variance(norm)

                def maximum(h):
                    dve.wait_ge(bank_full[h % 2], b[h % 2] + 2 + h // 2)
                    dve.tensor_reduce(neg_max[:, h, :], bank[:, h % 2, :].rearrange("p (t k) -> p t k", t=TB), AX_X,
                                      ALU.max, negate=True).then_inc(max_ready, 1)

                def normalise(h):
                    dve.wait_ge(bank_free[h % 2], b[h % 2] + 2 + h // 2)
                    step(dve.reciprocal(inv_sum[:, h, :], exp_sum[:, h, :]))
                    for t in range(TB):
                        pr = probs[:, h % 2, t, :]
                        last = dve.tensor_scalar(pr, pr, inv_sum[:, h, t:t + 1], None, ALU.mult)
                    last.then_inc(probs_ready, 1)

                def copy_probs(h):
                    dve.wait_ge(bank_full[2], b[2] + h + 1)
                    dve.tensor_copy(probs_t[:, h % 2, :, :].rearrange(flat), bank[:, 2, :]).then_inc(bank_free[2], 1)

                def output(h):
                    dve.wait_ge(halved_hi, ph.half + h + 1)
                    dve.tensor_tensor(h_lo[:, h, :], bank[:, 3, 0:S], h_hi32[:, h, :],
                                      ALU.subtract).then_inc(bank_free[3], 1)

                maximum(0)
                maximum(1)
                for h in range(XH):
                    normalise(h)
                    copy_probs(h)
                    if h + 2 < XH:
                        maximum(h + 2)
                    if h:
                        output(h - 1)
                output(XH - 1)
                narrow_out(f"xo{l}")

            def ffn(l):
                ph, norm = PH[f"fi{l}"], (N_F0, N_F1)[l]

                def hidden(i):
                    for m in range(2):
                        cols = bass.ds(i * (CK * S) + 2 * m * S, 2 * S)
                        dve.wait_ge(halved_hi, i * 2 + ph.half + m + 1)
                        dve.tensor_tensor(h_lo_flat[:, cols], bank[:, m, :], h_hi32_flat[:, cols],
                                          ALU.subtract).then_inc(bank_free[m], 1)

                def pair(i, first):
                    g = ph.group + 1
                    for j in range(16):
                        low(ph.unit + j + AHEAD, i, 16)
                        if j == 0 and first:
                            variance(norm)
                        if j == 0 and not first:
                            hidden(i - 1)
                        if j == 15:
                            if first:
                                dve.wait_ge(rs_ready, norm + 1)
                                dve.wait_ge(x_back, ph.chunk)
                            dve.wait_ge(acc_free[ph.group % 2], i + slot_count(ph.group) + 1)
                            dve.wait_ge(unit_used, i * 16 + ph.unit + 16)
                            for t in range(TB):
                                last = dve.scalar_tensor_tensor(
                                    out=h_tok[:, t, :], in0=acc[:, g % 2, t, :], scalar=rs[:, norm, t:t + 1],
                                    in1=s_tok[:, t, :], op0=ALU.mult, op1=ALU.mult)
                            last.then_inc(acc_free[g % 2], 1)

                pair(0, True)
                with dve.Fori(1, NP) as i:
                    pair(i, False)
                hidden(NP - 1)
                wide_out(f"fo{l}", FK)

            narrow_out("pool")
            xattn(0)
            ffn(0)

            ph, pp = PH["mi"], PH["mp"]

            def latent_turned(k, count, m, kb0, gain):
                turned(k, count, lambda kb: h_lo[:, kb0 + kb, :], lambda kb: h_hi32[:, kb0 + kb, :], (2 * m, 2 * m + 1),
                       lambda kb: gains[:, gain + kb:gain + kb + 1])

            for j in range(17):
                low(ph.unit + j + AHEAD)
                if j == 0:
                    variance(N_MLA)
                if j == 8:
                    variance(N_CQ, RANK)
                    for m in range(2):
                        latent_turned(m, ph.half + m + 1, m, 16, G_CQ)
                if j == 16:
                    variance(N_CKV, RANK)

            kv = pp.group + 1

            def heads_kv(i, dst, c0, done):
                dve.wait_ge(unit_used, i * 4 + pp.unit + 4)
                for t in range(TB):
                    src = acc[:, kv % 2, t, :].rearrange("p (h n) -> p h n", h=2)[:, :, c0:c0 + P]
                    last = dve.tensor_scalar(dst[:, t, :, :], src, rs[:, N_CKV, t:t + 1], None, ALU.mult)
                last.then_inc(done, 1)

            low(pp.unit + AHEAD)
            low(pp.unit + 1 + AHEAD)
            for m in range(2):
                latent_turned(2 + m, ph.half + 2 + m + 1, m, 20, G_CKV)
            low(pp.unit + 2 + AHEAD)
            low(pp.unit + 3 + AHEAD)
            dve.wait_ge(rs_ready, N_CKV + 1)
            dve.wait_ge(mask_ready, 2)
            heads_kv(0, kh_tok, 0, k_ready)

            def attend(i, more):
                b = pp.bank

                def ahead(j):
                    if more:
                        n = pp.unit + 4 + j + AHEAD
                        low(n, i, 4, width_of(n + (i * 4 if isinstance(i, int) else 0)))

                dve.wait_ge(bank_full[1], i * 2 + b[1] + 1)
                dve.tensor_copy(kh_t[:, :, :].rearrange(flat), bank[:, 1, :]).then_inc(bank_free[1], 1)
                heads_kv(i, vh_tok, NOPE, acc_free[kv % 2])
                ahead(0)
                for h in range(2):
                    k, count = (3, i * 2 + b[3] + 1) if h == 0 else (0, i * 3 + b[0] + 2)
                    dve.wait_ge(bank_full[k], count)
                    dve.memset(pace[:, h:h + 1], 0.0)
                    for t, (cols, m) in enumerate(((slice(0, P), mask[:, P:S]), (slice(P, 3 * P), mask[:, :]))):
                        last = dve.tensor_tensor_reduce(neg_s[:, h, cols], bank[:, k, cols], m, -1.0, 3.0e38, ALU.add,
                                                        ALU.min, neg_max[:, h, t:t + 1])
                    last.then_inc(bank_free[k], 1)
                ahead(1)
                for h in range(2):
                    dve.wait_ge(exp_ready, i * 2 + h + 1)
                    dve.reciprocal(inv_sum[:, h, :], exp_sum[:, h, :]).then_inc(dve_recip, 1)
                    dve.wait_ge(dve_recip, i * 2 + h + 1)
                    for t, cols in enumerate((slice(0, P), slice(P, 3 * P))):
                        last = dve.tensor_scalar(mprobs[:, h, cols], mprobs[:, h, cols], inv_sum[:, h, t:t + 1], None,
                                                 ALU.mult)
                    last.then_inc(probs_ready, 1)
                ahead(2)
                for h in range(2):
                    dve.wait_ge(bank_full[1 + h], i * 2 + b[1 + h] + 2)
                    dve.tensor_copy(mprobs_t[:, h, :], bank[:, 1 + h, 0:3 * P]).then_inc(bank_free[1 + h], 1)
                ahead(3)
                if more:
                    heads_kv(i + 1, kh_tok, 0, k_ready)
                for h in range(2):
                    k = 3 if h == 0 else 0
                    cols = bass.ds(i * (2 * S) + h * S, S)
                    dve.wait_ge(halved_hi, i * 2 + pp.half + h + 1)
                    dve.tensor_tensor(h_lo_flat[:, cols], bank[:, k, 0:S], h_hi32_flat[:, cols],
                                      ALU.subtract).then_inc(bank_free[k], 1)

            with dve.Fori(0, PAIRS - 2) as i:
                attend(i, True)
            attend(PAIRS - 2, True)
            attend(PAIRS - 1, False)
            wide_out("mo", KB)
            xattn(1)
            ffn(1)
            variance(N_OUT)
            dve.wait_ge(rs_ready, N_OUT + 1)
            dve.wait_ge(xg_ready, NC)
            dve.tensor_scalar(xg[:, 0, :], xg[:, 0, :], rs[:, N_OUT, 0:1], None, ALU.mult).then_inc(y_ready[0], 1)

        @block.gpsimd
        def _(pool):
            steps = [0]

            def step(ins):
                steps[0] += 1
                ins.then_inc(pool_step, 1)
                pool.wait_ge(pool_step, steps[0])

            pool.memset(ident[:, :], 0.0).then_inc(ident_ready, 1)
            pool.wait_ge(ident_ready, 1)
            pool.affine_select(out=ident[:, :], in_=ident[:, :], compare_op=ALU.not_equal, fill=1.0, base=0,
                               pattern=[[-1, P]], channel_multiplier=1).then_inc(ident_ready, 1)
            pool.memset(mask[:, :], 0.0).then_inc(mask_ready, 1)
            pool.wait_ge(mask_ready, 1)
            pool.affine_select(out=mask[:, P:S], in_=mask[:, P:S], compare_op=ALU.is_ge, fill=MASK, base=0,
                               pattern=[[-1, P]], channel_multiplier=1).then_inc(mask_ready, 1)
            step(pool.memset(minus_half[:, :], -0.5))

            def inverse_rms(norm, scale=None):
                pool.wait_ge(var_ready, norm + 1)
                ins = pool.tensor_tensor(rs[:, norm, :], var[:, norm, :], minus_half[:, :], ALU.pow)
                if scale is not None:
                    step(ins)
                    ins = pool.tensor_scalar(rsq[:, norm, :], rs[:, norm, :], scale, None, ALU.mult)
                ins.then_inc(rs_ready, 1)

            def write_back(c, xslot, g, count):
                pool.wait_ge(acc_free[g % 2], count)
                dst = x[:, :, c * CW:(c + 1) * CW] if isinstance(c, int) else x[:, :, bass.ds(c * CW, CW)]
                pool.tensor_copy(dst, xs[:, xslot, :, :]).then_inc(x_back, 1)

            def narrow_back(name):
                ph = PH[name]
                for c in range(NC):
                    write_back(c, c % 2, ph.group + c, slot_count(ph.group + c) + 1)

            def wide_back(name):
                ph = PH[name]
                with pool.Fori(0, NC // 2) as i:
                    for c in range(2):
                        write_back(i * 2 + c, c, ph.group + c, i + slot_count(ph.group + c) + 1)

            def rotate(x1, x2, t_shape, done):
                heads = t_shape

                def table(tab):
                    v = tab[:, :, :]
                    return v.unsqueeze(2).to_broadcast([P, TB, heads, HR]) if heads else v

                tmp = [rope_t[:, n, :, :, :] if heads else rope_t[:, n, :, 0, :] for n in range(4)]
                for n, (v, tab) in enumerate(((x1, cos), (x2, sin), (x2, cos), (x1, sin))):
                    ins = pool.tensor_tensor(tmp[n], v, table(tab), ALU.mult)
                ins.then_inc(rope_step, 1)
                return tmp

            inverse_rms(N_MEM)
            inverse_rms(N_POOL)
            narrow_back("pool")
            inverse_rms(N_X0, XSCALE)
            narrow_back("xo0")
            inverse_rms(N_F0)
            wide_back("fo0")
            inverse_rms(N_MLA)
            inverse_rms(N_CQ, MSCALE)
            kr = PH["mi"].group + 2
            pool.wait_ge(table_ready, 1)
            pool.wait_ge(acc_free[kr % 2], slot_count(kr) + 1)
            x1, x2 = kr_tok[:, :, 0:HR], kr_tok[:, :, HR:ROPE]
            tmp = rotate(x1, x2, 0, None)
            pool.wait_ge(rope_step, 1)
            pool.tensor_tensor(x1, tmp[0], tmp[1], ALU.subtract)
            pool.tensor_tensor(x2, tmp[2], tmp[3], ALU.add).then_inc(roped, 1)
            inverse_rms(N_CKV)
            pp = PH["mp"]
            q1, q2 = qh_tok[:, :, :, NOPE:NOPE + HR], qh_tok[:, :, :, NOPE + HR:NOPE + ROPE]
            with pool.Fori(0, PAIRS) as i:
                pool.wait_ge(acc_free[pp.group % 2], i + slot_count(pp.group) + 1)
                tmp = rotate(q1, q2, 2, None)
                pool.wait_ge(rope_step, i + 2)
                pool.tensor_tensor(q1, tmp[0], tmp[1], ALU.subtract)
                pool.tensor_tensor(q2, tmp[2], tmp[3], ALU.add).then_inc(roped, 1)
            wide_back("mo")
            inverse_rms(N_X1, XSCALE)
            narrow_back("xo1")
            inverse_rms(N_F1)
            ph = PH["fo1"]
            pool.wait_ge(g_in, 16)
            for c in range(NC):
                g = ph.group + c
                pool.wait_ge(acc_free[g % 2], slot_count(g) + 1)
                cols = slice(c * CW, (c + 1) * CW)
                gain = g_out[:, cols].unsqueeze(1).to_broadcast([P, TB, CW])
                pool.tensor_tensor(xg[:, :, cols], x[:, :, cols], gain, ALU.mult).then_inc(xg_ready, 1)
            inverse_rms(N_OUT)


def _bands():
    import numpy as np
    t = np.arange(S)[:, None]
    s = np.arange(S)[None, :]
    out = []
    for b in range(TB):
        for w in WINDOWS:
            m = np.where((t <= s) & (s < t + w), 1.0 / np.minimum(s + 1, w), 0.0) - (t == s)
            out.append(m[b * P:(b + 1) * P, b * P:min(S, b * P + REACH)])
    return np.ascontiguousarray(np.concatenate(out, axis=1), dtype=np.float32)


_INS = ["x", "mem", "positions", "norm_mix_g", "norm_xattn_g", "norm_mem_g", "norm_ffn_g", "pool_w", "pool_scale",
        "mla_w_in", "mla_q_norm_g", "mla_w_q_up", "mla_kv_norm_g", "mla_w_kv_up", "mla_w_out", "xattn_w_q",
        "xattn_w_kv", "xattn_w_o", "ffn_w_in", "ffn_w_out", "final_norm_g"]


def kernel(**inputs):
    import numpy as _np
    import concourse.bacc as _bacc
    from concourse import mybir as _mybir
    from concourse.bass_utils import run_bass_kernel_spmd as _run

    nc = _bacc.Bacc("TRN2", target_bir_lowering=False, num_devices=1)
    arrays, args = {}, {}
    given = [(name, inputs[name]) for name in _INS]
    given.append(("bands", _bands()))
    given.append(("inv_freq", (1.0 / 10000.0 ** (_np.arange(0, ROPE, 2) / ROPE)).astype(_np.float32)))
    for name, v in given:
        v = _np.ascontiguousarray(v)
        arrays[f"in_{name}"] = v
        args[name] = nc.dram_tensor(f"in_{name}", v.shape, _mybir.dt.from_np(v.dtype), kind="ExternalInput").ap()
    out = nc.dram_tensor("out_0", (1, S, D), _mybir.dt.from_np(_np.dtype("float32")), kind="ExternalOutput").ap()
    hybrid_kernel(nc, args, out)
    r = _run(nc, [arrays], core_ids=[0])
    return r.results[0]["out_0"]
```

```python
import math
from contextlib import ExitStack

import concourse.bass as bass
from concourse import mybir

F32 = mybir.dt.float32
F32R = mybir.dt.float32r
I32 = mybir.dt.int32
BF16 = mybir.dt.bfloat16
ALU = mybir.AluOpType
ACT = mybir.ActivationFunctionType
AX_X = mybir.AxisListType.X

P = 128
D = 2048
S = 256
TB = S // P
KB = D // P
CW = 512
NC = D // CW
CK = CW // P
F = 5632
FK = F // P
NP = F // CW
XH = 4
HEADS = 16
NOPE, ROPE, VD = 128, 64, 128
HR = ROPE // 2
RANK = 512
RK = RANK // P
QW = 2 * (NOPE + ROPE)
PAIRS = HEADS // 2
WINDOWS = (2, 4, 8, 16)
REACH = P + max(WINDOWS)
EPS = 1e-6
XSCALE = 1.0 / P ** 0.5
MSCALE = 1.0 / (NOPE + ROPE) ** 0.5
MASK = -1e30
RING = 4
UK = 2
UW = UK * CW
AHEAD = RING - 1
BANKS = 4
TWO_PI = 6.283185307179586


def _parts(value, count):
    out = []
    for _ in range(count):
        top = 2.0 ** (math.floor(math.log2(abs(value))) - 11)
        out.append(math.floor(value / top) * top)
        value -= out[-1]
    return out


TWO_PI_PARTS = _parts(TWO_PI, 4)
ROUND = 1.5 * 2.0 ** 23

N_MEM, N_POOL, N_X0, N_F0, N_MLA, N_CQ, N_CKV, N_X1, N_F1, N_OUT = range(10)
STATS = [8, 8, 8, 8, 8, 2, 2, 8, 8, 8]
STAT_END = [sum(STATS[:n + 1]) for n in range(len(STATS))]

G_MIX, G_X, G_FFN, G_MEM, G_CQ, G_CKV = 0, 32, 64, 96, 128, 132


class Phase:
    pass


def plan():
    table = [
        ("mem", 32, 4, (5, 5, 5, 5), 16, 0),
        ("pool", 8, 4, (0, 0, 4, 4), 8, 4),
        ("xq0", 8, 1, (3, 3, 4, 4), 4, 0), ("xo0", 8, 4, (0, 0, 4, 4), 8, 4),
        ("fi0", 16 * NP, 2 * NP, (NP, NP, 0, 0), 2 * NP, 0), ("fo0", 4 * FK // UK, 4, (0, 0, 4, 4), 8, 4),
        ("mi", 17, 3, (2, 1, 1, 1), 4, 0),
        ("mp", 4 * PAIRS, 2 * PAIRS, (3 * PAIRS, 2 * PAIRS, 2 * PAIRS, 2 * PAIRS), 2 * PAIRS, 0),
        ("mo", 32, 4, (0, 0, 4, 4), 8, 4),
        ("xq1", 8, 1, (3, 3, 4, 4), 4, 0), ("xo1", 8, 4, (0, 0, 4, 4), 8, 4),
        ("fi1", 16 * NP, 2 * NP, (NP, NP, 0, 0), 2 * NP, 0), ("fo1", 4 * FK // UK, 4, (0, 0, 0, 0), 0, 4),
    ]
    phases, u, g, b, h, c = {}, 0, 0, [0] * BANKS, 0, 0
    for name, nu, ng, nb, nh, nc_ in table:
        p = Phase()
        p.unit, p.group, p.bank, p.half, p.chunk = u, g, tuple(b), h, c
        phases[name] = p
        u, g, h, c = u + nu, g + ng, h + nh, c + nc_
        b = [x + y for x, y in zip(b, nb)]
    return phases, u


def hybrid_kernel(nc, a, out):
    PH, UNITS = plan()
    with ExitStack() as ctx:
        def sb(name, shape, dt=F32):
            return ctx.enter_context(nc.sbuf_tensor(name, shape, dt))

        def sem(name):
            return ctx.enter_context(nc.semaphore(name))

        raw = sb("raw", [P, RING, UW])
        w_hi = sb("w_hi", [P, RING, UW], F32R)
        w_lo = sb("w_lo", [P, RING, UW], F32R)
        x = sb("x", [P, TB, D])
        xs = sb("xs", [P, 2, TB, CW])
        k_mem1 = sb("k_mem1", [P, XH, S])
        v_mem1 = sb("v_mem1", [P, TB, XH, P])
        area_x = nc.sbuf_base
        sb("area_x", [P, 2 * KB * S])
        area_h = nc.sbuf_base
        sb("area_h", [P, 2 * FK * S])
        small = {}
        for name, shape, dt in (
                ("gains", [P, 136], F32), ("mem_gain_rows", [2 * KB, P], F32), ("gain_rows", [6 * KB, P], F32), ("gain_rows2", [2 * RK, P], F32),
                ("ident", [P, P], F32), ("mask", [P, S], F32), ("cos", [P, TB, HR], F32), ("sin", [P, TB, HR], F32),
                ("junk", [P, CW], BF16), ("sums", [P, 10, TB, NC], F32), ("var", [P, 10, TB], F32),
                ("total", [P, 10, TB], F32), ("rs", [P, 10, TB], F32), ("rsq", [P, 10, TB], F32),
                ("minus_half", [P, TB], F32), ("pace", [P, 2], F32), ("neg_max", [P, HEADS, TB], F32),
                ("exp_sum", [P, HEADS, TB], F32), ("inv_sum", [P, HEADS, TB], F32)):
            small[name] = sb(name, shape, dt)
        gains, mem_gain_rows, gain_rows, gain_rows2 = (
            small[n] for n in ("gains", "mem_gain_rows", "gain_rows", "gain_rows2"))
        ident, mask, cos, sin, junk = (small[n] for n in ("ident", "mask", "cos", "sin", "junk"))
        sums, var, total, rs, rsq = (small[n] for n in ("sums", "var", "total", "rs", "rsq"))
        minus_half, pace, neg_max, exp_sum, inv_sum = (
            small[n] for n in ("minus_half", "pace", "neg_max", "exp_sum", "inv_sum"))

        def at(name, shape, offset, dt=F32):
            return nc.alloc_sbuf_tensor_at(name, shape, dt, offset=offset)

        KBYTES = S * 4
        x_hi = at("x_hi", [P, KB, S], area_x, F32R)
        x_lo = at("x_lo", [P, KB, S], area_x + KB * KBYTES, F32R)
        mem = at("mem_tok", [P, TB, D], area_x)
        g_out = at("g_out", [P, D], area_x)
        xg = at("xg", [P, TB, D], area_x + KB * KBYTES)
        h_hi = at("h_hi", [P, FK, S], area_h, F32R)
        lo0 = area_h + FK * KBYTES
        h_lo = at("h_lo", [P, FK, S], lo0, F32R)
        r1, r2 = area_h + 32 * KBYTES, lo0 + 32 * KBYTES
        k_mem0 = at("k_mem0", [P, XH, S], r1)
        v_mem0 = at("v_mem0", [P, TB, XH, P], r1 + 4 * KBYTES)
        k_tok = at("k_tok", [P, TB, CW], r1 + 8 * KBYTES)
        pool_s = at("pool_s", [P, D], r2)
        xa = area_h + 8 * KBYTES
        q_tok = at("q_tok", [P, TB, CW], xa)
        q_t = at("q_t", [P, XH, S], xa + 4 * KBYTES)
        probs = at("probs", [P, 2, TB, S], xa + 8 * KBYTES)
        probs_t = at("probs_t", [P, 2, TB, S], xa + 12 * KBYTES)
        ma, mb = area_h + 24 * KBYTES, lo0 + 24 * KBYTES
        cq_tok = at("cq_tok", [P, TB, RANK], ma)
        ckv_tok = at("ckv_tok", [P, TB, RANK], ma + 4 * KBYTES)
        kh_tok = at("kh_tok", [P, TB, 2, NOPE], ma + 8 * KBYTES)
        vh_tok = at("vh_tok", [P, TB, 2, VD], ma + 10 * KBYTES)
        qh_tok = at("qh_tok", [P, TB, 2, NOPE + ROPE], ma + 12 * KBYTES)
        kr_tok = at("kr_tok", [P, TB, ROPE], ma + 15 * KBYTES)
        rope_t = at("rope_t", [P, 4, TB, 2, HR], ma + 16 * KBYTES)
        qh_t = at("qh_t", [P, 2, S], mb)
        kh_t = at("kh_t", [P, 2, S], mb + 2 * KBYTES)
        qr_t = at("qr_t", [ROPE, 2, S], mb + 4 * KBYTES)
        kr_t = at("kr_t", [ROPE, S], mb + 6 * KBYTES)
        neg_s = at("neg_s", [P, 2, 3 * P], mb + 7 * KBYTES)
        mprobs = at("mprobs", [P, 2, 3 * P], mb + 10 * KBYTES)
        mprobs_t = at("mprobs_t", [P, 2, 3 * P], mb + 13 * KBYTES)
        BAND = 4 * (REACH + P)
        bands = xs[:, :, :, :].rearrange("p a b n -> p (a b n)")[:, 0:BAND]
        band_of = (bands[:, 0:4 * REACH].rearrange("p (g n) -> p g n", g=4),
                   bands[:, 4 * REACH:BAND].rearrange("p (g n) -> p g n", g=4))
        s_tok, h_tok = xs[:, 0, :, :], xs[:, 1, :, :]
        angle_t = at("angle_t", [P, 6, TB, HR], r2 + 8 * KBYTES)
        pos_i = at("pos_i", [P, TB], r2 + 8 * KBYTES + 6 * TB * HR * 4, I32)
        pos_f = at("pos_f", [P, TB], r2 + 8 * KBYTES + 6 * TB * HR * 4 + 32)
        freq = at("freq", [P, HR], r2 + 8 * KBYTES + 6 * TB * HR * 4 + 64)

        acc = ctx.enter_context(nc.psum_tensor("acc", [P, 2, TB, CW], F32))
        bank = ctx.enter_context(nc.psum_tensor("bank", [P, BANKS, CW], F32))

        loaded = [sem(f"loaded{s}") for s in range(RING)]
        hi_ready = sem("hi_ready")
        lo_ready = sem("lo_ready")
        unit_used = sem("unit_used")
        acc_free = [sem(f"acc_free{s}") for s in range(2)]
        bank_full = [sem(f"bank_full{k}") for k in range(BANKS)]
        bank_free = [sem(f"bank_free{k}") for k in range(BANKS)]
        halved_hi = sem("halved_hi")
        stats = sem("stats")
        var_ready = sem("var_ready")
        rs_ready = sem("rs_ready")
        x_back = sem("x_back")
        k_ready = sem("k_ready")
        roped = sem("roped")
        max_ready = sem("max_ready")
        exp_ready = sem("exp_ready")
        probs_ready = sem("probs_ready")
        mem_in = [sem(f"mem_in{c}") for c in range(NC)]
        x_in, band_in, mem_row_in, rows_in, rope_in, scale_in, g_in = (
            sem(n) for n in ("x_in", "band_in", "mem_row_in", "rows_in", "rope_in", "scale_in", "g_in"))
        gain_cols = sem("gain_cols")
        gains_ready = sem("gains_ready")
        ident_ready, mask_ready, half_ready = sem("ident_ready"), sem("mask_ready"), sem("half_ready")
        bands_ready, angle_ready, table_ready = (sem(n) for n in ("bands_ready", "angle_ready", "table_ready"))
        dve_step, pool_step = sem("dve_step"), sem("pool_step")
        dve_recip, rope_step = sem("dve_recip"), sem("rope_step")
        xg_ready, stored = sem("xg_ready"), sem("stored")
        y_ready = [sem(f"y_ready{t}") for t in range(TB)]

        def slot_count(g):
            return g // 2

        def weights(w, k0, kbs, c0, width):
            return w[k0 * P:(k0 + kbs) * P, bass.ds(c0, width)].rearrange("(b p) n -> p b n", p=P)

        block = ctx.enter_context(nc.Block())

        @block.sync
        def _(sp):
            def load(n, slot, w, k0, c0, kbs=UK, width=CW):
                if not isinstance(n, int) or n >= RING:
                    sp.wait_ge(lo_ready, n - RING + 1)
                sp.dma_start(raw[:, slot, 0:kbs * width].rearrange("p (b n) -> p b n", b=kbs),
                             weights(w, k0, kbs, c0, width)).then_inc(loaded[slot], 16)

            def group(n, base, w, c0, nk, width=CW):
                for j in range(nk // UK):
                    load(n + j, (base + j) % RING, w, UK * j, c0, width=width)

            mem_v = a["mem"][0].rearrange("(t p) d -> p t d", p=P)

            def memory(c):
                cols = slice(c * CW, (c + 1) * CW)
                sp.dma_start(mem[:, :, cols], mem_v[:, :, cols]).then_inc(mem_in[c], 16)

            memory(0)
            for j in range(RING):
                load(j, j, a["xattn_w_kv"][0], UK * j, 0)
                if j == 1:
                    memory(1)
            memory(2)
            memory(3)
            for j in range(RING, 8):
                load(j, j % RING, a["xattn_w_kv"][0], UK * j, 0)
            for l in range(2):
                for c in range(2):
                    n = PH["mem"].unit + 16 * l + 8 * c
                    if n > 0:
                        group(n, n, a["xattn_w_kv"][l], c * CW, KB)
                    if l == 0 and c == 0:
                        sp.dma_start(x[:, :, :], a["x"][0].rearrange("(t p) d -> p t d", p=P)).then_inc(x_in, 16)
                        sp.dma_start(bands, a["bands"]).then_inc(band_in, 16)

            for g in range(len(WINDOWS)):
                n = PH["pool"].unit + 2 * g
                group(n, n, a["pool_w"][0, g], 0, CK)

            def wide_out(base, w, nk):
                per = nk // UK
                with sp.Fori(0, NC // 2) as i:
                    for c in range(2):
                        group(base + per * c + i * (2 * per), base + per * c, w, i * (2 * CW) + c * CW, nk)

            def xattn(l):
                n = PH[f"xq{l}"].unit
                group(n, n, a["xattn_w_q"][l], 0, KB)
                for c in range(NC):
                    n = PH[f"xo{l}"].unit + 2 * c
                    group(n, n, a["xattn_w_o"][l], c * CW, XH)

            def ffn(l):
                base = PH[f"fi{l}"].unit
                with sp.Fori(0, NP) as i:
                    group(base + i * 16, base, a["ffn_w_in"][l], i * CW, KB)
                    group(base + 8 + i * 16, base + 8, a["ffn_w_in"][l], i * CW + F, KB)
                wide_out(PH[f"fo{l}"].unit, a["ffn_w_out"][l], FK)

            xattn(0)
            ffn(0)
            n = PH["mi"].unit
            group(n, n, a["mla_w_in"][0], 0, KB)
            group(n + 8, n + 8, a["mla_w_in"][0], RANK, KB)
            load(n + 16, (n + 16) % RING, a["mla_w_in"][0], 0, 2 * RANK, kbs=KB, width=ROPE)
            base = PH["mp"].unit
            with sp.Fori(0, PAIRS) as i:
                group(base + i * 4, base, a["mla_w_q_up"][0], i * QW, RK, width=QW)
                group(base + 2 + i * 4, base + 2, a["mla_w_kv_up"][0], i * CW, RK)
            wide_out(PH["mo"].unit, a["mla_w_out"][0], KB)
            xattn(1)
            ffn(1)
            out_v = out[0].rearrange("(t p) d -> p t d", p=P)
            for t in range(TB):
                sp.wait_ge(y_ready[t], 1)
                sp.dma_start(out_v[:, t, :], xg[:, t, :]).then_inc(stored, 16)
            sp.wait_ge(stored, 16 * TB)

        @block.tensor
        def _(pe):
            def unit(n, base, src_hi, src_lo, k0, g_slot, first, last, kbs=UK, width=CW):
                slot = base % RING
                pe.wait_ge(lo_ready, n + 1)
                for b in range(kbs):
                    cols = slice(b * width, (b + 1) * width)
                    for t in range(TB):
                        o = acc[:, g_slot, t, 0:width]
                        hi = src_hi[:, k0 + b, t * P:(t + 1) * P]
                        lo = src_lo[:, k0 + b, t * P:(t + 1) * P]
                        pe.matmul(o, hi, w_hi[:, slot, cols], start=(first and b == 0), stop=False)
                        pe.matmul(o, hi, w_lo[:, slot, cols], start=False, stop=False)
                        mm = pe.matmul(o, lo, w_hi[:, slot, cols], start=False, stop=(last and b == kbs - 1))
                mm.then_inc(unit_used, 1)

            def slot_ready(g, count):
                if not isinstance(count, int) or count > 0:
                    pe.wait_ge(acc_free[g % 2], count)

            def bank_ready(k, count):
                if not isinstance(count, int) or count > 0:
                    pe.wait_ge(bank_free[k], count)

            def four(k, count, parts, rows=P):
                if count is not None:
                    bank_ready(k, count)
                for j, src in enumerate(parts):
                    tr = pe.transpose(bank[0:rows, k, j * P:(j + 1) * P], src, ident[:, :])
                tr.then_inc(bank_full[k], 1)

            def turn_chunk(name, c):
                ph = PH[name]
                g = ph.group + c
                pe.wait_ge(acc_free[g % 2], slot_count(g) + 1)
                for m in range(2):
                    four(2 + m, ph.bank[2] + c, [xs[:, c % 2, t, (2 * m + k) * P:(2 * m + k + 1) * P]
                                                 for k in range(2) for t in range(TB)])

            def turn_memory(m):
                pe.wait_ge(mem_in[m // 2], 16)
                four(m % 4, m // 4, [mem[:, t, (2 * m + k) * P:(2 * m + k + 1) * P]
                                     for k in range(2) for t in range(TB)])

            pe.wait_ge(ident_ready, 2)
            pe.wait_ge(mem_row_in, 16)
            pe.transpose(acc[:, 1, 1, 0:2 * KB], mem_gain_rows[:, :], ident[0:2 * KB, 0:2 * KB]).then_inc(gain_cols, 1)
            for m in range(3):
                turn_memory(m)
            turn = [2, 2, 2, 2]
            ph = PH["mem"]
            for l in range(2):
                for c in range(2):
                    g = ph.group + 2 * l + c
                    if g == 1:
                        pe.wait_ge(gains_ready, 2)
                    slot_ready(g, slot_count(g))
                    for j in range(8):
                        n = ph.unit + 16 * l + 8 * c + j
                        if l == 0 and c == 0:
                            pe.wait_ge(bank_free[j % 4], 1 + j // 4)
                        unit(n, n, h_hi[:, 16 * l:16 * l + 16, :], h_lo[:, 16 * l:16 * l + 16, :],
                             UK * j, g % 2, j == 0, j == 7)
                        if l == 0 and c == 0 and j + 3 < 8:
                            turn_memory(j + 3)
                        if l == 0 and c == 0 and j == 5:
                            pe.wait_ge(rows_in, 16 * 5)
                            pe.transpose(acc[:, 1, 0, 0:6 * KB], gain_rows[:, :], ident[0:6 * KB, 0:6 * KB])
                            pe.transpose(acc[:, 1, 1, P:P + 2 * RK], gain_rows2[:, :],
                                         ident[0:2 * RK, 0:2 * RK]).then_inc(gain_cols, 1)
                        if c == 1 and j == (0 if l else 4):
                            pe.wait_ge(acc_free[(g - 1) % 2], slot_count(g - 1) + 1)
                            for m in range(2):
                                k = 2 * l + m
                                four(k, turn[k], [k_tok[:, t, (2 * m + hh) * P:(2 * m + hh + 1) * P]
                                                  for hh in range(2) for t in range(TB)])
                                turn[k] += 1
                        if l == 1 and c == 1:
                            if j == 0:
                                pe.wait_ge(bands_ready, 2)
                            bank_ready(j % 4, turn[j % 4])
                            for k in range(2):
                                kb = 2 * j + k
                                o = bank[:, j % 4, k * S:(k + 1) * S]
                                for t in range(TB):
                                    to = slice(0, REACH) if t == 0 else slice(P, S)
                                    mm = pe.matmul(o[:, to], x[:, t, kb * P:(kb + 1) * P],
                                                   band_of[t][:, kb // CK, :], start=(k == 0 and t == 0),
                                                   stop=(t == 1), skip_group_check=True)
                            mm.then_inc(bank_full[j % 4], 1)
                            turn[j % 4] += 1

            def out_phase(name, src_hi, src_lo, per, waits=None, done=0, pool=False, rest=None):
                ph = PH[name]
                for c in range(NC):
                    g = ph.group + c
                    if c > 0 or done == 0:
                        slot_ready(g, slot_count(g))
                    for j in range(done if c == 0 else 0, per):
                        if waits:
                            waits(c, j)
                        n = ph.unit + per * c + j
                        unit(n, n, src_hi, src_lo, UK * j + (CK * c if pool else 0), g % 2, j == 0, j == per - 1)
                        if j == 1 and c > 0 and name != "fo1":
                            turn_chunk(name, c - 1)
                        if j == 1 and c == 0 and rest:
                            rest()

            def pooled(c, j):
                b = 2 * c + j
                pe.wait_ge(bank_free[b % 4], PH["pool"].bank[b % 4] - 1 + b // 4)

            out_phase("pool", x_hi, x_lo, CK // UK, pooled, pool=True)

            def wait_x(ph, j):
                pe.wait_ge(bank_free[2 + j % 2], ph.bank[2 + j % 2] - 3 + j // 2)

            def xattn(l):
                ph = PH[f"xq{l}"]
                k_mem, v_mem = (k_mem0, v_mem0) if l == 0 else (k_mem1, v_mem1)
                g, b = ph.group, list(ph.bank)
                slot_ready(g, slot_count(g))
                for j in range(8):
                    wait_x(ph, j)
                    unit(ph.unit + j, ph.unit + j, x_hi, x_lo, UK * j, g % 2, j == 0, j == 7)
                    if j == 1:
                        turn_chunk(("pool", "mo")[l], NC - 1)
                pe.wait_ge(acc_free[g % 2], slot_count(g) + 1)
                for m in range(2):
                    four(m, b[m], [q_tok[:, t, (2 * m + hh) * P:(2 * m + hh + 1) * P]
                                   for hh in range(2) for t in range(TB)])

                def scores(h):
                    bank_ready(h % 2, b[h % 2] + 1 + h // 2)
                    if h == 0:
                        bank_ready(1, b[1] + 1)
                    for t in range(TB):
                        mm = pe.matmul(bank[:, h % 2, t * S:(t + 1) * S], q_t[:, h, t * P:(t + 1) * P],
                                       k_mem[:, h, :], start=(t == 0), stop=True, skip_group_check=True)
                    mm.then_inc(bank_full[h % 2], 1)

                def turn_probs(h):
                    pe.wait_ge(probs_ready, XH * l + (HEADS if l else 0) + h + 1)
                    four(2, b[2] + h, [probs[:, h % 2, t, k * P:(k + 1) * P] for k in range(TB) for t in range(TB)])

                def values(h):
                    bank_ready(2, b[2] + h + 1)
                    bank_ready(3, b[3] + h)
                    for k in range(TB):
                        mm = pe.matmul(bank[:, 3, 0:S], v_mem[:, k, h, :], probs_t[:, h % 2, k, :],
                                       start=(k == 0), stop=(k == TB - 1))
                    mm.then_inc(bank_full[3], 1)

                scores(0)
                scores(1)
                for h in range(XH):
                    turn_probs(h)
                    if h + 2 < XH:
                        scores(h + 2)
                    if h:
                        values(h - 1)
                values(XH - 1)
                out_phase(f"xo{l}", h_hi, h_lo, XH // UK,
                          lambda c, j: bank_ready(3, b[3] + UK * (j + 1)) if c == 0 else None)

            def ffn(l):
                ph = PH[f"fi{l}"]

                def turn_hidden(i, cnt_up):
                    pe.wait_ge(acc_free[(ph.group + 1) % 2], cnt_up)
                    for m in range(2):
                        four(m, ph.bank[m] + i, [h_tok[:, t, (2 * m + k) * P:(2 * m + k + 1) * P]
                                                 for k in range(2) for t in range(TB)])

                def pair(i, first):
                    for c in range(2):
                        g = ph.group + c
                        slot_ready(g, slot_count(g) + i)
                        for j in range(8):
                            if first and c == 0:
                                wait_x(ph, j)
                            unit(ph.unit + 8 * c + j + i * 16, ph.unit + 8 * c + j, x_hi, x_lo, UK * j,
                                 g % 2, j == 0, j == 7)
                            if c == 0 and j == 1 and first:
                                turn_chunk(f"xo{l}", NC - 1)
                            if c == 0 and j == 0 and not first:
                                turn_hidden(i - 1, slot_count(ph.group + 1) + i)

                pair(0, True)
                with pe.Fori(1, NP) as i:
                    pair(i, False)

                def last_hidden(c, j):
                    if c == 0 and j >= FK // UK - 2:
                        m = j - (FK // UK - 2)
                        bank_ready(m, ph.bank[m] + NP)

                out_phase(f"fo{l}", h_hi, h_lo, FK // UK, last_hidden,
                          rest=lambda: turn_hidden(NP - 1, slot_count(ph.group + 1) + NP))

            xattn(0)
            ffn(0)

            ph, pp = PH["mi"], PH["mp"]
            cq, ckv, kr = ph.group, ph.group + 1, ph.group + 2
            for n, g in enumerate((cq, ckv)):
                slot_ready(g, slot_count(g))
                for j in range(8):
                    if n == 0:
                        wait_x(ph, j)
                    unit(ph.unit + 8 * n + j, ph.unit + 8 * n + j, x_hi, x_lo, UK * j, g % 2, j == 0, j == 7)
                    if n == 0 and j == 1:
                        turn_chunk("fo0", NC - 1)
                    if n == 1 and j == 0:
                        pe.wait_ge(acc_free[cq % 2], slot_count(cq) + 1)
                        for m in range(2):
                            four(m, ph.bank[m], [cq_tok[:, t, (2 * m + k) * P:(2 * m + k + 1) * P]
                                                 for k in range(2) for t in range(TB)])
            slot_ready(kr, slot_count(kr))
            unit(ph.unit + 16, ph.unit + 16, x_hi, x_lo, 0, kr % 2, True, True, kbs=KB, width=ROPE)

            def q_up(i, j):
                g = pp.group
                if j == 0:
                    slot_ready(g, slot_count(g) + i)
                unit(pp.unit + j + i * 4, pp.unit + j, h_hi[:, 16:20, :], h_lo[:, 16:20, :], UK * j, g % 2,
                     j == 0, j == 1, width=QW)

            def kv_up(i, j):
                g = pp.group + 1
                if j == 0:
                    slot_ready(g, slot_count(g) + i)
                unit(pp.unit + 2 + j + i * 4, pp.unit + 2 + j, h_hi[:, 20:24, :], h_lo[:, 20:24, :], UK * j, g % 2,
                     j == 0, j == 1)

            for m in range(2):
                bank_ready(m, ph.bank[m] + 1)
            q_up(0, 0)
            q_up(0, 1)
            pe.wait_ge(acc_free[ckv % 2], slot_count(ckv) + 1)
            for m in range(2):
                four(2 + m, ph.bank[2 + m], [ckv_tok[:, t, (2 * m + k) * P:(2 * m + k + 1) * P]
                                             for k in range(2) for t in range(TB)])
            pe.wait_ge(roped, 1)
            four(0, ph.bank[0] + 1, [kr_tok[:, t, :] for t in range(TB)], rows=ROPE)
            for m in range(2):
                bank_ready(2 + m, ph.bank[2 + m] + 1)
            kv_up(0, 0)
            kv_up(0, 1)

            def output_up(j):
                po = PH["mo"]
                if j == 0:
                    slot_ready(po.group, slot_count(po.group))
                unit(po.unit + j, po.unit + j, h_hi, h_lo, UK * j, po.group % 2, j == 0, False)

            def attend(i, more):
                b = pp.bank
                heads = range(2)

                def between(j):
                    if not more:
                        output_up(j)
                    elif j < 2:
                        q_up(i + 1, j)
                    else:
                        kv_up(i + 1, j - 2)

                pe.wait_ge(k_ready, i + 1)
                four(1, b[1] + i * 2, [kh_tok[:, t, h, :] for h in heads for t in range(TB)])
                pe.wait_ge(roped, i + 2)
                bank_ready(2, b[2] + i * 2)
                pe.wait_ge(acc_free[pp.group % 2], slot_count(pp.group) + 1 + i)
                four(0, b[0] + i * 3, [qh_tok[:, t, h, 0:NOPE] for h in heads for t in range(TB)])
                four(2, None, [qh_tok[:, t, h, NOPE:] for h in heads for t in range(TB)], rows=ROPE)
                between(0)
                for k, count in ((0, b[0] + 1 + i * 3), (1, b[1] + 1 + i * 2), (2, b[2] + 1 + i * 2)):
                    bank_ready(k, count)
                for h in heads:
                    k, count = (3, b[3] + i * 2) if h == 0 else (0, b[0] + 1 + i * 3)
                    bank_ready(k, count)
                    for t in range(TB):
                        keys = (t + 1) * P
                        o = bank[:, k, t * P:t * P + keys]
                        pe.matmul(o, qh_t[:, h, t * P:(t + 1) * P], kh_t[:, h, 0:keys], start=True, stop=False)
                        mm = pe.matmul(o, qr_t[:, h, t * P:(t + 1) * P], kr_t[:, 0:keys], start=False, stop=True)
                    mm.then_inc(bank_full[k], 1)
                between(1)
                between(2)
                for h in heads:
                    pe.wait_ge(probs_ready, XH + h + 1 + i * 2)
                    four(1 + h, b[1 + h] + 1 + i * 2, [mprobs[:, h, j * P:(j + 1) * P] for j in range(3)])
                between(3)
                for h in heads:
                    k, count = (3, b[3] + 1 + i * 2) if h == 0 else (0, b[0] + 2 + i * 3)
                    bank_ready(1 + h, b[1 + h] + 2 + i * 2)
                    bank_ready(k, count)
                    if h == 0:
                        pe.wait_ge(acc_free[(pp.group + 1) % 2], slot_count(pp.group + 1) + 1 + i)
                    pe.matmul(bank[:, k, 0:S], vh_tok[:, 0, h, :], mprobs_t[:, h, 0:S], start=True, stop=False)
                    pe.matmul(bank[:, k, P:S], vh_tok[:, 1, h, :], mprobs_t[:, h, S:S + P], start=False,
                              stop=True).then_inc(bank_full[k], 1)

            with pe.Fori(0, PAIRS - 1) as i:
                attend(i, True)
            attend(PAIRS - 1, False)

            def last_heads(c, j):
                if c == 0 and j == KB // UK - 1:
                    for k, per in ((0, 3), (3, 2)):
                        bank_ready(k, pp.bank[k] + per * PAIRS)

            out_phase("mo", h_hi, h_lo, KB // UK, last_heads, done=4)
            xattn(1)
            ffn(1)

        def width_of(n):
            j = n - PH["mp"].unit
            return UK * QW if 0 <= j < 4 * PAIRS and j % 4 < 2 else UW

        flat = "p k s -> p (k s)"
        x_hi32, x_lo_f = x_hi[:, :, :].bitcast(F32), x_lo
        h_hi32 = h_hi[:, :, :].bitcast(F32)
        h_hi_flat, h_lo_flat = h_hi[:, :, :].rearrange(flat), h_lo[:, :, :].rearrange(flat)
        h_hi32_flat = h_hi32.rearrange(flat)

        TURNED = {"pool": (G_X, N_X0), "xo0": (G_FFN, N_F0), "fo0": (G_MIX + KB, N_MLA), "mo": (G_X + KB, N_X1),
                  "xo1": (G_FFN + KB, N_F1), "fo1": (None, N_OUT)}

        @block.scalar
        def _(act):
            def half(s, i=0, per=0, width=None):
                if isinstance(i, int):
                    s, i, per = s + i * per, 0, 0
                if s >= UNITS:
                    return
                width = width or width_of(s)
                slot = s % RING
                act.wait_ge(loaded[slot], i * (16 * per // RING) + 16 * (s // RING + 1))
                if s >= RING:
                    act.wait_ge(unit_used, i * per + s - RING + 1)
                act.activation(w_hi[:, slot, 0:width], raw[:, slot, 0:width], ACT.Copy).then_inc(hi_ready, 1)

            def squares(norm, t, c, src, before):
                before = before + STAT_END[norm] - STATS[norm]
                if not isinstance(before, int) or before > 0:
                    act.wait_ge(stats, before)
                act.activation(junk[:, :], src, ACT.Square, accum_out=sums[:, norm, t, c:c + 1] if isinstance(c, int)
                               else sums[:, norm, t, bass.ds(c, 1)]).then_inc(stats, 1)

            def turned(k, count, dst, kbs, gain):
                act.wait_ge(bank_full[k], count)
                for j, kb in enumerate(kbs):
                    last = act.activation(dst(kb), bank[:, k, j * S:(j + 1) * S], ACT.Copy, scale=gain(kb))
                last.then_inc(halved_hi, 1)

            act.dma_start(mem_gain_rows[:, :],
                          a["norm_mem_g"].rearrange("l (k p) -> (l k) p", p=P)).then_inc(mem_row_in, 16)
            for s in range(AHEAD):
                half(s)
                if s == 0:
                    for n, name in enumerate(("norm_mix_g", "norm_xattn_g", "norm_ffn_g")):
                        act.dma_start(gain_rows[32 * n:32 * n + 32, :],
                                      a[name].rearrange("l (k p) -> (l k) p", p=P)).then_inc(rows_in, 16)
                    for n, name in enumerate(("mla_q_norm_g", "mla_kv_norm_g")):
                        act.dma_start(gain_rows2[n * RK:(n + 1) * RK, :],
                                      a[name].rearrange("l (k p) -> (l k) p", p=P)).then_inc(rows_in, 16)
            ph = PH["mem"]
            for j in range(32):
                if j < KB // 2:
                    if j == 0:
                        act.wait_ge(gains_ready, 1)
                    act.wait_ge(bank_full[j % 4], 1 + j // 4)
                    for l in range(2):
                        for k in range(2):
                            kb = 2 * j + k
                            last = act.activation(h_hi[:, 16 * l + kb, :], bank[:, j % 4, k * S:(k + 1) * S], ACT.Copy,
                                                  scale=gains[:, G_MEM + 16 * l + kb:G_MEM + 16 * l + kb + 1])
                    last.then_inc(halved_hi, 1)
                half(ph.unit + j + AHEAD)
                if j == 2:
                    act.dma_start(pos_i[:, :], a["positions"][0].rearrange("(t p) -> p t", p=P),
                                  allow_slow_non_contiguous=True).then_inc(rope_in, 16)
                    act.dma_start(freq[:, :], a["inv_freq"].partition_broadcast(P)).then_inc(rope_in, 16)
                if j == 16:
                    act.dma_start(pool_s[:, :], a["pool_scale"][0].partition_broadcast(P)).then_inc(scale_in, 16)
                if 6 <= j < 10:
                    for n in range(2 * (j - 6), 2 * (j - 6) + 2):
                        squares(N_MEM, n // NC, n % NC, mem[:, n // NC, n % NC * CW:(n % NC + 1) * CW], n)
                if 10 <= j < 18:
                    n = j - 10
                    if n == 0:
                        act.wait_ge(x_in, 16)
                    squares(N_POOL, n // NC, n % NC, x[:, n // NC, n % NC * CW:(n % NC + 1) * CW], n)
                if j == 18:
                    act.wait_ge(angle_ready, 1)
                    act.activation(sin[:, :, :], angle_t[:, 1, :, :], ACT.Sin)
                    act.activation(cos[:, :, :], angle_t[:, 2, :, :], ACT.Sin).then_inc(table_ready, 1)
                if j in (12, 24):
                    l = j // 24
                    k_mem = k_mem1 if l else k_mem0
                    for m in range(2):
                        k = 2 * l + m
                        act.wait_ge(bank_full[k], 3)
                        act.activation(k_mem[:, 2 * m:2 * m + 2, :].rearrange(flat), bank[:, k, :],
                                       ACT.Copy).then_inc(bank_free[k], 1)
                if j == 24:
                    act.wait_ge(gains_ready, 2)
                if j >= 24:
                    m = j - 24
                    k = m % 4
                    turned(k, PH["pool"].bank[k] - 1 + m // 4, lambda kb: x_hi[:, kb, :], (2 * m, 2 * m + 1),
                           lambda kb: gains[:, G_MIX + kb:G_MIX + kb + 1])

            def chunk_squares(name, c):
                g = PH[name].group + c
                act.wait_ge(acc_free[g % 2], slot_count(g) + 1)
                for t in range(TB):
                    src = xs[:, c % 2, t, :] if name != "fo1" else x[:, t, c * CW:(c + 1) * CW]
                    squares(TURNED[name][1], t, c, src, c * 2 + t)

            def chunk_turned(name, c):
                gain = TURNED[name][0]
                for m in range(2):
                    c0 = c * CK + 2 * m
                    turned(2 + m, PH[name].bank[2] + c + 1, lambda kb: x_hi[:, kb, :], (c0, c0 + 1),
                           lambda kb: gains[:, gain + kb:gain + kb + 1])

            def out_phase(name, per, done=0, rest=None):
                ph = PH[name]
                for c in range(NC):
                    for j in range(done if c == 0 else 0, per):
                        half(ph.unit + per * c + j + AHEAD)
                        if j == 1 and c > 0 and name != "fo1":
                            chunk_turned(name, c - 1)
                        if j == 1 and c == 0 and rest:
                            rest()
                    chunk_squares(name, c)

            def by_token(g, count, unit_count, dst, scale, width=CW):
                act.wait_ge(unit_used, unit_count)
                for t in range(TB):
                    last = act.activation(dst(t), acc[:, g % 2, t, 0:width], ACT.Copy, scale=scale(t))
                last.then_inc(acc_free[g % 2], 1)

            def xattn(l):
                ph = PH[f"xq{l}"]
                norm, b = (N_X0, N_X1)[l], ph.bank
                for j in range(8):
                    half(ph.unit + j + AHEAD)
                    if j == 1:
                        chunk_turned(("pool", "mo")[l], NC - 1)
                act.wait_ge(rs_ready, norm + 1)
                by_token(ph.group, None, ph.unit + 8, lambda t: q_tok[:, t, :], lambda t: rsq[:, norm, t:t + 1])
                for m in range(2):
                    act.wait_ge(bank_full[m], b[m] + 1)
                    act.activation(q_t[:, 2 * m:2 * m + 2, :].rearrange(flat), bank[:, m, :],
                                   ACT.Copy).then_inc(bank_free[m], 1)

                def exps(h):
                    act.wait_ge(max_ready, XH * l + h + 1)
                    for t in range(TB):
                        last = act.activation(probs[:, h % 2, t, :], bank[:, h % 2, t * S:(t + 1) * S], ACT.Exp,
                                              bias=neg_max[:, h, t:t + 1], accum_out=exp_sum[:, h, t:t + 1])
                    last.then_inc(bank_free[h % 2], 1)

                def output(h):
                    act.wait_ge(bank_full[3], b[3] + h + 1)
                    act.activation(h_hi[:, h, :], bank[:, 3, 0:S], ACT.Copy).then_inc(halved_hi, 1)

                exps(0)
                exps(1)
                exps(2)
                output(0)
                exps(3)
                output(1)
                output(2)
                output(3)
                out_phase(f"xo{l}", XH // UK)

            def ffn(l):
                ph, norm = PH[f"fi{l}"], (N_F0, N_F1)[l]

                def hidden(i):
                    for m in range(2):
                        act.wait_ge(bank_full[m], i + ph.bank[m] + 1)
                        act.activation(h_hi_flat[:, bass.ds(i * (CK * S) + 2 * m * S, 2 * S)], bank[:, m, :],
                                       ACT.Copy).then_inc(halved_hi, 1)

                def pair(i, first):
                    for j in range(16):
                        half(ph.unit + j + AHEAD, i, 16)
                        if j == 1 and first:
                            chunk_turned(f"xo{l}", NC - 1)
                        if j == 0 and not first:
                            hidden(i - 1)
                        if j == 7:
                            if first:
                                act.wait_ge(rs_ready, norm + 1)
                                act.wait_ge(x_back, ph.chunk)
                            act.wait_ge(unit_used, i * 16 + ph.unit + 8)
                            for t in range(TB):
                                last = act.activation(s_tok[:, t, :], acc[:, ph.group % 2, t, :], ACT.Silu,
                                                      scale=rs[:, norm, t:t + 1])
                            last.then_inc(acc_free[ph.group % 2], 1)

                pair(0, True)
                with act.Fori(1, NP) as i:
                    pair(i, False)

                def rest():
                    hidden(NP - 1)
                    if l == 1:
                        act.wait_ge(unit_used, PH["fo1"].unit)
                        act.dma_start(g_out[:, :], a["final_norm_g"].partition_broadcast(P)).then_inc(g_in, 16)

                out_phase(f"fo{l}", FK // UK, rest=rest)

            out_phase("pool", CK // UK)
            xattn(0)
            ffn(0)

            ph, pp = PH["mi"], PH["mp"]
            cq, ckv, kr = ph.group, ph.group + 1, ph.group + 2

            def latent(g, n, dst, norm):
                by_token(g, None, n, lambda t: dst[:, t, :], lambda t: rs[:, N_MLA, t:t + 1])
                act.wait_ge(acc_free[g % 2], slot_count(g) + 1)
                for t in range(TB):
                    squares(norm, t, 0, dst[:, t, :], t)

            def latent_turned(k, count, m, kb0, gain):
                turned(k, count, lambda kb: h_hi[:, kb0 + kb, :], (2 * m, 2 * m + 1),
                       lambda kb: gains[:, gain + kb:gain + kb + 1])

            for j in range(17):
                half(ph.unit + j + AHEAD)
                if j == 1:
                    chunk_turned("fo0", NC - 1)
                if j == 7:
                    act.wait_ge(rs_ready, N_MLA + 1)
                    latent(cq, ph.unit + 8, cq_tok, N_CQ)
                if j == 8:
                    for m in range(2):
                        latent_turned(m, ph.bank[m] + 1, m, 16, G_CQ)
                if j == 15:
                    latent(ckv, ph.unit + 16, ckv_tok, N_CKV)
                if j == 16:
                    by_token(kr, None, ph.unit + 17, lambda t: kr_tok[:, t, :], lambda t: rs[:, N_MLA, t:t + 1], ROPE)

            def queries(i):
                by_token(pp.group, None, i * 4 + pp.unit + 2,
                         lambda t: qh_tok[:, t, :, :].rearrange("p h n -> p (h n)"), lambda t: rsq[:, N_CQ, t:t + 1], QW)

            half(pp.unit + AHEAD)
            half(pp.unit + 1 + AHEAD)
            for m in range(2):
                latent_turned(2 + m, ph.bank[2 + m] + 1, m, 20, G_CKV)
            act.wait_ge(bank_full[0], ph.bank[0] + 2)
            act.activation(kr_t[:, :], bank[0:ROPE, 0, 0:S], ACT.Copy).then_inc(bank_free[0], 1)
            act.wait_ge(rs_ready, N_CQ + 1)
            queries(0)
            half(pp.unit + 2 + AHEAD)
            half(pp.unit + 3 + AHEAD)

            def attend(i, more):
                b = pp.bank

                def ahead(j):
                    n = pp.unit + 4 + j + AHEAD
                    half(n, i, 4, width_of(n + (i * 4 if isinstance(i, int) else 0)))

                act.wait_ge(bank_full[0], i * 3 + b[0] + 1)
                act.activation(qh_t[:, :, :].rearrange(flat), bank[:, 0, :], ACT.Copy).then_inc(bank_free[0], 1)
                act.wait_ge(bank_full[2], i * 2 + b[2] + 1)
                act.activation(qr_t[:, :, :].rearrange(flat), bank[0:ROPE, 2, :], ACT.Copy).then_inc(bank_free[2], 1)
                ahead(0)
                for h in range(2):
                    k, count = (3, i * 2 + b[3] + 1) if h == 0 else (0, i * 3 + b[0] + 2)
                    act.wait_ge(bank_free[k], count)
                    for t, cols in enumerate((slice(0, P), slice(P, 3 * P))):
                        last = act.activation(mprobs[:, h, cols], neg_s[:, h, cols], ACT.Exp, scale=-1.0,
                                              bias=neg_max[:, h, t:t + 1], accum_out=exp_sum[:, h, t:t + 1])
                    last.then_inc(exp_ready, 1)
                ahead(1)
                if more:
                    queries(i + 1)
                ahead(2)
                ahead(3)
                for h in range(2):
                    k, count = (3, i * 2 + b[3] + 2) if h == 0 else (0, i * 3 + b[0] + 3)
                    act.wait_ge(bank_full[k], count)
                    act.activation(h_hi_flat[:, bass.ds(i * (2 * S) + h * S, S)], bank[:, k, 0:S],
                                   ACT.Copy).then_inc(halved_hi, 1)

            with act.Fori(0, PAIRS - 2) as i:
                attend(i, True)
            attend(PAIRS - 2, True)
            attend(PAIRS - 1, False)
            out_phase("mo", KB // UK, done=4)
            xattn(1)
            ffn(1)
            act.wait_ge(rs_ready, N_OUT + 1)
            act.wait_ge(xg_ready, NC)
            act.activation(xg[:, 1, :], xg[:, 1, :], ACT.Copy, scale=rs[:, N_OUT, 1:2]).then_inc(y_ready[1], 1)

        @block.vector
        def _(dve):
            steps = [0]

            def step(ins):
                steps[0] += 1
                ins.then_inc(dve_step, 1)
                dve.wait_ge(dve_step, steps[0])

            def low(s, i=0, per=0, width=None):
                if isinstance(i, int):
                    s, i, per = s + i * per, 0, 0
                if s >= UNITS:
                    return
                width = width or width_of(s)
                slot = s % RING
                dve.wait_ge(hi_ready, i * per + s + 1)
                dve.tensor_tensor(w_lo[:, slot, 0:width], raw[:, slot, 0:width],
                                  w_hi[:, slot, 0:width].bitcast(F32), ALU.subtract).then_inc(lo_ready, 1)

            def turned(k, count, dst, hi32, kbs, gain):
                dve.wait_ge(halved_hi, count)
                for j, kb in enumerate(kbs):
                    last = dve.scalar_tensor_tensor(out=dst(kb), in0=bank[:, k, j * S:(j + 1) * S], scalar=gain(kb),
                                                    in1=hi32(kb), op0=ALU.mult, op1=ALU.subtract)
                last.then_inc(bank_free[k], 1)

            def variance(norm, width=D):
                dve.wait_ge(stats, STAT_END[norm])
                if width == D:
                    step(dve.tensor_reduce(total[:, norm, :], sums[:, norm, :, :], AX_X, ALU.add))
                    src = total[:, norm, :]
                else:
                    src = sums[:, norm, :, 0]
                dve.tensor_scalar(var[:, norm, :], src, 1.0 / width, EPS, ALU.mult, ALU.add).then_inc(var_ready, 1)

            def rope_angles():
                dve.wait_ge(rope_in, 32)
                step(dve.tensor_copy(pos_f[:, :], pos_i[:, :]))
                for t in range(TB):
                    ins = dve.tensor_scalar(angle_t[:, 0, t, :], freq[:, :], pos_f[:, t:t + 1], None, ALU.mult)
                step(ins)
                r, whole = angle_t[:, 0, :, :], angle_t[:, 3, :, :]
                for block_of in (2048.0, 1.0):
                    step(dve.tensor_scalar(whole, r, 1.0 / (TWO_PI * block_of), ROUND, ALU.mult, ALU.add))
                    step(dve.tensor_scalar(whole, whole, ROUND, None, ALU.subtract))
                    for part in TWO_PI_PARTS:
                        step(dve.scalar_tensor_tensor(out=angle_t[:, 1, :, :], in0=whole, scalar=-part * block_of,
                                                      in1=r, op0=ALU.mult, op1=ALU.add))
                        r = angle_t[:, 1, :, :]
                step(dve.tensor_scalar(r, r, 3.1415925, -3.1415925, ALU.min, ALU.max))
                step(dve.tensor_scalar(whole, r, -1.0, None, ALU.mult))
                step(dve.tensor_tensor(whole, whole, r, ALU.max))
                dve.tensor_scalar(angle_t[:, 2, :, :], whole, -1.0, TWO_PI / 4, ALU.mult, ALU.add).then_inc(angle_ready, 1)

            dve.wait_ge(gain_cols, 1)
            dve.tensor_copy(gains[:, G_MEM:G_MEM + 2 * KB], acc[:, 1, 1, 0:2 * KB]).then_inc(gains_ready, 1)
            for s in range(AHEAD):
                low(s)
            dve.wait_ge(gains_ready, 1)
            ph = PH["mem"]
            for j in range(32):
                if j < KB // 2:
                    dve.wait_ge(halved_hi, j + 1)
                    for l in range(2):
                        for k in range(2):
                            kb = 16 * l + 2 * j + k
                            last = dve.scalar_tensor_tensor(
                                out=h_lo[:, kb, :], in0=bank[:, j % 4, k * S:(k + 1) * S],
                                scalar=gains[:, G_MEM + kb:G_MEM + kb + 1], in1=h_hi32[:, kb, :],
                                op0=ALU.mult, op1=ALU.subtract)
                    last.then_inc(bank_free[j % 4], 1)
                low(ph.unit + j + AHEAD)
                if j == 6:
                    dve.wait_ge(gain_cols, 2)
                    dve.tensor_copy(gains[:, 0:6 * KB], acc[:, 1, 0, 0:6 * KB])
                    dve.tensor_copy(gains[:, G_CQ:G_CQ + 2 * RK], acc[:, 1, 1, P:P + 2 * RK]).then_inc(gains_ready, 1)
                if j == 9:
                    variance(N_MEM)
                if j == 13:
                    rope_angles()
                if j == 17:
                    variance(N_POOL)
                if j == 19:
                    dve.wait_ge(band_in, 16)
                    dve.wait_ge(rs_ready, N_POOL + 1)
                    for t in range(TB):
                        dve.tensor_scalar(band_of[t], band_of[t], rs[:, N_POOL, t:t + 1], None,
                                          ALU.mult).then_inc(bands_ready, 1)
                if j in (11, 15, 23, 31):
                    q = (11, 15, 23, 31).index(j)
                    g, l, values = ph.group + q, q // 2, q % 2
                    if q == 0:
                        dve.wait_ge(rs_ready, N_MEM + 1)
                    dve.wait_ge(unit_used, ph.unit + 8 * q + 8)
                    v_mem = (v_mem0, v_mem1)[l]
                    for t in range(TB):
                        dst = v_mem[:, t, :, :].rearrange("p h n -> p (h n)") if values else k_tok[:, t, :]
                        last = dve.tensor_scalar(dst, acc[:, g % 2, t, :], rs[:, N_MEM, t:t + 1], None, ALU.mult)
                    last.then_inc(acc_free[g % 2], 1)
                if j == 24:
                    dve.wait_ge(gains_ready, 2)
                if j >= 24:
                    m = j - 24
                    turned(m % 4, PH["mem"].half + 8 + m + 1, lambda kb: x_lo[:, kb, :], lambda kb: x_hi32[:, kb, :],
                           (2 * m, 2 * m + 1), lambda kb: gains[:, G_MIX + kb:G_MIX + kb + 1])

            def add_chunk(name, c, units):
                g, chunk = PH[name].group + c, PH[name].chunk + c
                dve.wait_ge(unit_used, units)
                if name == "fo1":
                    for t in range(TB):
                        xc = x[:, t, c * CW:(c + 1) * CW]
                        last = dve.tensor_tensor(xc, acc[:, g % 2, t, :], xc, ALU.add)
                    last.then_inc(acc_free[g % 2], 1)
                    return
                if chunk > 1:
                    dve.wait_ge(x_back, chunk - 1)
                dst, old = xs[:, c % 2, :, :], x[:, :, c * CW:(c + 1) * CW]
                if name == "pool":
                    if c == 0:
                        dve.wait_ge(scale_in, 16)
                    for t in range(TB):
                        last = dve.tensor_tensor(dst[:, t, :], acc[:, g % 2, t, :], pool_s[:, c * CW:(c + 1) * CW],
                                                 ALU.mult)
                    step(last)
                    dve.tensor_tensor(dst, dst, old, ALU.add).then_inc(acc_free[g % 2], 1)
                else:
                    for t in range(TB):
                        last = dve.tensor_tensor(dst[:, t, :], acc[:, g % 2, t, :], old[:, t, :], ALU.add)
                    last.then_inc(acc_free[g % 2], 1)

            def chunk_turned(name, c):
                gain = TURNED[name][0]
                for m in range(2):
                    c0 = c * CK + 2 * m
                    turned(2 + m, PH[name].half + 2 * c + m + 1, lambda kb: x_lo[:, kb, :],
                           lambda kb: x_hi32[:, kb, :], (c0, c0 + 1), lambda kb: gains[:, gain + kb:gain + kb + 1])

            def out_phase(name, per, done=0, rest=None):
                ph = PH[name]
                for c in range(NC):
                    for j in range(done if c == 0 else 0, per):
                        low(ph.unit + per * c + j + AHEAD)
                        if j == 1 and c > 0 and name != "fo1":
                            chunk_turned(name, c - 1)
                        if j == 1 and c == 0 and rest:
                            rest()
                    add_chunk(name, c, ph.unit + per * (c + 1))

            def xattn(l):
                ph = PH[f"xq{l}"]
                b, norm = ph.bank, (N_X0, N_X1)[l]
                for j in range(8):
                    low(ph.unit + j + AHEAD)
                    if j == 0:
                        variance(norm)
                    if j == 1:
                        chunk_turned(("pool", "mo")[l], NC - 1)

                def maximum(h):
                    dve.wait_ge(bank_full[h % 2], b[h % 2] + 2 + h // 2)
                    dve.tensor_reduce(neg_max[:, h, :], bank[:, h % 2, :].rearrange("p (t k) -> p t k", t=TB), AX_X,
                                      ALU.max, negate=True).then_inc(max_ready, 1)

                def normalise(h):
                    dve.wait_ge(bank_free[h % 2], b[h % 2] + 2 + h // 2)
                    step(dve.reciprocal(inv_sum[:, h, :], exp_sum[:, h, :]))
                    for t in range(TB):
                        pr = probs[:, h % 2, t, :]
                        last = dve.tensor_scalar(pr, pr, inv_sum[:, h, t:t + 1], None, ALU.mult)
                    last.then_inc(probs_ready, 1)

                def copy_probs(h):
                    dve.wait_ge(bank_full[2], b[2] + h + 1)
                    dve.tensor_copy(probs_t[:, h % 2, :, :].rearrange(flat), bank[:, 2, :]).then_inc(bank_free[2], 1)

                def output(h):
                    dve.wait_ge(halved_hi, ph.half + h + 1)
                    dve.tensor_tensor(h_lo[:, h, :], bank[:, 3, 0:S], h_hi32[:, h, :],
                                      ALU.subtract).then_inc(bank_free[3], 1)

                maximum(0)
                maximum(1)
                for h in range(XH):
                    normalise(h)
                    copy_probs(h)
                    if h + 2 < XH:
                        maximum(h + 2)
                    if h:
                        output(h - 1)
                output(XH - 1)
                out_phase(f"xo{l}", XH // UK)

            def ffn(l):
                ph, norm = PH[f"fi{l}"], (N_F0, N_F1)[l]

                def hidden(i):
                    for m in range(2):
                        cols = bass.ds(i * (CK * S) + 2 * m * S, 2 * S)
                        dve.wait_ge(halved_hi, i * 2 + ph.half + m + 1)
                        dve.tensor_tensor(h_lo_flat[:, cols], bank[:, m, :], h_hi32_flat[:, cols],
                                          ALU.subtract).then_inc(bank_free[m], 1)

                def pair(i, first):
                    g = ph.group + 1
                    for j in range(16):
                        low(ph.unit + j + AHEAD, i, 16)
                        if j == 0 and first:
                            variance(norm)
                        if j == 1 and first:
                            chunk_turned(f"xo{l}", NC - 1)
                        if j == 0 and not first:
                            hidden(i - 1)
                        if j == 15:
                            if first:
                                dve.wait_ge(rs_ready, norm + 1)
                                dve.wait_ge(x_back, ph.chunk)
                            dve.wait_ge(acc_free[ph.group % 2], i + slot_count(ph.group) + 1)
                            dve.wait_ge(unit_used, i * 16 + ph.unit + 16)
                            for t in range(TB):
                                last = dve.scalar_tensor_tensor(
                                    out=h_tok[:, t, :], in0=acc[:, g % 2, t, :], scalar=rs[:, norm, t:t + 1],
                                    in1=s_tok[:, t, :], op0=ALU.mult, op1=ALU.mult)
                            last.then_inc(acc_free[g % 2], 1)

                pair(0, True)
                with dve.Fori(1, NP) as i:
                    pair(i, False)
                out_phase(f"fo{l}", FK // UK, rest=lambda: hidden(NP - 1))

            out_phase("pool", CK // UK)
            xattn(0)
            ffn(0)

            ph, pp = PH["mi"], PH["mp"]

            def latent_turned(k, count, m, kb0, gain):
                turned(k, count, lambda kb: h_lo[:, kb0 + kb, :], lambda kb: h_hi32[:, kb0 + kb, :], (2 * m, 2 * m + 1),
                       lambda kb: gains[:, gain + kb:gain + kb + 1])

            for j in range(17):
                low(ph.unit + j + AHEAD)
                if j == 0:
                    variance(N_MLA)
                if j == 1:
                    chunk_turned("fo0", NC - 1)
                if j == 8:
                    variance(N_CQ, RANK)
                    for m in range(2):
                        latent_turned(m, ph.half + m + 1, m, 16, G_CQ)
                if j == 16:
                    variance(N_CKV, RANK)

            kv = pp.group + 1

            def heads_kv(i, dst, c0, done):
                dve.wait_ge(unit_used, i * 4 + pp.unit + 4)
                for t in range(TB):
                    src = acc[:, kv % 2, t, :].rearrange("p (h n) -> p h n", h=2)[:, :, c0:c0 + P]
                    last = dve.tensor_scalar(dst[:, t, :, :], src, rs[:, N_CKV, t:t + 1], None, ALU.mult)
                last.then_inc(done, 1)

            low(pp.unit + AHEAD)
            low(pp.unit + 1 + AHEAD)
            for m in range(2):
                latent_turned(2 + m, ph.half + 2 + m + 1, m, 20, G_CKV)
            low(pp.unit + 2 + AHEAD)
            low(pp.unit + 3 + AHEAD)
            dve.wait_ge(rs_ready, N_CKV + 1)
            dve.wait_ge(mask_ready, 2)
            heads_kv(0, kh_tok, 0, k_ready)

            def attend(i, more):
                b = pp.bank

                def ahead(j):
                    n = pp.unit + 4 + j + AHEAD
                    low(n, i, 4, width_of(n + (i * 4 if isinstance(i, int) else 0)))

                dve.wait_ge(bank_full[1], i * 2 + b[1] + 1)
                dve.tensor_copy(kh_t[:, :, :].rearrange(flat), bank[:, 1, :]).then_inc(bank_free[1], 1)
                heads_kv(i, vh_tok, NOPE, acc_free[kv % 2])
                ahead(0)
                for h in range(2):
                    k, count = (3, i * 2 + b[3] + 1) if h == 0 else (0, i * 3 + b[0] + 2)
                    dve.wait_ge(bank_full[k], count)
                    dve.memset(pace[:, h:h + 1], 0.0)
                    for t, (cols, m) in enumerate(((slice(0, P), mask[:, P:S]), (slice(P, 3 * P), mask[:, :]))):
                        last = dve.tensor_tensor_reduce(neg_s[:, h, cols], bank[:, k, cols], m, -1.0, 3.0e38, ALU.add,
                                                        ALU.min, neg_max[:, h, t:t + 1])
                    last.then_inc(bank_free[k], 1)
                ahead(1)
                for h in range(2):
                    dve.wait_ge(exp_ready, i * 2 + h + 1)
                    dve.reciprocal(inv_sum[:, h, :], exp_sum[:, h, :]).then_inc(dve_recip, 1)
                    dve.wait_ge(dve_recip, i * 2 + h + 1)
                    for t, cols in enumerate((slice(0, P), slice(P, 3 * P))):
                        last = dve.tensor_scalar(mprobs[:, h, cols], mprobs[:, h, cols], inv_sum[:, h, t:t + 1], None,
                                                 ALU.mult)
                    last.then_inc(probs_ready, 1)
                ahead(2)
                for h in range(2):
                    dve.wait_ge(bank_full[1 + h], i * 2 + b[1 + h] + 2)
                    dve.tensor_copy(mprobs_t[:, h, :], bank[:, 1 + h, 0:3 * P]).then_inc(bank_free[1 + h], 1)
                ahead(3)
                if more:
                    heads_kv(i + 1, kh_tok, 0, k_ready)
                for h in range(2):
                    k = 3 if h == 0 else 0
                    cols = bass.ds(i * (2 * S) + h * S, S)
                    dve.wait_ge(halved_hi, i * 2 + pp.half + h + 1)
                    dve.tensor_tensor(h_lo_flat[:, cols], bank[:, k, 0:S], h_hi32_flat[:, cols],
                                      ALU.subtract).then_inc(bank_free[k], 1)

            with dve.Fori(0, PAIRS - 2) as i:
                attend(i, True)
            attend(PAIRS - 2, True)
            attend(PAIRS - 1, False)
            out_phase("mo", KB // UK, done=4)
            xattn(1)
            ffn(1)
            variance(N_OUT)
            dve.wait_ge(rs_ready, N_OUT + 1)
            dve.wait_ge(xg_ready, NC)
            dve.tensor_scalar(xg[:, 0, :], xg[:, 0, :], rs[:, N_OUT, 0:1], None, ALU.mult).then_inc(y_ready[0], 1)

        @block.gpsimd
        def _(pool):
            steps = [0]

            def step(ins):
                steps[0] += 1
                ins.then_inc(pool_step, 1)
                pool.wait_ge(pool_step, steps[0])

            pool.memset(ident[:, :], 0.0).then_inc(ident_ready, 1)
            pool.wait_ge(ident_ready, 1)
            pool.affine_select(out=ident[:, :], in_=ident[:, :], compare_op=ALU.not_equal, fill=1.0, base=0,
                               pattern=[[-1, P]], channel_multiplier=1).then_inc(ident_ready, 1)
            pool.memset(mask[:, :], 0.0).then_inc(mask_ready, 1)
            pool.wait_ge(mask_ready, 1)
            pool.affine_select(out=mask[:, P:S], in_=mask[:, P:S], compare_op=ALU.is_ge, fill=MASK, base=0,
                               pattern=[[-1, P]], channel_multiplier=1).then_inc(mask_ready, 1)
            step(pool.memset(minus_half[:, :], -0.5))

            def inverse_rms(norm, scale=None):
                pool.wait_ge(var_ready, norm + 1)
                ins = pool.tensor_tensor(rs[:, norm, :], var[:, norm, :], minus_half[:, :], ALU.pow)
                if scale is not None:
                    step(ins)
                    ins = pool.tensor_scalar(rsq[:, norm, :], rs[:, norm, :], scale, None, ALU.mult)
                ins.then_inc(rs_ready, 1)

            def write_back(name):
                for c in range(NC):
                    g = PH[name].group + c
                    pool.wait_ge(acc_free[g % 2], slot_count(g) + 1)
                    pool.tensor_copy(x[:, :, c * CW:(c + 1) * CW], xs[:, c % 2, :, :]).then_inc(x_back, 1)

            def rotate(x1, x2, t_shape, done):
                heads = t_shape

                def table(tab):
                    v = tab[:, :, :]
                    return v.unsqueeze(2).to_broadcast([P, TB, heads, HR]) if heads else v

                tmp = [rope_t[:, n, :, :, :] if heads else rope_t[:, n, :, 0, :] for n in range(4)]
                for n, (v, tab) in enumerate(((x1, cos), (x2, sin), (x2, cos), (x1, sin))):
                    ins = pool.tensor_tensor(tmp[n], v, table(tab), ALU.mult)
                ins.then_inc(rope_step, 1)
                return tmp

            inverse_rms(N_MEM)
            inverse_rms(N_POOL)
            write_back("pool")
            inverse_rms(N_X0, XSCALE)
            write_back("xo0")
            inverse_rms(N_F0)
            write_back("fo0")
            inverse_rms(N_MLA)
            inverse_rms(N_CQ, MSCALE)
            kr = PH["mi"].group + 2
            pool.wait_ge(table_ready, 1)
            pool.wait_ge(acc_free[kr % 2], slot_count(kr) + 1)
            x1, x2 = kr_tok[:, :, 0:HR], kr_tok[:, :, HR:ROPE]
            tmp = rotate(x1, x2, 0, None)
            pool.wait_ge(rope_step, 1)
            pool.tensor_tensor(x1, tmp[0], tmp[1], ALU.subtract)
            pool.tensor_tensor(x2, tmp[2], tmp[3], ALU.add).then_inc(roped, 1)
            inverse_rms(N_CKV)
            pp = PH["mp"]
            q1, q2 = qh_tok[:, :, :, NOPE:NOPE + HR], qh_tok[:, :, :, NOPE + HR:NOPE + ROPE]
            with pool.Fori(0, PAIRS) as i:
                pool.wait_ge(acc_free[pp.group % 2], i + slot_count(pp.group) + 1)
                tmp = rotate(q1, q2, 2, None)
                pool.wait_ge(rope_step, i + 2)
                pool.tensor_tensor(q1, tmp[0], tmp[1], ALU.subtract)
                pool.tensor_tensor(q2, tmp[2], tmp[3], ALU.add).then_inc(roped, 1)
            write_back("mo")
            inverse_rms(N_X1, XSCALE)
            write_back("xo1")
            inverse_rms(N_F1)
            ph = PH["fo1"]
            pool.wait_ge(g_in, 16)
            for c in range(NC):
                g = ph.group + c
                pool.wait_ge(acc_free[g % 2], slot_count(g) + 1)
                cols = slice(c * CW, (c + 1) * CW)
                gain = g_out[:, cols].unsqueeze(1).to_broadcast([P, TB, CW])
                pool.tensor_tensor(xg[:, :, cols], x[:, :, cols], gain, ALU.mult).then_inc(xg_ready, 1)
            inverse_rms(N_OUT)


def _bands():
    import numpy as np
    t = np.arange(S)[:, None]
    s = np.arange(S)[None, :]
    out = []
    for b in range(TB):
        for w in WINDOWS:
            m = np.where((t <= s) & (s < t + w), 1.0 / np.minimum(s + 1, w), 0.0) - (t == s)
            out.append(m[b * P:(b + 1) * P, b * P:min(S, b * P + REACH)])
    return np.ascontiguousarray(np.concatenate(out, axis=1), dtype=np.float32)


_INS = ["x", "mem", "positions", "norm_mix_g", "norm_xattn_g", "norm_mem_g", "norm_ffn_g", "pool_w", "pool_scale",
        "mla_w_in", "mla_q_norm_g", "mla_w_q_up", "mla_kv_norm_g", "mla_w_kv_up", "mla_w_out", "xattn_w_q",
        "xattn_w_kv", "xattn_w_o", "ffn_w_in", "ffn_w_out", "final_norm_g"]


def kernel(**inputs):
    import numpy as _np
    import concourse.bacc as _bacc
    from concourse import mybir as _mybir
    from concourse.bass_utils import run_bass_kernel_spmd as _run

    nc = _bacc.Bacc("TRN2", target_bir_lowering=False, num_devices=1)
    arrays, args = {}, {}
    given = [(name, inputs[name]) for name in _INS]
    given.append(("bands", _bands()))
    given.append(("inv_freq", (1.0 / 10000.0 ** (_np.arange(0, ROPE, 2) / ROPE)).astype(_np.float32)))
    for name, v in given:
        v = _np.ascontiguousarray(v)
        arrays[f"in_{name}"] = v
        args[name] = nc.dram_tensor(f"in_{name}", v.shape, _mybir.dt.from_np(v.dtype), kind="ExternalInput").ap()
    out = nc.dram_tensor("out_0", (1, S, D), _mybir.dt.from_np(_np.dtype("float32")), kind="ExternalOutput").ap()
    hybrid_kernel(nc, args, out)
    r = _run(nc, [arrays], core_ids=[0])
    return r.results[0]["out_0"]
```

```python
import math
from contextlib import ExitStack

import concourse.bass as bass
from concourse import mybir

F32 = mybir.dt.float32
F32R = mybir.dt.float32r
I32 = mybir.dt.int32
BF16 = mybir.dt.bfloat16
ALU = mybir.AluOpType
ACT = mybir.ActivationFunctionType
AX_X = mybir.AxisListType.X

P = 128
D = 2048
S = 256
TB = S // P
KB = D // P
CW = 512
NC = D // CW
CK = CW // P
F = 5632
FK = F // P
NP = F // CW
XH = 4
HEADS = 16
NOPE, ROPE, VD = 128, 64, 128
HR = ROPE // 2
RANK = 512
RK = RANK // P
QW = 2 * (NOPE + ROPE)
PAIRS = HEADS // 2
LATENTS = 2 * RANK + ROPE
LATENT_COLS = ((0, 384), (384, 384), (768, LATENTS - 768))
WINDOWS = (2, 4, 8, 16)
REACH = P + max(WINDOWS)
EPS = 1e-6
XSCALE = 1.0 / P ** 0.5
MSCALE = 1.0 / (NOPE + ROPE) ** 0.5
MASK = -1e30
RING = 4
UK = 2
UW = UK * CW
AHEAD = RING - 1
BANKS = 4
TWO_PI = 6.283185307179586


def _parts(value, count):
    out = []
    for _ in range(count):
        top = 2.0 ** (math.floor(math.log2(abs(value))) - 11)
        out.append(math.floor(value / top) * top)
        value -= out[-1]
    return out


TWO_PI_PARTS = _parts(TWO_PI, 4)
ROUND = 1.5 * 2.0 ** 23

N_MEM, N_POOL, N_X0, N_F0, N_MLA, N_CQ, N_CKV, N_X1, N_F1, N_OUT = range(10)
STATS = [8, 8, 8, 8, 8, 2, 2, 8, 8, 8]
STAT_END = [sum(STATS[:n + 1]) for n in range(len(STATS))]

G_MIX, G_X, G_FFN, G_MEM, G_CQ, G_CKV = 0, 32, 64, 96, 128, 132


class Phase:
    pass


def plan():
    table = [
        ("mem", 32, 4, (5, 5, 5, 5), 16),
        ("pool", 8, 4, (0, 0, 4, 4), 8),
        ("xq0", 8, 2, (2, 2, 4, 4), 4), ("xo0", 8, 4, (0, 0, 4, 4), 8),
        ("fi0", 16 * NP, 2 * NP, (NP, NP, 0, 0), 2 * NP), ("fo0", 4 * FK // UK, 4, (0, 0, 4, 4), 8),
        ("mi", 24, 3, (2, 1, 1, 1), 4),
        ("mp", 4 * PAIRS, 2 * PAIRS, (2 * PAIRS, 2 * PAIRS, 2 * PAIRS, 2 * PAIRS), PAIRS),
        ("mo", 32, 4, (0, 0, 4, 4), 8),
        ("xq1", 8, 2, (2, 2, 4, 4), 4), ("xo1", 8, 4, (0, 0, 4, 4), 8),
        ("fi1", 16 * NP, 2 * NP, (NP, NP, 0, 0), 2 * NP), ("fo1", 4 * FK // UK, 4, (0, 0, 0, 0), 0),
    ]
    phases, u, g, b, h = {}, 0, 0, [0] * BANKS, 0
    for name, nu, ng, nb, nh in table:
        p = Phase()
        p.unit, p.group, p.bank, p.half = u, g, tuple(b), h
        phases[name] = p
        u, g, h = u + nu, g + ng, h + nh
        b = [x + y for x, y in zip(b, nb)]
    return phases, u


Q_UNITS = ((0, 0), (1, 0), (2, 0), (0, 1), (1, 1), (2, 1), (3, 0), (3, 1))
QK = KB // 2


def out_steps(name, per):
    if name in ("xo0", "xo1"):
        order = ((0, 0), (1, 0), (0, 1), (1, 1), (2, 0), (2, 1), (3, 0), (3, 1))
        turned = {4: 0, 5: 1, 7: 2}
    else:
        order = [(c, j) for c in range(NC) for j in range(per)]
        turned = {per * c + 1: c - 1 for c in range(1, NC)} if name != "fo1" else {}
    return [(c, j, c if j == per - 1 else None, turned.get(n)) for n, (c, j) in enumerate(order)]


def hybrid_kernel(nc, a, out):
    PH, UNITS = plan()
    with ExitStack() as ctx:
        def sb(name, shape, dt=F32):
            return ctx.enter_context(nc.sbuf_tensor(name, shape, dt))

        def sem(name):
            return ctx.enter_context(nc.semaphore(name))

        raw = sb("raw", [P, RING, UW])
        w_hi = sb("w_hi", [P, RING, UW], F32R)
        w_lo = sb("w_lo", [P, RING, UW], F32R)
        x = sb("x", [P, TB, D])
        xs = sb("xs", [P, 2, TB, CW])
        k_mem1 = sb("k_mem1", [P, XH, S])
        v_mem1 = sb("v_mem1", [P, TB, XH, P])
        area_x = nc.sbuf_base
        sb("area_x", [P, 2 * KB * S])
        area_h = nc.sbuf_base
        sb("area_h", [P, 2 * FK * S])
        small = {}
        for name, shape, dt in (
                ("gains", [P, 136], F32), ("mem_gain_rows", [2 * KB, P], F32),
                ("gain_rows", [6 * KB, P], F32), ("gain_rows2", [2 * RK, P], F32),
                ("ident", [P, P], F32), ("mask", [P, S], F32), ("cos", [P, TB, HR], F32), ("sin", [P, TB, HR], F32),
                ("junk", [P, CW], BF16), ("sums", [P, 10, TB, NC], F32), ("var", [P, 10, TB], F32),
                ("total", [P, 10, TB], F32), ("rs", [P, 10, TB], F32), ("rsq", [P, 10, TB], F32),
                ("minus_half", [P, TB], F32), ("pace", [P, 2], F32), ("neg_max", [P, HEADS, TB], F32),
                ("exp_sum", [P, HEADS, TB], F32), ("inv_sum", [P, HEADS, TB], F32),
                ("scaled_max", [P, XH, TB], F32)):
            small[name] = sb(name, shape, dt)
        gains, mem_gain_rows, gain_rows, gain_rows2 = (
            small[n] for n in ("gains", "mem_gain_rows", "gain_rows", "gain_rows2"))
        ident, mask, cos, sin, junk = (small[n] for n in ("ident", "mask", "cos", "sin", "junk"))
        sums, var, total, rs, rsq = (small[n] for n in ("sums", "var", "total", "rs", "rsq"))
        minus_half, pace, neg_max, exp_sum, inv_sum, scaled_max = (
            small[n] for n in ("minus_half", "pace", "neg_max", "exp_sum", "inv_sum", "scaled_max"))

        def at(name, shape, offset, dt=F32):
            return nc.alloc_sbuf_tensor_at(name, shape, dt, offset=offset)

        KBYTES = S * 4
        x_hi = at("x_hi", [P, KB, S], area_x, F32R)
        x_lo = at("x_lo", [P, KB, S], area_x + KB * KBYTES, F32R)
        mem = at("mem_tok", [P, TB, D], area_x)
        g_out = at("g_out", [P, D], area_x)
        xg = at("xg", [P, TB, D], area_x + KB * KBYTES)
        h_hi = at("h_hi", [P, FK, S], area_h, F32R)
        lo0 = area_h + FK * KBYTES
        h_lo = at("h_lo", [P, FK, S], lo0, F32R)
        r1, r2 = area_h + 32 * KBYTES, lo0 + 32 * KBYTES
        k_mem0 = at("k_mem0", [P, XH, S], r1)
        v_mem0 = at("v_mem0", [P, TB, XH, P], r1 + 4 * KBYTES)
        k_tok = at("k_tok", [P, TB, CW], r1 + 8 * KBYTES)
        pool_s = at("pool_s", [P, D], r2)
        xa = area_h + 8 * KBYTES
        q_t = at("q_t", [P, XH, S], xa + 4 * KBYTES)
        probs = at("probs", [P, 2, TB, S], xa + 8 * KBYTES)
        probs_t = at("probs_t", [P, 2, TB, S], xa + 12 * KBYTES)
        ma, mb = area_h + 24 * KBYTES, lo0 + 24 * KBYTES
        latent_tok = at("latent_tok", [P, TB, LATENTS], ma)
        kh_tok = at("kh_tok", [P, TB, 2, NOPE], ma + 9 * KBYTES)
        vh_tok = at("vh_tok", [P, TB, 2, VD], ma + 11 * KBYTES)
        qh_tok = at("qh_tok", [P, TB, 2, NOPE + ROPE], ma + 13 * KBYTES)
        rope_t = at("rope_t", [P, 4, TB, 2, HR], ma + 16 * KBYTES)
        qh_t = at("qh_t", [P, 2, S], mb)
        kh_t = at("kh_t", [P, 2, S], mb + 2 * KBYTES)
        qr_t = at("qr_t", [ROPE, 2, S], mb + 4 * KBYTES)
        kr_t = at("kr_t", [ROPE, S], mb + 6 * KBYTES)
        neg_s = at("neg_s", [P, 2, 3 * P], mb + 7 * KBYTES)
        mprobs = at("mprobs", [P, 2, 3 * P], mb + 10 * KBYTES)
        mprobs_t = at("mprobs_t", [P, 2, 3 * P], mb + 13 * KBYTES)
        BAND = 4 * (REACH + P)
        bands = xs[:, :, :, :].rearrange("p a b n -> p (a b n)")[:, 0:BAND]
        band_of = (bands[:, 0:4 * REACH].rearrange("p (g n) -> p g n", g=4),
                   bands[:, 4 * REACH:BAND].rearrange("p (g n) -> p g n", g=4))
        s_tok, h_tok = xs[:, 0, :, :], xs[:, 1, :, :]
        angle_t = at("angle_t", [P, 6, TB, HR], r2 + 8 * KBYTES)
        pos_i = at("pos_i", [P, TB], r2 + 8 * KBYTES + 6 * TB * HR * 4, I32)
        pos_f = at("pos_f", [P, TB], r2 + 8 * KBYTES + 6 * TB * HR * 4 + 32)
        freq = at("freq", [P, HR], r2 + 8 * KBYTES + 6 * TB * HR * 4 + 64)

        acc = ctx.enter_context(nc.psum_tensor("acc", [P, 2, TB, CW], F32))
        bank = ctx.enter_context(nc.psum_tensor("bank", [P, BANKS, CW], F32))

        loaded = [sem(f"loaded{s}") for s in range(RING)]
        hi_ready = sem("hi_ready")
        lo_ready = sem("lo_ready")
        unit_used = sem("unit_used")
        acc_free = [sem(f"acc_free{s}") for s in range(2)]
        bank_full = [sem(f"bank_full{k}") for k in range(BANKS)]
        bank_free = [sem(f"bank_free{k}") for k in range(BANKS)]
        halved_hi = sem("halved_hi")
        stats = sem("stats")
        var_ready = sem("var_ready")
        rs_ready = sem("rs_ready")
        mixed = sem("mixed")
        k_ready = sem("k_ready")
        roped = sem("roped")
        mem_halved = sem("mem_halved")
        q_ready = sem("q_ready")
        max_ready = sem("max_ready")
        exp_ready = sem("exp_ready")
        probs_ready = sem("probs_ready")
        mem_in, x_in = ([sem(f"{n}{c}") for c in range(NC)] for n in ("mem_in", "x_in"))
        band_in, mem_row_in, rows_in, rope_in, scale_in, g_in = (
            sem(n) for n in ("band_in", "mem_row_in", "rows_in", "rope_in", "scale_in", "g_in"))
        gain_cols = sem("gain_cols")
        gains_ready = sem("gains_ready")
        ident_ready, mask_ready = sem("ident_ready"), sem("mask_ready")
        bands_ready, angle_ready, table_ready = (sem(n) for n in ("bands_ready", "angle_ready", "table_ready"))
        dve_step, pool_step = sem("dve_step"), sem("pool_step")
        dve_recip, rope_step = sem("dve_recip"), sem("rope_step")
        last_product = sem("last_product")
        last_added = sem("last_added")
        xg_ready, stored = sem("xg_ready"), sem("stored")
        y_left, y_right = sem("y_left"), sem("y_right")

        def slot_count(g):
            return g // 2

        def weights(w, k0, kbs, c0, width):
            return w[k0 * P:(k0 + kbs) * P, bass.ds(c0, width)].rearrange("(b p) n -> p b n", p=P)

        block = ctx.enter_context(nc.Block())

        @block.sync
        def _(sp):
            def load(n, slot, w, k0, c0, kbs=UK, width=CW):
                if not isinstance(n, int) or n >= RING:
                    sp.wait_ge(lo_ready, n - RING + 1)
                sp.dma_start(raw[:, slot, 0:kbs * width].rearrange("p (b n) -> p b n", b=kbs),
                             weights(w, k0, kbs, c0, width)).then_inc(loaded[slot], 16)

            def group(n, base, w, c0, nk, width=CW):
                for j in range(nk // UK):
                    load(n + j, (base + j) % RING, w, UK * j, c0, width=width)

            mem_v = a["mem"][0].rearrange("(t p) d -> p t d", p=P)

            def memory(c):
                cols = slice(c * CW, (c + 1) * CW)
                sp.dma_start(mem[:, :, cols], mem_v[:, :, cols]).then_inc(mem_in[c], 16)

            memory(0)
            for j in range(RING):
                load(j, j, a["xattn_w_kv"][0], UK * j, 0)
                if j == 1:
                    memory(1)
            memory(2)
            memory(3)
            for j in range(RING, 8):
                load(j, j % RING, a["xattn_w_kv"][0], UK * j, 0)
            x_v = a["x"][0].rearrange("(t p) d -> p t d", p=P)
            for j in range(8):
                load(8 + j, j % RING, a["xattn_w_kv"][0], UK * j, CW)
                if j % 2 == 1:
                    cols = slice(j // 2 * CW, (j // 2 + 1) * CW)
                    sp.dma_start(x[:, :, cols], x_v[:, :, cols]).then_inc(x_in[j // 2], 16)
            sp.dma_start(bands, a["bands"]).then_inc(band_in, 16)
            for c in range(2):
                n = PH["mem"].unit + 16 + 8 * c
                group(n, n, a["xattn_w_kv"][1], c * CW, KB)

            for g in range(len(WINDOWS)):
                n = PH["pool"].unit + 2 * g
                group(n, n, a["pool_w"][0, g], 0, CK)

            def wide_out(base, w, nk):
                per = nk // UK
                with sp.Fori(0, NC // 2) as i:
                    for c in range(2):
                        group(base + per * c + i * (2 * per), base + per * c, w, i * (2 * CW) + c * CW, nk)

            def xattn(l):
                for u, (h, part) in enumerate(Q_UNITS):
                    n = PH[f"xq{l}"].unit + u
                    load(n, n % RING, a["xattn_w_q"][l], QK * part, h * P, kbs=QK, width=P)
                for u, (c, j, _, _) in enumerate(out_steps(f"xo{l}", XH // UK)):
                    n = PH[f"xo{l}"].unit + u
                    load(n, n % RING, a["xattn_w_o"][l], UK * j, c * CW)

            def ffn(l):
                base = PH[f"fi{l}"].unit
                with sp.Fori(0, NP) as i:
                    group(base + i * 16, base, a["ffn_w_in"][l], i * CW, KB)
                    group(base + 8 + i * 16, base + 8, a["ffn_w_in"][l], i * CW + F, KB)
                wide_out(PH[f"fo{l}"].unit, a["ffn_w_out"][l], FK)

            xattn(0)
            ffn(0)
            for q, (c0, width) in enumerate(LATENT_COLS):
                n = PH["mi"].unit + 8 * q
                group(n, n, a["mla_w_in"][0], c0, KB, width=width)
            base = PH["mp"].unit
            with sp.Fori(0, PAIRS) as i:
                group(base + i * 4, base, a["mla_w_q_up"][0], i * QW, RK, width=QW)
                group(base + 2 + i * 4, base + 2, a["mla_w_kv_up"][0], i * CW, RK)
            wide_out(PH["mo"].unit, a["mla_w_out"][0], KB)
            xattn(1)
            ffn(1)
            out_v = out[0].rearrange("(t p) d -> p t d", p=P)
            for t in range(TB):
                for ready, cols in ((y_left, slice(0, D // 2)), (y_right, slice(D // 2, D))):
                    sp.wait_ge(ready, t + 1)
                    sp.dma_start(out_v[:, t, cols], xg[:, t, cols]).then_inc(stored, 16)
            sp.wait_ge(stored, 16 * 2 * TB)

        @block.tensor
        def _(pe):
            def unit(n, base, src_hi, src_lo, k0, g_slot, first, last, kbs=UK, width=CW, before=None):
                slot = base % RING
                pe.wait_ge(lo_ready, n + 1)
                for b in range(kbs):
                    if before:
                        before(b)
                    cols = slice(b * width, (b + 1) * width)
                    for t in range(TB):
                        o = acc[:, g_slot, t, 0:width]
                        hi = src_hi[:, k0 + b, t * P:(t + 1) * P]
                        lo = src_lo[:, k0 + b, t * P:(t + 1) * P]
                        pe.matmul(o, hi, w_hi[:, slot, cols], start=(first and b == 0), stop=False)
                        pe.matmul(o, hi, w_lo[:, slot, cols], start=False, stop=False)
                        mm = pe.matmul(o, lo, w_hi[:, slot, cols], start=False, stop=(last and b == kbs - 1))
                mm.then_inc(unit_used, 1)

            def slot_ready(g, count):
                if not isinstance(count, int) or count > 0:
                    pe.wait_ge(acc_free[g % 2], count)

            def bank_ready(k, count):
                if not isinstance(count, int) or count > 0:
                    pe.wait_ge(bank_free[k], count)

            def four(k, count, parts, rows=P):
                if count is not None:
                    bank_ready(k, count)
                for j, src in enumerate(parts):
                    tr = pe.transpose(bank[0:rows, k, j * P:(j + 1) * P], src, ident[:, :])
                tr.then_inc(bank_full[k], 1)

            def turn_chunk(name, c):
                ph = PH[name]
                g = ph.group + c
                if name == "pool":
                    pe.wait_ge(mixed, c + 1)
                else:
                    pe.wait_ge(acc_free[g % 2], slot_count(g) + 1)
                for m in range(2):
                    four(2 + m, ph.bank[2] + c, [x[:, t, kb * P:(kb + 1) * P]
                                                 for kb in range(c * CK + 2 * m, c * CK + 2 * m + 2) for t in range(TB)])

            def turn_memory(m):
                pe.wait_ge(mem_in[m // 2], 16)
                four(m % 4, m // 4, [mem[:, t, (2 * m + k) * P:(2 * m + k + 1) * P]
                                     for k in range(2) for t in range(TB)])

            def keep_warm(count):
                for _ in range(count):
                    pe.transpose(acc[:, 0, 0, 0:P], ident[:, :], ident[:, :])

            pe.wait_ge(ident_ready, 2)
            keep_warm(12)
            pe.wait_ge(mem_row_in, 16)
            pe.transpose(acc[:, 1, 1, 0:2 * KB], mem_gain_rows[:, :], ident[0:2 * KB, 0:2 * KB]).then_inc(gain_cols, 1)
            for m in range(3):
                turn_memory(m)
                if m == 1:
                    keep_warm(10)
            turn = [2, 2, 2, 2]
            ph = PH["mem"]
            for l in range(2):
                for c in range(2):
                    g = ph.group + 2 * l + c
                    if g == 1:
                        pe.wait_ge(gains_ready, 2)
                    slot_ready(g, slot_count(g))
                    for j in range(8):
                        n = ph.unit + 16 * l + 8 * c + j
                        if l == 0 and c == 0:
                            pe.wait_ge(mem_halved, j + 1)
                        if l == 1 and c == 0:
                            pe.wait_ge(bank_free[j % 4], 1 + j // 4)
                        unit(n, n, h_hi[:, 16 * l:16 * l + 16, :], h_lo[:, 16 * l:16 * l + 16, :],
                             UK * j, g % 2, j == 0, j == 7)
                        if l == 0 and c == 0 and j + 3 < 8:
                            turn_memory(j + 3)
                        if l == 0 and c == 0 and j == 5:
                            pe.wait_ge(rows_in, 16 * 5)
                            pe.transpose(acc[:, 1, 0, 0:6 * KB], gain_rows[:, :], ident[0:6 * KB, 0:6 * KB])
                            pe.transpose(acc[:, 1, 1, P:P + 2 * RK], gain_rows2[:, :],
                                         ident[0:2 * RK, 0:2 * RK]).then_inc(gain_cols, 1)
                        if c == 1 and j == (0 if l else 4):
                            pe.wait_ge(acc_free[(g - 1) % 2], slot_count(g - 1) + 1)
                            for m in range(2):
                                k = 2 * l + m
                                four(k, turn[k], [k_tok[:, t, (2 * m + hh) * P:(2 * m + hh + 1) * P]
                                                  for hh in range(2) for t in range(TB)])
                                turn[k] += 1
                        if l == 1 and c == 1:
                            if j == 0:
                                pe.wait_ge(bands_ready, 2)
                            bank_ready(j % 4, turn[j % 4])
                            for k in range(2):
                                kb = 2 * j + k
                                o = bank[:, j % 4, k * S:(k + 1) * S]
                                for t in range(TB):
                                    to = slice(0, REACH) if t == 0 else slice(P, S)
                                    mm = pe.matmul(o[:, to], x[:, t, kb * P:(kb + 1) * P],
                                                   band_of[t][:, kb // CK, :], start=(k == 0 and t == 0),
                                                   stop=(t == 1), skip_group_check=True)
                            mm.then_inc(bank_full[j % 4], 1)
                            turn[j % 4] += 1

            def out_phase(name, src_hi, src_lo, per, before=None, done=0, pool=False, rest=None):
                ph = PH[name]
                for u, (c, j, _, turned) in enumerate(out_steps(name, per)):
                    if u < done:
                        continue
                    g = ph.group + c
                    n = ph.unit + u
                    if n >= UNITS - RING:
                        continue
                    if j == 0:
                        slot_ready(g, slot_count(g))
                    unit(n, n, src_hi, src_lo, UK * j + (CK * c if pool else 0), g % 2, j == 0, j == per - 1,
                         before=(lambda b: before(c, j, b)) if before else None)
                    if turned is not None:
                        turn_chunk(name, turned)
                    if u == 1 and rest:
                        rest()

            def pooled(c, j, b):
                m = 2 * c + j
                if b == 0:
                    pe.wait_ge(bank_free[m % 4], PH["pool"].bank[m % 4] - 1 + m // 4)

            out_phase("pool", x_hi, x_lo, CK // UK, pooled, pool=True)

            def wait_x(ph, j):
                pe.wait_ge(bank_free[2 + j % 2], ph.bank[2 + j % 2] - 3 + j // 2)

            def xattn(l):
                ph = PH[f"xq{l}"]
                k_mem, v_mem = (k_mem0, v_mem0) if l == 0 else (k_mem1, v_mem1)
                b = ph.bank

                def queries(u, middle=None):
                    h, part = Q_UNITS[u]
                    n, g = ph.unit + u, ph.group + h // 2
                    slot = n % RING
                    if h % 2 == 0 and part == 0:
                        slot_ready(g, slot_count(g))
                    pe.wait_ge(lo_ready, n + 1)
                    o = acc[:, g % 2, h % 2, 0:S]
                    for k in range(QK):
                        kb = QK * part + k
                        if h == 0 and kb % 2 == 0:
                            wait_x(ph, kb // 2)
                        if k == QK // 2 and middle:
                            middle()
                        wh, wl = (w[:, slot, k * P:(k + 1) * P] for w in (w_hi, w_lo))
                        pe.matmul(o, wh, x_hi[:, kb, :], start=(kb == 0), stop=False)
                        pe.matmul(o, wh, x_lo[:, kb, :], start=False, stop=False)
                        mm = pe.matmul(o, wl, x_hi[:, kb, :], start=False, stop=(kb == KB - 1))
                    mm.then_inc(unit_used, 1)

                def scores(h):
                    g = ph.group + h // 2
                    if h % 2 == 0:
                        pe.wait_ge(q_ready, TB * l + h // 2 + 1)
                    else:
                        pe.wait_ge(acc_free[g % 2], slot_count(g) + 1)
                    bank_ready(h % 2, b[h % 2] + h // 2)
                    for t in range(TB):
                        mm = pe.matmul(bank[:, h % 2, t * S:(t + 1) * S], q_t[:, h, t * P:(t + 1) * P],
                                       k_mem[:, h, :], start=(t == 0), stop=True, skip_group_check=True)
                    mm.then_inc(bank_full[h % 2], 1)

                def turn_probs(h):
                    pe.wait_ge(probs_ready, XH * l + (HEADS if l else 0) + h + 1)
                    four(2, b[2] + h, [probs[:, h % 2, t, k * P:(k + 1) * P] for k in range(TB) for t in range(TB)])

                def values(h):
                    bank_ready(2, b[2] + h + 1)
                    bank_ready(3, b[3] + h)
                    for k in range(TB):
                        mm = pe.matmul(bank[:, 3, 0:S], v_mem[:, k, h, :], probs_t[:, h % 2, k, :],
                                       start=(k == 0), stop=(k == TB - 1))
                    mm.then_inc(bank_full[3], 1)

                queries(0)
                queries(1)
                turn_chunk(("pool", "mo")[l], NC - 1)
                queries(2)
                queries(3)
                queries(4, lambda: scores(0))
                queries(5, lambda: scores(1))
                turn_probs(0)

                def middle_of_6():
                    scores(2)
                    values(0)
                    turn_probs(1)

                queries(6, middle_of_6)
                values(1)
                queries(7, lambda: turn_probs(2))
                values(2)

                def heads_out(c, j, k):
                    if (c, j, k) == (0, 0, 1):
                        scores(3)
                    if (c, j, k) == (1, 0, 1):
                        turn_probs(3)
                    if (c, j, k) == (0, 1, 0):
                        values(3)
                    if c == 0:
                        bank_ready(3, b[3] + UK * j + k + 1)

                out_phase(f"xo{l}", h_hi, h_lo, XH // UK, heads_out)

            def ffn(l):
                ph = PH[f"fi{l}"]

                def turn_hidden(i, cnt_up):
                    pe.wait_ge(acc_free[(ph.group + 1) % 2], cnt_up)
                    for m in range(2):
                        four(m, ph.bank[m] + i, [h_tok[:, t, (2 * m + k) * P:(2 * m + k + 1) * P]
                                                 for k in range(2) for t in range(TB)])

                def pair(i, first):
                    for c in range(2):
                        g = ph.group + c
                        slot_ready(g, slot_count(g) + i)
                        for j in range(8):
                            if first and c == 0:
                                wait_x(ph, j)
                            unit(ph.unit + 8 * c + j + i * 16, ph.unit + 8 * c + j, x_hi, x_lo, UK * j,
                                 g % 2, j == 0, j == 7)
                            if c == 0 and j == 1 and first:
                                turn_chunk(f"xo{l}", NC - 1)
                            if c == 0 and j == 0 and not first:
                                turn_hidden(i - 1, slot_count(ph.group + 1) + i)

                pair(0, True)
                with pe.Fori(1, NP) as i:
                    pair(i, False)

                def last_hidden(c, j, b):
                    if c == 0 and j >= FK // UK - 2 and b == 0:
                        m = j - (FK // UK - 2)
                        bank_ready(m, ph.bank[m] + NP)

                out_phase(f"fo{l}", h_hi, h_lo, FK // UK, last_hidden,
                          rest=lambda: turn_hidden(NP - 1, slot_count(ph.group + 1) + NP))

            xattn(0)
            ffn(0)

            ph, pp = PH["mi"], PH["mp"]
            for q, (c0, width) in enumerate(LATENT_COLS):
                g = ph.group + q
                slot_ready(g, slot_count(g))
                for j in range(8):
                    if q == 0:
                        wait_x(ph, j)
                    n = ph.unit + 8 * q + j
                    unit(n, n, x_hi, x_lo, UK * j, g % 2, j == 0, j == 7, width=width)
                    if q == 0 and j == 1:
                        turn_chunk("fo0", NC - 1)
                    if q == 2 and j == 1:
                        g1 = ph.group + 1
                        pe.wait_ge(acc_free[g1 % 2], slot_count(g1) + 1)
                        for m in range(2):
                            four(m, ph.bank[m], [latent_tok[:, t, kb * P:(kb + 1) * P]
                                                 for kb in (2 * m, 2 * m + 1) for t in range(TB)])

            def q_up(i, j):
                g = pp.group
                if j == 0:
                    slot_ready(g, slot_count(g) + i)
                unit(pp.unit + j + i * 4, pp.unit + j, h_hi[:, 16:20, :], h_lo[:, 16:20, :], UK * j, g % 2,
                     j == 0, j == 1, width=QW)

            def kv_up(i, j):
                g = pp.group + 1
                if j == 0:
                    slot_ready(g, slot_count(g) + i)
                unit(pp.unit + 2 + j + i * 4, pp.unit + 2 + j, h_hi[:, 20:24, :], h_lo[:, 20:24, :], UK * j, g % 2,
                     j == 0, j == 1)

            for m in range(2):
                bank_ready(m, ph.bank[m] + 1)
            q_up(0, 0)
            g2 = ph.group + 2
            pe.wait_ge(acc_free[g2 % 2], slot_count(g2) + 1)
            for m in range(2):
                four(2 + m, ph.bank[2 + m], [latent_tok[:, t, kb * P:(kb + 1) * P]
                                             for kb in (RK + 2 * m, RK + 2 * m + 1) for t in range(TB)])
            q_up(0, 1)
            pe.wait_ge(roped, 1)
            four(0, ph.bank[0] + 1, [latent_tok[:, t, 2 * RANK:] for t in range(TB)], rows=ROPE)
            for m in range(2):
                bank_ready(2 + m, ph.bank[2 + m] + 1)
            kv_up(0, 0)
            kv_up(0, 1)

            def output_up(j):
                po = PH["mo"]
                if j == 0:
                    slot_ready(po.group, slot_count(po.group))
                unit(po.unit + j, po.unit + j, h_hi, h_lo, UK * j, po.group % 2, j == 0, False)

            def attend(i, more):
                b = pp.bank
                heads = range(2)

                def between(j):
                    if not more:
                        output_up(j)
                    elif j < 2:
                        q_up(i + 1, j)
                    else:
                        kv_up(i + 1, j - 2)

                pe.wait_ge(k_ready, i + 1)
                four(1, b[1] + i * 2, [kh_tok[:, t, h, :] for h in heads for t in range(TB)])
                pe.wait_ge(roped, i + 2)
                bank_ready(2, b[2] + i * 2)
                pe.wait_ge(acc_free[pp.group % 2], slot_count(pp.group) + 1 + i)
                four(3, b[3] + i * 2, [qh_tok[:, t, h, 0:NOPE] for h in heads for t in range(TB)])
                four(2, None, [qh_tok[:, t, h, NOPE:] for h in heads for t in range(TB)], rows=ROPE)
                between(0)
                for k in (1, 3, 2):
                    bank_ready(k, b[k] + 1 + i * 2)
                for h in heads:
                    k, count = (3, b[3] + 1 + i * 2) if h == 0 else (0, b[0] + i * 2)
                    bank_ready(k, count)
                    for t in range(TB):
                        keys = (t + 1) * P
                        o = bank[:, k, t * P:t * P + keys]
                        pe.matmul(o, qh_t[:, h, t * P:(t + 1) * P], kh_t[:, h, 0:keys], start=True, stop=False)
                        mm = pe.matmul(o, qr_t[:, h, t * P:(t + 1) * P], kr_t[:, 0:keys], start=False, stop=True)
                    mm.then_inc(bank_full[k], 1)
                between(1)
                between(2)
                for h in heads:
                    pe.wait_ge(probs_ready, XH + h + 1 + i * 2)
                    four(1 + h, b[1 + h] + 1 + i * 2, [mprobs[:, h, j * P:(j + 1) * P] for j in range(3)])
                between(3)
                bank_ready(0, b[0] + 1 + i * 2)
                pe.wait_ge(acc_free[(pp.group + 1) % 2], slot_count(pp.group + 1) + 1 + i)
                for h in heads:
                    bank_ready(1 + h, b[1 + h] + 2 + i * 2)
                    o = bank[:, 0, h * S:(h + 1) * S]
                    pe.matmul(o, vh_tok[:, 0, h, :], mprobs_t[:, h, 0:S], start=True, stop=False)
                    mm = pe.matmul(o[:, P:S], vh_tok[:, 1, h, :], mprobs_t[:, h, S:S + P], start=False, stop=True)
                mm.then_inc(bank_full[0], 1)

            with pe.Fori(0, PAIRS - 1) as i:
                attend(i, True)
            attend(PAIRS - 1, False)

            def last_heads(c, j, b):
                if c == 0 and j == KB // UK - 1 and b == 0:
                    bank_ready(0, pp.bank[0] + 2 * PAIRS)

            out_phase("mo", h_hi, h_lo, KB // UK, last_heads, done=4)
            xattn(1)
            ffn(1)
            g = PH["fo1"].group + NC - 1
            for t in range(TB):
                for n in range(UNITS - RING, UNITS):
                    if t == 0:
                        pe.wait_ge(lo_ready, n + 1)
                    for b in range(UK):
                        k, cols = FK - UK * (UNITS - n) + b, slice(b * CW, (b + 1) * CW)
                        hi, lo = (h[:, k, t * P:(t + 1) * P] for h in (h_hi, h_lo))
                        o = acc[:, g % 2, t, :]
                        pe.matmul(o, hi, w_hi[:, n % RING, cols], start=False, stop=False)
                        pe.matmul(o, hi, w_lo[:, n % RING, cols], start=False, stop=False)
                        mm = pe.matmul(o, lo, w_hi[:, n % RING, cols], start=False, stop=(k == FK - 1))
                mm.then_inc(last_product, 1)

        def width_of(n):
            j = n - PH["mi"].unit
            if 0 <= j < 24:
                return UK * LATENT_COLS[j // 8][1]
            j = n - PH["mp"].unit
            return UK * QW if 0 <= j < 4 * PAIRS and j % 4 < 2 else UW

        flat = "p k s -> p (k s)"
        x_hi32 = x_hi[:, :, :].bitcast(F32)
        h_hi32 = h_hi[:, :, :].bitcast(F32)
        h_hi_flat, h_lo_flat = h_hi[:, :, :].rearrange(flat), h_lo[:, :, :].rearrange(flat)
        h_hi32_flat = h_hi32.rearrange(flat)

        TURNED = {"pool": (G_X, N_X0), "xo0": (G_FFN, N_F0), "fo0": (G_MIX + KB, N_MLA), "mo": (G_X + KB, N_X1),
                  "xo1": (G_FFN + KB, N_F1), "fo1": (None, N_OUT)}

        @block.scalar
        def _(act):
            def half(s, i=0, per=0, width=None):
                if isinstance(i, int):
                    s, i, per = s + i * per, 0, 0
                if s >= UNITS:
                    return
                width = width or width_of(s)
                slot = s % RING
                act.wait_ge(loaded[slot], i * (16 * per // RING) + 16 * (s // RING + 1))
                if s >= RING:
                    act.wait_ge(unit_used, i * per + s - RING + 1)
                act.activation(w_hi[:, slot, 0:width], raw[:, slot, 0:width], ACT.Copy).then_inc(hi_ready, 1)

            def squares(norm, t, c, src, before):
                before += STAT_END[norm] - STATS[norm]
                if before > 0:
                    act.wait_ge(stats, before)
                act.activation(junk[:, :], src, ACT.Square, accum_out=sums[:, norm, t, c:c + 1]).then_inc(stats, 1)

            def turned(k, count, dst, kbs, gain):
                act.wait_ge(bank_full[k], count)
                for j, kb in enumerate(kbs):
                    last = act.activation(dst(kb), bank[:, k, j * S:(j + 1) * S], ACT.Copy, scale=gain(kb))
                last.then_inc(halved_hi, 1)

            act.dma_start(mem_gain_rows[:, :],
                          a["norm_mem_g"].rearrange("l (k p) -> (l k) p", p=P)).then_inc(mem_row_in, 16)
            act.wait_ge(ident_ready, 2)
            act.activation(pace[:, 1:2], ident[:, 0:1], ACT.Copy)

            def memory_halved(m):
                act.wait_ge(bank_full[m % 4], 1 + m // 4)
                for l in range(2):
                    for k in range(2):
                        kb = 2 * m + k
                        last = act.activation(h_hi[:, 16 * l + kb, :], bank[:, m % 4, k * S:(k + 1) * S], ACT.Copy,
                                              scale=gains[:, G_MEM + 16 * l + kb:G_MEM + 16 * l + kb + 1])
                last.then_inc(halved_hi, 1)
                if m < AHEAD:
                    half(m)

            act.wait_ge(gains_ready, 1)
            for m in range(AHEAD):
                memory_halved(m)
            ph = PH["mem"]
            for j in range(32):
                half(ph.unit + j + AHEAD)
                if j + AHEAD < KB // 2:
                    memory_halved(j + AHEAD)
                if j == 1:
                    for n, name in enumerate(("norm_mix_g", "norm_xattn_g", "norm_ffn_g")):
                        act.dma_start(gain_rows[32 * n:32 * n + 32, :],
                                      a[name].rearrange("l (k p) -> (l k) p", p=P)).then_inc(rows_in, 16)
                    for n, name in enumerate(("mla_q_norm_g", "mla_kv_norm_g")):
                        act.dma_start(gain_rows2[n * RK:(n + 1) * RK, :],
                                      a[name].rearrange("l (k p) -> (l k) p", p=P)).then_inc(rows_in, 16)
                if j == 3:
                    act.dma_start(pos_i[:, :], a["positions"][0].rearrange("(t p) -> p t", p=P),
                                  allow_slow_non_contiguous=True).then_inc(rope_in, 16)
                    act.dma_start(freq[:, :], a["inv_freq"].partition_broadcast(P)).then_inc(rope_in, 16)
                if j == 16:
                    act.dma_start(pool_s[:, :], a["pool_scale"][0].partition_broadcast(P)).then_inc(scale_in, 16)
                if 6 <= j < 10:
                    for n in range(2 * (j - 6), 2 * (j - 6) + 2):
                        squares(N_MEM, n // NC, n % NC, mem[:, n // NC, n % NC * CW:(n % NC + 1) * CW], n)
                if 10 <= j < 18:
                    n = j - 10
                    t, c = n % TB, n // TB
                    if t == 0:
                        act.wait_ge(x_in[c], 16)
                    squares(N_POOL, t, c, x[:, t, c * CW:(c + 1) * CW], n)
                if j == 18:
                    act.wait_ge(angle_ready, 1)
                    act.activation(sin[:, :, :], angle_t[:, 1, :, :], ACT.Sin)
                    act.activation(cos[:, :, :], angle_t[:, 2, :, :], ACT.Sin).then_inc(table_ready, 1)
                if j in (12, 24):
                    l = j // 24
                    k_mem = k_mem1 if l else k_mem0
                    for m in range(2):
                        k = 2 * l + m
                        act.wait_ge(bank_full[k], 3)
                        act.activation(k_mem[:, 2 * m:2 * m + 2, :].rearrange(flat), bank[:, k, :],
                                       ACT.Copy).then_inc(bank_free[k], 1)
                if j == 24:
                    act.wait_ge(gains_ready, 2)
                if j >= 24:
                    m = j - 24
                    k = m % 4
                    turned(k, PH["pool"].bank[k] - 1 + m // 4, lambda kb: x_hi[:, kb, :], (2 * m, 2 * m + 1),
                           lambda kb: gains[:, G_MIX + kb:G_MIX + kb + 1])

            def chunk_squares(name, c):
                g = PH[name].group + c
                if name == "pool":
                    act.wait_ge(mixed, c + 1)
                else:
                    act.wait_ge(acc_free[g % 2], slot_count(g) + 1)
                for t in range(TB):
                    squares(TURNED[name][1], t, c, x[:, t, c * CW:(c + 1) * CW], c * 2 + t)

            def chunk_turned(name, c):
                gain = TURNED[name][0]
                for m in range(2):
                    c0 = c * CK + 2 * m
                    turned(2 + m, PH[name].bank[2] + c + 1, lambda kb: x_hi[:, kb, :], (c0, c0 + 1),
                           lambda kb: gains[:, gain + kb:gain + kb + 1])

            def out_phase(name, per, done=0, rest=None):
                ph, ended = PH[name], None
                for u, (_, _, ends, turned) in enumerate(out_steps(name, per)):
                    if u < done:
                        continue
                    half(ph.unit + u + AHEAD)
                    if ended is not None:
                        chunk_squares(name, ended)
                    ended = ends
                    if turned is not None:
                        chunk_turned(name, turned)
                    if u == 1 and rest:
                        rest()

            def by_token(g, unit_count, dst, scale, width=CW):
                act.wait_ge(unit_used, unit_count)
                for t in range(TB):
                    last = act.activation(dst(t), acc[:, g % 2, t, 0:width], ACT.Copy, scale=scale(t))
                last.then_inc(acc_free[g % 2], 1)

            def xattn(l):
                ph, po = PH[f"xq{l}"], PH[f"xo{l}"]
                norm, b = (N_X0, N_X1)[l], ph.bank

                def queries(h):
                    g = ph.group + h // 2
                    act.wait_ge(unit_used, ph.unit + Q_UNITS.index((h, 1)) + 1)
                    act.activation(q_t[:, h, :], acc[:, g % 2, h % 2, 0:S],
                                   ACT.Copy).then_inc(acc_free[g % 2] if h % 2 else q_ready, 1)

                def exps(h):
                    act.wait_ge(max_ready, XH * l + h + 1)
                    for t in range(TB):
                        last = act.activation(probs[:, h % 2, t, :], bank[:, h % 2, t * S:(t + 1) * S], ACT.Exp,
                                              scale=rsq[:, norm, t:t + 1], bias=scaled_max[:, h, t:t + 1],
                                              accum_out=exp_sum[:, h, t:t + 1])
                    last.then_inc(bank_free[h % 2], 1)

                def output(h):
                    act.wait_ge(bank_full[3], b[3] + h + 1)
                    act.activation(h_hi[:, h, :], bank[:, 3, 0:S], ACT.Copy).then_inc(halved_hi, 1)

                half(ph.unit + AHEAD)
                chunk_squares(("pool", "mo")[l], NC - 1)
                half(ph.unit + 1 + AHEAD)
                chunk_turned(("pool", "mo")[l], NC - 1)
                half(ph.unit + 5)
                act.wait_ge(rs_ready, norm + 1)
                act.activation(pace[:, 1:2], rsq[:, norm, 0:1], ACT.Exp, scale=0.0)
                queries(0)
                half(ph.unit + 6)
                half(ph.unit + 7)
                exps(0)
                queries(1)
                half(po.unit)
                exps(1)
                queries(2)
                half(po.unit + 1)
                output(0)
                exps(2)
                output(1)
                half(po.unit + 2)
                queries(3)
                half(po.unit + 3)
                output(2)
                exps(3)
                half(po.unit + 4)
                output(3)
                out_phase(f"xo{l}", XH // UK, done=2)

            def ffn(l):
                ph, norm = PH[f"fi{l}"], (N_F0, N_F1)[l]

                def hidden(i):
                    for m in range(2):
                        act.wait_ge(bank_full[m], i + ph.bank[m] + 1)
                        act.activation(h_hi_flat[:, bass.ds(i * (CK * S) + 2 * m * S, 2 * S)], bank[:, m, :],
                                       ACT.Copy).then_inc(halved_hi, 1)

                def pair(i, first):
                    for j in range(16):
                        half(ph.unit + j + AHEAD, i, 16)
                        if j == 0 and first:
                            chunk_squares(f"xo{l}", NC - 1)
                        if j == 1 and first:
                            chunk_turned(f"xo{l}", NC - 1)
                        if j == 0 and not first:
                            hidden(i - 1)
                        if j == 7:
                            if first:
                                act.wait_ge(rs_ready, norm + 1)
                                act.wait_ge(mixed, NC)
                            act.wait_ge(unit_used, i * 16 + ph.unit + 8)
                            for t in range(TB):
                                last = act.activation(s_tok[:, t, :], acc[:, ph.group % 2, t, :], ACT.Silu,
                                                      scale=rs[:, norm, t:t + 1])
                            last.then_inc(acc_free[ph.group % 2], 1)

                pair(0, True)
                with act.Fori(1, NP) as i:
                    pair(i, False)

                def rest():
                    hidden(NP - 1)
                    if l == 1:
                        act.wait_ge(unit_used, PH["fo1"].unit)
                        act.dma_start(g_out[:, :], a["final_norm_g"].partition_broadcast(P)).then_inc(g_in, 16)

                out_phase(f"fo{l}", FK // UK, rest=rest)

            out_phase("pool", CK // UK)
            xattn(0)
            ffn(0)

            ph, pp = PH["mi"], PH["mp"]

            def latent(q):
                c0, width = LATENT_COLS[q]
                by_token(ph.group + q, ph.unit + 8 * q + 8, lambda t: latent_tok[:, t, c0:c0 + width],
                         lambda t: rs[:, N_MLA, t:t + 1], width)

            def latent_squares(norm, q, c0):
                for g in (ph.group + q - 1, ph.group + q):
                    act.wait_ge(acc_free[g % 2], slot_count(g) + 1)
                for t in range(TB):
                    squares(norm, t, 0, latent_tok[:, t, c0:c0 + RANK], t)

            def latent_turned(k, count, m, kb0, gain):
                turned(k, count, lambda kb: h_hi[:, kb0 + kb, :], (2 * m, 2 * m + 1),
                       lambda kb: gains[:, gain + kb:gain + kb + 1])

            for j in range(24):
                half(ph.unit + j + AHEAD)
                if j == 0:
                    chunk_squares("fo0", NC - 1)
                if j == 1:
                    chunk_turned("fo0", NC - 1)
                if j == 7:
                    act.wait_ge(rs_ready, N_MLA + 1)
                    latent(0)
                if j == 15:
                    latent(1)
                    latent_squares(N_CQ, 1, 0)
                if j == 17:
                    for m in range(2):
                        latent_turned(m, ph.bank[m] + 1, m, 16, G_CQ)
                if j == 23:
                    latent(2)

            def queries(i):
                by_token(pp.group, i * 4 + pp.unit + 2,
                         lambda t: qh_tok[:, t, :, :].rearrange("p h n -> p (h n)"), lambda t: rsq[:, N_CQ, t:t + 1], QW)

            half(pp.unit + AHEAD)
            for m in range(2):
                latent_turned(2 + m, ph.bank[2 + m] + 1, m, 20, G_CKV)
            latent_squares(N_CKV, 2, RANK)
            half(pp.unit + 1 + AHEAD)
            act.wait_ge(bank_full[0], ph.bank[0] + 2)
            act.activation(kr_t[:, :], bank[0:ROPE, 0, 0:S], ACT.Copy).then_inc(bank_free[0], 1)
            act.wait_ge(rs_ready, N_CQ + 1)
            queries(0)
            half(pp.unit + 2 + AHEAD)
            half(pp.unit + 3 + AHEAD)

            def ahead(i, j):
                n = pp.unit + 4 + j + AHEAD
                half(n, i, 4, width_of(n + (i * 4 if isinstance(i, int) else 0)))

            def attend(i):
                b = pp.bank
                act.wait_ge(bank_full[3], i * 2 + b[3] + 1)
                act.activation(qh_t[:, :, :].rearrange(flat), bank[:, 3, :], ACT.Copy).then_inc(bank_free[3], 1)
                act.wait_ge(bank_full[2], i * 2 + b[2] + 1)
                act.activation(qr_t[:, :, :].rearrange(flat), bank[0:ROPE, 2, :], ACT.Copy).then_inc(bank_free[2], 1)
                ahead(i, 0)
                for h in range(2):
                    k, count = (3, i * 2 + b[3] + 2) if h == 0 else (0, i * 2 + b[0] + 1)
                    act.wait_ge(bank_free[k], count)
                    for t, cols in enumerate((slice(0, P), slice(P, 3 * P))):
                        last = act.activation(mprobs[:, h, cols], neg_s[:, h, cols], ACT.Exp, scale=-1.0,
                                              bias=neg_max[:, h, t:t + 1], accum_out=exp_sum[:, h, t:t + 1])
                    last.then_inc(exp_ready, 1)
                ahead(i, 1)

            def attended(i, more):
                if more:
                    queries(i + 1)
                ahead(i, 2)
                ahead(i, 3)
                act.wait_ge(bank_full[0], i * 2 + pp.bank[0] + 2)
                act.activation(h_hi_flat[:, bass.ds(i * (2 * S), 2 * S)], bank[:, 0, :],
                               ACT.Copy).then_inc(halved_hi, 1)

            attend(0)
            with act.Fori(0, PAIRS - 3) as i:
                attended(i, True)
                attend(i + 1)
            for i in range(PAIRS - 3, PAIRS):
                attended(i, i + 1 < PAIRS)
                if i + 1 < PAIRS:
                    attend(i + 1)
            out_phase("mo", KB // UK, done=4)
            xattn(1)
            ffn(1)
            for t in range(TB):
                act.wait_ge(last_added, t + 1)
                squares(N_OUT, t, NC - 1, x[:, t, D - CW:D], 2 * (NC - 1) + t)
                if t == 0:
                    act.wait_ge(xg_ready, 2)
                act.wait_ge(rs_ready, N_OUT + 1 + t)
                act.activation(xg[:, t, 0:D // 2], xg[:, t, 0:D // 2], ACT.Copy,
                               scale=rs[:, N_OUT, t:t + 1]).then_inc(y_left, 1)

        @block.vector
        def _(dve):
            steps = [0]

            def step(ins):
                steps[0] += 1
                ins.then_inc(dve_step, 1)
                dve.wait_ge(dve_step, steps[0])

            def low(s, i=0, per=0, width=None):
                if isinstance(i, int):
                    s, i, per = s + i * per, 0, 0
                if s >= UNITS:
                    return
                width = width or width_of(s)
                slot = s % RING
                dve.wait_ge(hi_ready, i * per + s + 1)
                dve.tensor_tensor(w_lo[:, slot, 0:width], raw[:, slot, 0:width],
                                  w_hi[:, slot, 0:width].bitcast(F32), ALU.subtract).then_inc(lo_ready, 1)

            def turned(k, count, dst, hi32, kbs, gain):
                dve.wait_ge(halved_hi, count)
                for j, kb in enumerate(kbs):
                    last = dve.scalar_tensor_tensor(out=dst(kb), in0=bank[:, k, j * S:(j + 1) * S], scalar=gain(kb),
                                                    in1=hi32(kb), op0=ALU.mult, op1=ALU.subtract)
                last.then_inc(bank_free[k], 1)

            def variance(norm, width=D):
                dve.wait_ge(stats, STAT_END[norm])
                if width == D:
                    step(dve.tensor_reduce(total[:, norm, :], sums[:, norm, :, :], AX_X, ALU.add))
                    src = total[:, norm, :]
                else:
                    src = sums[:, norm, :, 0]
                dve.tensor_scalar(var[:, norm, :], src, 1.0 / width, EPS, ALU.mult, ALU.add).then_inc(var_ready, 1)

            def rope_angles():
                dve.wait_ge(rope_in, 32)
                step(dve.tensor_copy(pos_f[:, :], pos_i[:, :]))
                for t in range(TB):
                    ins = dve.tensor_scalar(angle_t[:, 0, t, :], freq[:, :], pos_f[:, t:t + 1], None, ALU.mult)
                step(ins)
                r, whole = angle_t[:, 0, :, :], angle_t[:, 3, :, :]
                for block_of in (2048.0, 1.0):
                    step(dve.tensor_scalar(whole, r, 1.0 / (TWO_PI * block_of), ROUND, ALU.mult, ALU.add))
                    step(dve.tensor_scalar(whole, whole, ROUND, None, ALU.subtract))
                    for part in TWO_PI_PARTS:
                        step(dve.scalar_tensor_tensor(out=angle_t[:, 1, :, :], in0=whole, scalar=-part * block_of,
                                                      in1=r, op0=ALU.mult, op1=ALU.add))
                        r = angle_t[:, 1, :, :]
                step(dve.tensor_scalar(r, r, 3.1415925, -3.1415925, ALU.min, ALU.max))
                step(dve.tensor_scalar(whole, r, -1.0, None, ALU.mult))
                step(dve.tensor_tensor(whole, whole, r, ALU.max))
                dve.tensor_scalar(angle_t[:, 2, :, :], whole, -1.0, TWO_PI / 4, ALU.mult, ALU.add).then_inc(angle_ready, 1)

            dve.wait_ge(gain_cols, 1)
            dve.tensor_copy(gains[:, G_MEM:G_MEM + 2 * KB], acc[:, 1, 1, 0:2 * KB]).then_inc(gains_ready, 1)
            dve.wait_ge(gains_ready, 1)

            def memory_halved(m):
                dve.wait_ge(halved_hi, m + 1)
                for l in range(2):
                    for k in range(2):
                        kb = 16 * l + 2 * m + k
                        last = dve.scalar_tensor_tensor(
                            out=h_lo[:, kb, :], in0=bank[:, m % 4, k * S:(k + 1) * S],
                            scalar=gains[:, G_MEM + kb:G_MEM + kb + 1], in1=h_hi32[:, kb, :],
                            op0=ALU.mult, op1=ALU.subtract)
                    last.then_inc(bank_free[m % 4] if l else mem_halved, 1)
                    if l == 0 and m < AHEAD:
                        low(m)

            for m in range(AHEAD):
                memory_halved(m)
            ph = PH["mem"]
            for j in range(32):
                low(ph.unit + j + AHEAD)
                if j + AHEAD < KB // 2:
                    memory_halved(j + AHEAD)
                if j == 6:
                    dve.wait_ge(gain_cols, 2)
                    dve.tensor_copy(gains[:, 0:6 * KB], acc[:, 1, 0, 0:6 * KB])
                    dve.tensor_copy(gains[:, G_CQ:G_CQ + 2 * RK], acc[:, 1, 1, P:P + 2 * RK]).then_inc(gains_ready, 1)
                if j == 9:
                    variance(N_MEM)
                if j == 13:
                    rope_angles()
                if j == 17:
                    variance(N_POOL)
                if j == 19:
                    dve.wait_ge(band_in, 16)
                    dve.wait_ge(rs_ready, N_POOL + 1)
                    for t in range(TB):
                        dve.tensor_scalar(band_of[t], band_of[t], rs[:, N_POOL, t:t + 1], None,
                                          ALU.mult).then_inc(bands_ready, 1)
                if j in (11, 15, 23, 31):
                    q = (11, 15, 23, 31).index(j)
                    g, l, values = ph.group + q, q // 2, q % 2
                    if q == 0:
                        dve.wait_ge(rs_ready, N_MEM + 1)
                    dve.wait_ge(unit_used, ph.unit + 8 * q + 8)
                    v_mem = (v_mem0, v_mem1)[l]
                    for t in range(TB):
                        dst = v_mem[:, t, :, :].rearrange("p h n -> p (h n)") if values else k_tok[:, t, :]
                        last = dve.tensor_scalar(dst, acc[:, g % 2, t, :], rs[:, N_MEM, t:t + 1], None, ALU.mult)
                    last.then_inc(acc_free[g % 2], 1)
                if j == 24:
                    dve.wait_ge(gains_ready, 2)
                if j >= 24:
                    m = j - 24
                    turned(m % 4, PH["mem"].half + KB // 2 + m + 1, lambda kb: x_lo[:, kb, :], lambda kb: x_hi32[:, kb, :],
                           (2 * m, 2 * m + 1), lambda kb: gains[:, G_MIX + kb:G_MIX + kb + 1])

            def add_chunk(name, c, units):
                g, cols = PH[name].group + c, slice(c * CW, (c + 1) * CW)
                dve.wait_ge(unit_used, units)
                if name == "pool":
                    if c == 0:
                        dve.wait_ge(scale_in, 16)
                    if c >= 2:
                        dve.wait_ge(mixed, c - 1)
                for t in range(TB):
                    xc = x[:, t, cols]
                    if name == "pool":
                        last = dve.tensor_tensor(xs[:, c % 2, t, :], acc[:, g % 2, t, :], pool_s[:, cols], ALU.mult)
                    else:
                        last = dve.tensor_tensor(xc, acc[:, g % 2, t, :], xc, ALU.add)
                last.then_inc(acc_free[g % 2], 1)

            def chunk_turned(name, c):
                gain = TURNED[name][0]
                for m in range(2):
                    c0 = c * CK + 2 * m
                    turned(2 + m, PH[name].half + 2 * c + m + 1, lambda kb: x_lo[:, kb, :],
                           lambda kb: x_hi32[:, kb, :], (c0, c0 + 1), lambda kb: gains[:, gain + kb:gain + kb + 1])

            def out_phase(name, per, done=0, rest=None):
                ph = PH[name]
                for u, (_, _, ends, turned) in enumerate(out_steps(name, per)):
                    if u < done:
                        continue
                    if ends is not None and ph.unit + u + 1 < UNITS:
                        add_chunk(name, ends, ph.unit + u + 1)
                    low(ph.unit + u + AHEAD)
                    if turned is not None:
                        chunk_turned(name, turned)
                    if u == 1 and rest:
                        rest()

            def xattn(l):
                ph, po = PH[f"xq{l}"], PH[f"xo{l}"]
                b, norm = ph.bank, (N_X0, N_X1)[l]

                def maximum(h):
                    dve.wait_ge(bank_full[h % 2], b[h % 2] + 1 + h // 2)
                    step(dve.tensor_reduce(neg_max[:, h, :], bank[:, h % 2, :].rearrange("p (t k) -> p t k", t=TB),
                                           AX_X, ALU.max, negate=True))
                    dve.tensor_tensor(scaled_max[:, h, :], neg_max[:, h, :], rsq[:, norm, :],
                                      ALU.mult).then_inc(max_ready, 1)

                def normalise(h):
                    dve.wait_ge(bank_free[h % 2], b[h % 2] + 1 + h // 2)
                    step(dve.reciprocal(inv_sum[:, h, :], exp_sum[:, h, :]))
                    for t in range(TB):
                        pr = probs[:, h % 2, t, :]
                        last = dve.tensor_scalar(pr, pr, inv_sum[:, h, t:t + 1], None, ALU.mult)
                    last.then_inc(probs_ready, 1)

                def copy_probs(h):
                    dve.wait_ge(bank_full[2], b[2] + h + 1)
                    dve.tensor_copy(probs_t[:, h % 2, :, :].rearrange(flat), bank[:, 2, :]).then_inc(bank_free[2], 1)

                def output(h):
                    dve.wait_ge(halved_hi, ph.half + h + 1)
                    dve.tensor_tensor(h_lo[:, h, :], bank[:, 3, 0:S], h_hi32[:, h, :],
                                      ALU.subtract).then_inc(bank_free[3], 1)

                low(ph.unit + AHEAD)
                low(ph.unit + 1 + AHEAD)
                chunk_turned(("pool", "mo")[l], NC - 1)
                variance(norm)
                low(ph.unit + 5)
                dve.wait_ge(rs_ready, norm + 1)
                maximum(0)
                low(ph.unit + 6)
                normalise(0)
                maximum(1)
                low(ph.unit + 7)
                copy_probs(0)
                normalise(1)
                maximum(2)
                copy_probs(1)
                output(0)
                normalise(2)
                low(po.unit)
                copy_probs(2)
                output(1)
                low(po.unit + 1)
                output(2)
                maximum(3)
                low(po.unit + 2)
                normalise(3)
                copy_probs(3)
                low(po.unit + 3)
                output(3)
                low(po.unit + 4)
                out_phase(f"xo{l}", XH // UK, done=2)

            def ffn(l):
                ph, norm = PH[f"fi{l}"], (N_F0, N_F1)[l]

                def hidden(i):
                    for m in range(2):
                        cols = bass.ds(i * (CK * S) + 2 * m * S, 2 * S)
                        dve.wait_ge(halved_hi, i * 2 + ph.half + m + 1)
                        dve.tensor_tensor(h_lo_flat[:, cols], bank[:, m, :], h_hi32_flat[:, cols],
                                          ALU.subtract).then_inc(bank_free[m], 1)

                def pair(i, first):
                    g = ph.group + 1
                    for j in range(16):
                        low(ph.unit + j + AHEAD, i, 16)
                        if j == 1 and first:
                            chunk_turned(f"xo{l}", NC - 1)
                            variance(norm)
                        if j == 0 and not first:
                            hidden(i - 1)
                        if j == 15:
                            if first:
                                dve.wait_ge(rs_ready, norm + 1)
                                dve.wait_ge(mixed, NC)
                            dve.wait_ge(acc_free[ph.group % 2], i + slot_count(ph.group) + 1)
                            dve.wait_ge(unit_used, i * 16 + ph.unit + 16)
                            for t in range(TB):
                                last = dve.scalar_tensor_tensor(
                                    out=h_tok[:, t, :], in0=acc[:, g % 2, t, :], scalar=rs[:, norm, t:t + 1],
                                    in1=s_tok[:, t, :], op0=ALU.mult, op1=ALU.mult)
                            last.then_inc(acc_free[g % 2], 1)

                pair(0, True)
                with dve.Fori(1, NP) as i:
                    pair(i, False)
                out_phase(f"fo{l}", FK // UK, rest=lambda: hidden(NP - 1))

            out_phase("pool", CK // UK)
            xattn(0)
            ffn(0)

            ph, pp = PH["mi"], PH["mp"]

            def latent_turned(k, count, m, kb0, gain):
                turned(k, count, lambda kb: h_lo[:, kb0 + kb, :], lambda kb: h_hi32[:, kb0 + kb, :], (2 * m, 2 * m + 1),
                       lambda kb: gains[:, gain + kb:gain + kb + 1])

            for j in range(24):
                low(ph.unit + j + AHEAD)
                if j == 1:
                    chunk_turned("fo0", NC - 1)
                    variance(N_MLA)
                if j == 17:
                    variance(N_CQ, RANK)
                    for m in range(2):
                        latent_turned(m, ph.half + m + 1, m, 16, G_CQ)

            kv = pp.group + 1

            def heads_kv(i, dst, c0, done):
                dve.wait_ge(unit_used, i * 4 + pp.unit + 4)
                for t in range(TB):
                    src = acc[:, kv % 2, t, :].rearrange("p (h n) -> p h n", h=2)[:, :, c0:c0 + P]
                    last = dve.tensor_scalar(dst[:, t, :, :], src, rs[:, N_CKV, t:t + 1], None, ALU.mult)
                last.then_inc(done, 1)

            low(pp.unit + AHEAD)
            for m in range(2):
                latent_turned(2 + m, ph.half + 2 + m + 1, m, 20, G_CKV)
            variance(N_CKV, RANK)
            low(pp.unit + 1 + AHEAD)
            low(pp.unit + 2 + AHEAD)
            low(pp.unit + 3 + AHEAD)
            dve.wait_ge(rs_ready, N_CKV + 1)
            dve.wait_ge(mask_ready, 2)
            heads_kv(0, kh_tok, 0, k_ready)

            def attend(i, more):
                b = pp.bank

                def ahead(j):
                    n = pp.unit + 4 + j + AHEAD
                    low(n, i, 4, width_of(n + (i * 4 if isinstance(i, int) else 0)))

                dve.wait_ge(bank_full[1], i * 2 + b[1] + 1)
                dve.tensor_copy(kh_t[:, :, :].rearrange(flat), bank[:, 1, :]).then_inc(bank_free[1], 1)
                heads_kv(i, vh_tok, NOPE, acc_free[kv % 2])
                ahead(0)
                for h in range(2):
                    k, count = (3, i * 2 + b[3] + 2) if h == 0 else (0, i * 2 + b[0] + 1)
                    dve.wait_ge(bank_full[k], count)
                    dve.memset(pace[:, h:h + 1], 0.0)
                    for t, (cols, m) in enumerate(((slice(0, P), mask[:, P:S]), (slice(P, 3 * P), mask[:, :]))):
                        last = dve.tensor_tensor_reduce(neg_s[:, h, cols], bank[:, k, cols], m, -1.0, 3.0e38, ALU.add,
                                                        ALU.min, neg_max[:, h, t:t + 1])
                    last.then_inc(bank_free[k], 1)
                ahead(1)
                for h in range(2):
                    dve.wait_ge(exp_ready, i * 2 + h + 1)
                    dve.reciprocal(inv_sum[:, h, :], exp_sum[:, h, :]).then_inc(dve_recip, 1)
                    dve.wait_ge(dve_recip, i * 2 + h + 1)
                    for t, cols in enumerate((slice(0, P), slice(P, 3 * P))):
                        last = dve.tensor_scalar(mprobs[:, h, cols], mprobs[:, h, cols], inv_sum[:, h, t:t + 1], None,
                                                 ALU.mult)
                    last.then_inc(probs_ready, 1)
                ahead(2)
                for h in range(2):
                    dve.wait_ge(bank_full[1 + h], i * 2 + b[1 + h] + 2)
                    dve.tensor_copy(mprobs_t[:, h, :], bank[:, 1 + h, 0:3 * P]).then_inc(bank_free[1 + h], 1)
                ahead(3)
                if more:
                    heads_kv(i + 1, kh_tok, 0, k_ready)
                cols = bass.ds(i * (2 * S), 2 * S)
                dve.wait_ge(halved_hi, i + pp.half + 1)
                dve.tensor_tensor(h_lo_flat[:, cols], bank[:, 0, :], h_hi32_flat[:, cols],
                                  ALU.subtract).then_inc(bank_free[0], 1)

            with dve.Fori(0, PAIRS - 2) as i:
                attend(i, True)
            attend(PAIRS - 2, True)
            attend(PAIRS - 1, False)
            out_phase("mo", KB // UK, done=4)
            xattn(1)
            ffn(1)
            left, mid = D - CW, D // 2
            for t in range(TB):
                dve.wait_ge(last_product, t + 1)
                dve.tensor_tensor(x[:, t, left:D], acc[:, (PH["fo1"].group + NC - 1) % 2, t, :], x[:, t, left:D],
                                  ALU.add).then_inc(last_added, 1)
                dve.wait_ge(stats, STAT_END[N_OUT] - TB + t + 1)
                step(dve.tensor_reduce(total[:, N_OUT, t:t + 1], sums[:, N_OUT, t, :], AX_X, ALU.add))
                dve.tensor_scalar(var[:, N_OUT, t:t + 1], total[:, N_OUT, t:t + 1], 1.0 / D, EPS, ALU.mult,
                                  ALU.add).then_inc(var_ready, 1)
                dve.wait_ge(rs_ready, N_OUT + 1 + t)
                scale = rs[:, N_OUT, t:t + 1]
                dve.scalar_tensor_tensor(out=xg[:, t, left:D], in0=x[:, t, left:D], scalar=scale, in1=g_out[:, left:D],
                                         op0=ALU.mult, op1=ALU.mult)
                if t == 0:
                    dve.wait_ge(xg_ready, NC - 1)
                dve.tensor_scalar(xg[:, t, mid:left], xg[:, t, mid:left], scale, None,
                                  ALU.mult).then_inc(y_right, 1)

        @block.gpsimd
        def _(pool):
            steps = [0]

            def step(ins):
                steps[0] += 1
                ins.then_inc(pool_step, 1)
                pool.wait_ge(pool_step, steps[0])

            pool.memset(ident[:, :], 0.0).then_inc(ident_ready, 1)
            pool.wait_ge(ident_ready, 1)
            pool.affine_select(out=ident[:, :], in_=ident[:, :], compare_op=ALU.not_equal, fill=1.0, base=0,
                               pattern=[[-1, P]], channel_multiplier=1).then_inc(ident_ready, 1)
            pool.memset(mask[:, :], 0.0).then_inc(mask_ready, 1)
            pool.wait_ge(mask_ready, 1)
            pool.affine_select(out=mask[:, P:S], in_=mask[:, P:S], compare_op=ALU.is_ge, fill=MASK, base=0,
                               pattern=[[-1, P]], channel_multiplier=1).then_inc(mask_ready, 1)
            step(pool.memset(minus_half[:, :], -0.5))

            def inverse_rms(norm, scale=None):
                pool.wait_ge(var_ready, norm + 1)
                ins = pool.tensor_tensor(rs[:, norm, :], var[:, norm, :], minus_half[:, :], ALU.pow)
                if scale is not None:
                    step(ins)
                    ins = pool.tensor_scalar(rsq[:, norm, :], rs[:, norm, :], scale, None, ALU.mult)
                ins.then_inc(rs_ready, 1)

            def rotate(x1, x2, heads):

                def table(tab):
                    v = tab[:, :, :]
                    return v.unsqueeze(2).to_broadcast([P, TB, heads, HR]) if heads else v

                tmp = [rope_t[:, n, :, :, :] if heads else rope_t[:, n, :, 0, :] for n in range(4)]
                for n, (v, tab) in enumerate(((x1, cos), (x2, sin), (x2, cos), (x1, sin))):
                    ins = pool.tensor_tensor(tmp[n], v, table(tab), ALU.mult)
                ins.then_inc(rope_step, 1)
                return tmp

            inverse_rms(N_MEM)
            inverse_rms(N_POOL)
            for c in range(NC):
                g, cols = PH["pool"].group + c, slice(c * CW, (c + 1) * CW)
                pool.wait_ge(acc_free[g % 2], slot_count(g) + 1)
                pool.tensor_tensor(x[:, :, cols], x[:, :, cols], xs[:, c % 2, :, :], ALU.add).then_inc(mixed, 1)
            inverse_rms(N_X0, XSCALE)
            inverse_rms(N_F0)
            inverse_rms(N_MLA)
            inverse_rms(N_CQ, MSCALE)
            kr = PH["mi"].group + 2
            pool.wait_ge(table_ready, 1)
            pool.wait_ge(acc_free[kr % 2], slot_count(kr) + 1)
            x1, x2 = latent_tok[:, :, 2 * RANK:2 * RANK + HR], latent_tok[:, :, 2 * RANK + HR:LATENTS]
            tmp = rotate(x1, x2, 0)
            pool.wait_ge(rope_step, 1)
            pool.tensor_tensor(x1, tmp[0], tmp[1], ALU.subtract)
            pool.tensor_tensor(x2, tmp[2], tmp[3], ALU.add).then_inc(roped, 1)
            inverse_rms(N_CKV)
            pp = PH["mp"]
            q1, q2 = qh_tok[:, :, :, NOPE:NOPE + HR], qh_tok[:, :, :, NOPE + HR:NOPE + ROPE]
            with pool.Fori(0, PAIRS) as i:
                pool.wait_ge(acc_free[pp.group % 2], i + slot_count(pp.group) + 1)
                tmp = rotate(q1, q2, 2)
                pool.wait_ge(rope_step, i + 2)
                pool.tensor_tensor(q1, tmp[0], tmp[1], ALU.subtract)
                pool.tensor_tensor(q2, tmp[2], tmp[3], ALU.add).then_inc(roped, 1)
            inverse_rms(N_X1, XSCALE)
            inverse_rms(N_F1)
            ph = PH["fo1"]
            pool.wait_ge(g_in, 16)
            for c in range(NC - 1):
                g = ph.group + c
                pool.wait_ge(acc_free[g % 2], slot_count(g) + 1)
                cols = slice(c * CW, (c + 1) * CW)
                gain = g_out[:, cols].unsqueeze(1).to_broadcast([P, TB, CW])
                pool.tensor_tensor(xg[:, :, cols], x[:, :, cols], gain, ALU.mult).then_inc(xg_ready, 1)
            for t in range(TB):
                pool.wait_ge(var_ready, N_OUT + 1 + t)
                pool.tensor_tensor(rs[:, N_OUT, t:t + 1], var[:, N_OUT, t:t + 1], minus_half[:, t:t + 1],
                                   ALU.pow).then_inc(rs_ready, 1)


def _bands():
    import numpy as np
    t = np.arange(S)[:, None]
    s = np.arange(S)[None, :]
    out = []
    for b in range(TB):
        for w in WINDOWS:
            m = np.where((t <= s) & (s < t + w), 1.0 / np.minimum(s + 1, w), 0.0) - (t == s)
            out.append(m[b * P:(b + 1) * P, b * P:min(S, b * P + REACH)])
    return np.ascontiguousarray(np.concatenate(out, axis=1), dtype=np.float32)


_INS = ["x", "mem", "positions", "norm_mix_g", "norm_xattn_g", "norm_mem_g", "norm_ffn_g", "pool_w", "pool_scale",
        "mla_w_in", "mla_q_norm_g", "mla_w_q_up", "mla_kv_norm_g", "mla_w_kv_up", "mla_w_out", "xattn_w_q",
        "xattn_w_kv", "xattn_w_o", "ffn_w_in", "ffn_w_out", "final_norm_g"]


def kernel(**inputs):
    import numpy as _np
    import concourse.bacc as _bacc
    from concourse import mybir as _mybir
    from concourse.bass_utils import run_bass_kernel_spmd as _run

    nc = _bacc.Bacc("TRN2", target_bir_lowering=False, num_devices=1)
    arrays, args = {}, {}
    given = [(name, inputs[name]) for name in _INS]
    given.append(("bands", _bands()))
    given.append(("inv_freq", (1.0 / 10000.0 ** (_np.arange(0, ROPE, 2) / ROPE)).astype(_np.float32)))
    for name, v in given:
        v = _np.ascontiguousarray(v)
        arrays[f"in_{name}"] = v
        args[name] = nc.dram_tensor(f"in_{name}", v.shape, _mybir.dt.from_np(v.dtype), kind="ExternalInput").ap()
    out = nc.dram_tensor("out_0", (1, S, D), _mybir.dt.from_np(_np.dtype("float32")), kind="ExternalOutput").ap()
    hybrid_kernel(nc, args, out)
    r = _run(nc, [arrays], core_ids=[0])
    return r.results[0]["out_0"]
```
